# Optimizing a Trainium2 kernel written in Bass

```python
import math
import jax, jax.numpy as jnp
from jax import lax
import numpy as np

D_MODEL = 2048
BATCH = 1
SEQ = 256
DEPTH = 2

HEAD_DIM = 128
A_HEADS = 6
A_HALF = HEAD_DIM // 2
A_WIDTH = A_HEADS * HEAD_DIM
B_HEADS = 6
B_WIDTH = B_HEADS * HEAD_DIM
B_Q_RANK = 512
B_KV_RANK = 256
IDX_HEADS = 16
IDX_DIM = 64
TOPK_MAX = 256
C_GROUPS = 4
C_GROUP_DIM = 128
C_WIDTH = C_GROUPS * C_GROUP_DIM
CHUNK = 128
MIX_WIDTH = A_WIDTH + B_WIDTH + C_WIDTH
IN_SIZES = (A_WIDTH, A_WIDTH, A_WIDTH, B_Q_RANK, B_KV_RANK, IDX_DIM, IDX_HEADS, C_WIDTH, C_WIDTH)
IN_COLS = sum(IN_SIZES)
MEM_LEN = 256
X_HEADS = 4
X_DIM = 128
FFN_HIDDEN = ((-(-8 * D_MODEL // 3) + 255) // 256) * 256
REL_BUCKETS = 32
REL_MAX_DIST = 128
REL_HEADS = A_HEADS + B_HEADS
Q_BLOCK = 128
EPS = 1e-6


def rms_norm(x, g):
    xf = x.astype(jnp.float32)
    y = xf * lax.rsqrt(jnp.mean(xf * xf, axis=-1, keepdims=True) + EPS)
    return (y * g.astype(jnp.float32)).astype(x.dtype)

def layer_norm(x, g, b):
    xf = x.astype(jnp.float32)
    mu = jnp.mean(xf, axis=-1, keepdims=True)
    xc = xf - mu
    var = jnp.mean(xc * xc, axis=-1, keepdims=True)
    return (xc * lax.rsqrt(var + EPS) * g.astype(jnp.float32) + b.astype(jnp.float32)).astype(x.dtype)

def rel_bucket(dist):
    n = jnp.maximum(dist, 0)
    max_exact = REL_BUCKETS // 2
    nf = jnp.maximum(n, 1).astype(jnp.float32)
    large = max_exact + (jnp.log(nf / max_exact) / math.log(REL_MAX_DIST / max_exact)
                         * (REL_BUCKETS - max_exact)).astype(jnp.int32)
    large = jnp.minimum(large, REL_BUCKETS - 1)
    return jnp.where(n < max_exact, n, large)

def to_blocks(t):
    b, s = t.shape[:2]
    return jnp.moveaxis(t.reshape((b, s // Q_BLOCK, Q_BLOCK) + t.shape[2:]), 1, 0)

def from_blocks(t):
    t = jnp.moveaxis(t, 0, 1)
    return t.reshape((t.shape[0], t.shape[1] * t.shape[2]) + t.shape[3:])

def diff_attention(q, k, v, lam, bias_tab, sub_g, lam_init):
    s_len = q.shape[1]
    kpos = jnp.arange(s_len)
    scale = A_HALF ** -0.5

    def block(args):
        qi, i = args
        qpos = i * Q_BLOCK + jnp.arange(Q_BLOCK)
        dist = qpos[:, None] - kpos[None, :]
        bias = jnp.transpose(bias_tab[rel_bucket(dist)], (2, 0, 1)).astype(jnp.float32)
        logits = jnp.einsum('bqhmd,bshmd->bhmqs', qi, k).astype(jnp.float32) * scale
        logits = logits + bias[None, :, None]
        logits = jnp.where((dist >= 0)[None, None, None], logits, -jnp.inf)
        p = jax.nn.softmax(logits, axis=-1)
        attn = p[:, :, 0] - lam * p[:, :, 1]
        return jnp.einsum('bhqs,bshd->bqhd', attn.astype(v.dtype), v)

    nblk = s_len // Q_BLOCK
    o = from_blocks(lax.map(block, (to_blocks(q), jnp.arange(nblk))))
    return rms_norm(o, sub_g) * (1.0 - lam_init)

def dsa_attention(c_q, c_kv, k_idx, w_idx, w_uq, w_qidx, w_uk, w_uv, bias_tab):
    bsz, s_len = c_q.shape[:2]
    topk = min(TOPK_MAX, s_len // 4)
    q = jnp.einsum('bsr,rhd->bshd', c_q, w_uq)
    q_lat = jnp.einsum('bshd,rhd->bshr', q, w_uk)
    q_idx = jnp.einsum('bsr,rgd->bsgd', c_q, w_qidx)
    w_idx = w_idx * (IDX_HEADS ** -0.5)
    kpos = jnp.arange(s_len)
    bidx = jnp.arange(bsz)[:, None, None]

    def block(args):
        qi, wi, ql, i = args
        qpos = i * Q_BLOCK + jnp.arange(Q_BLOCK)
        dots = jnp.einsum('bqgd,bsd->bqsg', qi, k_idx) * (IDX_DIM ** -0.5)
        score = jnp.einsum('bqsg,bqg->bqs', jax.nn.relu(dots), wi).astype(jnp.float32)
        causal = kpos[None, :] <= qpos[:, None]
        score = jnp.where(causal[None], score, -jnp.inf)
        top_score, idx = lax.top_k(score, topk)
        valid = jnp.isfinite(top_score)
        c_sel = c_kv[bidx, idx]
        dist = qpos[None, :, None] - idx
        bias = jnp.transpose(bias_tab[rel_bucket(dist)], (0, 3, 1, 2)).astype(jnp.float32)
        logits = jnp.einsum('bqhr,bqkr->bhqk', ql, c_sel).astype(jnp.float32) * (HEAD_DIM ** -0.5) + bias
        logits = jnp.where(valid[:, None], logits, -jnp.inf)
        p = jax.nn.softmax(logits, axis=-1)
        return jnp.einsum('bhqk,bqkr->bqhr', p.astype(c_sel.dtype), c_sel)

    nblk = s_len // Q_BLOCK
    o_lat = from_blocks(lax.map(block, (to_blocks(q_idx), to_blocks(w_idx), to_blocks(q_lat),
                                        jnp.arange(nblk))))
    return jnp.einsum('bshr,rhd->bshd', o_lat, w_uv)

def chunk_spatial_gating(u, v, ln_g, ln_b, w_s, b_s):
    v = layer_norm(v, ln_g, ln_b)
    bsz, s_len = v.shape[:2]
    vc = v.reshape(bsz, s_len // CHUNK, CHUNK, C_GROUPS, C_GROUP_DIM)
    mask = jnp.tril(jnp.ones((CHUNK, CHUNK), dtype=bool))
    w = jnp.where(mask[None], w_s, jnp.zeros_like(w_s))
    y = jnp.einsum('gts,bnsgc->bntgc', w, vc) + jnp.transpose(b_s)[None, None, :, :, None]
    return u * y.reshape(bsz, s_len, C_WIDTH)

def memory_attention(h, mem_n, wq, wkv, wo):
    q = jnp.einsum('bsd,dhe->bshe', h, wq)
    kv = jnp.einsum('bmd,dche->bmche', mem_n, wkv)
    k, v = kv[:, :, 0], kv[:, :, 1]
    logits = jnp.einsum('bshe,bmhe->bhsm', q, k).astype(jnp.float32) * (X_DIM ** -0.5)
    p = jax.nn.softmax(logits, axis=-1)
    o = jnp.einsum('bhsm,bmhe->bshe', p.astype(v.dtype), v)
    return jnp.einsum('bshe,hed->bsd', o, wo)

def swiglu(h, w_gu, w_down):
    gu = jnp.einsum('bsd,dcf->bscf', h, w_gu)
    return jnp.einsum('bsf,fd->bsd', jax.nn.silu(gu[:, :, 0]) * gu[:, :, 1], w_down)

def first_inputs(seed: int = 0) -> dict:
    key = jax.random.key(seed)
    ks = iter(jax.random.split(key, 40))
    f32 = jnp.float32

    def nrm(shape, scale):
        return jax.random.normal(next(ks), shape, f32) * scale

    def gain(shape):
        return 1.0 + 0.05 * jax.random.normal(next(ks), shape, f32)

    L = DEPTH
    return {
        "x": nrm((BATCH, SEQ, D_MODEL), 1.0),
        "mem": nrm((BATCH, MEM_LEN, D_MODEL), 1.0),
        "rel_bias": nrm((REL_BUCKETS, REL_HEADS), 0.5),
        "mix_pre_g": gain((L, D_MODEL)),
        "mix_post_g": gain((L, D_MODEL)),
        "w_in": nrm((L, D_MODEL, IN_COLS), D_MODEL ** -0.5),
        "w_out": nrm((L, MIX_WIDTH, D_MODEL), MIX_WIDTH ** -0.5),
        "a_lambda": nrm((L, 4, A_HALF), 0.1),
        "a_sub_g": gain((L, HEAD_DIM)),
        "b_cq_g": gain((L, B_Q_RANK)),
        "b_ckv_g": gain((L, B_KV_RANK)),
        "b_w_uq": nrm((L, B_Q_RANK, B_HEADS, HEAD_DIM), B_Q_RANK ** -0.5),
        "b_w_qidx": nrm((L, B_Q_RANK, IDX_HEADS, IDX_DIM), B_Q_RANK ** -0.5),
        "b_w_uk": nrm((L, B_KV_RANK, B_HEADS, HEAD_DIM), B_KV_RANK ** -0.5),
        "b_w_uv": nrm((L, B_KV_RANK, B_HEADS, HEAD_DIM), B_KV_RANK ** -0.5),
        "c_ln_g": gain((L, C_WIDTH)),
        "c_ln_b": nrm((L, C_WIDTH), 0.02),
        "c_w_s": nrm((L, C_GROUPS, CHUNK, CHUNK), CHUNK ** -0.5),
        "c_b_s": 1.0 + nrm((L, C_GROUPS, CHUNK), 0.1),
        "x_pre_g": gain((L, D_MODEL)),
        "x_post_g": gain((L, D_MODEL)),
        "mem_g": gain((L, D_MODEL)),
        "x_wq": nrm((L, D_MODEL, X_HEADS, X_DIM), D_MODEL ** -0.5),
        "x_wkv": nrm((L, D_MODEL, 2, X_HEADS, X_DIM), D_MODEL ** -0.5),
        "x_wo": nrm((L, X_HEADS, X_DIM, D_MODEL), (X_HEADS * X_DIM) ** -0.5),
        "f_pre_g": gain((L, D_MODEL)),
        "f_post_g": gain((L, D_MODEL)),
        "f_w_gu": nrm((L, D_MODEL, 2, FFN_HIDDEN), D_MODEL ** -0.5),
        "f_w_down": nrm((L, FFN_HIDDEN, D_MODEL), FFN_HIDDEN ** -0.5),
    }

def first_block(x, mem, rel_bias, mix_pre_g, mix_post_g, w_in, w_out, a_lambda, a_sub_g,
              b_cq_g, b_ckv_g, b_w_uq, b_w_qidx, b_w_uk, b_w_uv,
              c_ln_g, c_ln_b, c_w_s, c_b_s,
              x_pre_g, x_post_g, mem_g, x_wq, x_wkv, x_wo,
              f_pre_g, f_post_g, f_w_gu, f_w_down):
    bsz, s_len, _ = x.shape
    bias_a = rel_bias[:, :A_HEADS]
    bias_b = rel_bias[:, A_HEADS:]
    split_at = np.cumsum(IN_SIZES)[:-1].tolist()
    h = x
    for l in range(DEPTH):
        lam_init = 0.8 - 0.6 * math.exp(-0.3 * l)
        xn = rms_norm(h, mix_pre_g[l])
        proj = jnp.einsum('bsd,dc->bsc', xn, w_in[l])
        qa, ka, va, cq, ckv, kidx, widx, cu, cv = jnp.split(proj, split_at, axis=-1)
        lp = a_lambda[l].astype(jnp.float32)
        lam = jnp.exp(jnp.sum(lp[0] * lp[1])) - jnp.exp(jnp.sum(lp[2] * lp[3])) + lam_init
        oa = diff_attention(qa.reshape(bsz, s_len, A_HEADS, 2, A_HALF),
                            ka.reshape(bsz, s_len, A_HEADS, 2, A_HALF),
                            va.reshape(bsz, s_len, A_HEADS, HEAD_DIM),
                            lam, bias_a, a_sub_g[l], lam_init)
        ob = dsa_attention(rms_norm(cq, b_cq_g[l]), rms_norm(ckv, b_ckv_g[l]), kidx, widx,
                           b_w_uq[l], b_w_qidx[l], b_w_uk[l], b_w_uv[l], bias_b)
        oc = chunk_spatial_gating(jax.nn.gelu(cu), jax.nn.gelu(cv), c_ln_g[l], c_ln_b[l],
                                  c_w_s[l], c_b_s[l])
        mix = jnp.concatenate([oa.reshape(bsz, s_len, A_WIDTH),
                               ob.reshape(bsz, s_len, B_WIDTH), oc], axis=-1)
        h = h + rms_norm(jnp.einsum('bsc,cd->bsd', mix, w_out[l]), mix_post_g[l])
        xa = memory_attention(rms_norm(h, x_pre_g[l]), rms_norm(mem, mem_g[l]),
                              x_wq[l], x_wkv[l], x_wo[l])
        h = h + rms_norm(xa, x_post_g[l])
        ff = swiglu(rms_norm(h, f_pre_g[l]), f_w_gu[l], f_w_down[l])
        h = h + rms_norm(ff, f_post_g[l])
    return h


DEPTH_2 = 1

HEAD_DIM_2 = 64
N_Q_HEADS = D_MODEL // 128
N_KV_HEADS = 4
Q_PER_KV = N_Q_HEADS // N_KV_HEADS
ATTN_W = N_Q_HEADS * HEAD_DIM_2
KV_W = N_KV_HEADS * HEAD_DIM_2
WINDOW = 128
BLOCK = 128
SSM_W = D_MODEL // 2
GROUP = 16
N_GROUPS = SSM_W // GROUP
STATE = 64
IN_SIZES_2 = (ATTN_W, KV_W, KV_W, ATTN_W, SSM_W, SSM_W, D_MODEL, D_MODEL)
IN_W = sum(IN_SIZES_2)
NORM_EPS = 1e-6


def rms_norm_2(x, w):
    xf = x.astype(jnp.float32)
    y = xf * lax.rsqrt(jnp.mean(xf * xf, axis=-1, keepdims=True) + NORM_EPS)
    return (y * w.astype(jnp.float32)).astype(x.dtype)

def sliding_window_attention(q, k, v, sinks):
    b, l = q.shape[0], q.shape[1]
    nb = l // BLOCK
    qb = q.reshape(b, nb, BLOCK, N_KV_HEADS, Q_PER_KV, HEAD_DIM_2)
    kb = k.reshape(b, nb, BLOCK, N_KV_HEADS, HEAD_DIM_2)
    vb = v.reshape(b, nb, BLOCK, N_KV_HEADS, HEAD_DIM_2)
    k_prev = jnp.concatenate([jnp.zeros_like(kb[:, :1]), kb[:, :-1]], axis=1)
    v_prev = jnp.concatenate([jnp.zeros_like(vb[:, :1]), vb[:, :-1]], axis=1)
    kk = jnp.concatenate([k_prev, kb], axis=2)
    vv = jnp.concatenate([v_prev, vb], axis=2)
    scale = 1.0 / math.sqrt(HEAD_DIM_2)
    scores = jnp.einsum('bnqgrd,bnsgd->bngrqs', qb, kk).astype(jnp.float32) * scale
    q_loc = jnp.arange(BLOCK)[:, None] + BLOCK
    k_loc = jnp.arange(2 * BLOCK)[None, :]
    diff = q_loc - k_loc
    k_abs = (jnp.arange(nb)[:, None, None] - 1) * BLOCK + k_loc[None]
    valid = (diff >= 0)[None] & (diff < WINDOW)[None] & (k_abs >= 0)
    scores = jnp.where(valid[None, :, None, None], scores, -1e30)
    sink = jnp.broadcast_to(
        sinks.astype(jnp.float32).reshape(1, 1, N_KV_HEADS, Q_PER_KV, 1, 1),
        scores.shape[:-1] + (1,))
    probs = jax.nn.softmax(jnp.concatenate([scores, sink], axis=-1), axis=-1)[..., :-1]
    out = jnp.einsum('bngrqs,bnsgd->bnqgrd', probs.astype(v.dtype), vv)
    return out.reshape(b, l, ATTN_W)

def s5_ssm(u, A_re, A_im, log_dt, B_re, B_im, C_re, C_im, D_skip):
    dt = jnp.exp(log_dt)[:, None]
    mag = jnp.exp(dt * A_re)
    ab_re = mag * jnp.cos(dt * A_im)
    ab_im = mag * jnp.sin(dt * A_im)
    num_re = ab_re - 1.0
    num_im = ab_im
    den = A_re * A_re + A_im * A_im
    cf_re = (num_re * A_re + num_im * A_im) / den
    cf_im = (num_im * A_re - num_re * A_im) / den
    bu_re = jnp.einsum('blgh,gph->blgp', u, B_re)
    bu_im = jnp.einsum('blgh,gph->blgp', u, B_im)
    b_re = cf_re * bu_re - cf_im * bu_im
    b_im = cf_re * bu_im + cf_im * bu_re
    a_re = jnp.broadcast_to(ab_re, b_re.shape)
    a_im = jnp.broadcast_to(ab_im, b_im.shape)

    def combine(e1, e2):
        a1r, a1i, b1r, b1i = e1
        a2r, a2i, b2r, b2i = e2
        return (a2r * a1r - a2i * a1i,
                a2r * a1i + a2i * a1r,
                a2r * b1r - a2i * b1i + b2r,
                a2r * b1i + a2i * b1r + b2i)

    _, _, s_re, s_im = lax.associative_scan(combine, (a_re, a_im, b_re, b_im), axis=1)
    y = (jnp.einsum('blgp,ghp->blgh', s_re, C_re)
         - jnp.einsum('blgp,ghp->blgh', s_im, C_im)
         + D_skip * u)
    return y

def second_inputs(seed: int = 0) -> dict:
    key = jax.random.key(seed)
    ks = jax.random.split(key, 20)
    f32 = jnp.float32
    n = jnp.arange(STATE, dtype=f32)
    x = jax.random.normal(ks[0], (BATCH, SEQ, D_MODEL), f32)
    norm_w = 1.0 + 0.02 * jax.random.normal(ks[1], (D_MODEL,), f32)
    w_in = jax.random.normal(ks[2], (D_MODEL, IN_W), f32) * D_MODEL ** -0.5
    q_norm_w = 1.0 + 0.02 * jax.random.normal(ks[3], (HEAD_DIM_2,), f32)
    k_norm_w = 1.0 + 0.02 * jax.random.normal(ks[4], (HEAD_DIM_2,), f32)
    sinks = jax.random.normal(ks[5], (N_Q_HEADS,), f32)
    w_attn_proj = jax.random.normal(ks[6], (ATTN_W, D_MODEL), f32) * ATTN_W ** -0.5
    A_re = -0.5 + 0.01 * jax.random.normal(ks[7], (N_GROUPS, STATE), f32)
    A_im = math.pi * n[None, :] + 0.01 * jax.random.normal(ks[8], (N_GROUPS, STATE), f32)
    log_dt = jax.random.uniform(ks[9], (N_GROUPS,), f32, math.log(1e-3), math.log(1e-1))
    b_scale = (2.0 * GROUP) ** -0.5
    B_re = jax.random.normal(ks[10], (N_GROUPS, STATE, GROUP), f32) * b_scale
    B_im = jax.random.normal(ks[11], (N_GROUPS, STATE, GROUP), f32) * b_scale
    c_scale = (2.0 * STATE) ** -0.5
    C_re = jax.random.normal(ks[12], (N_GROUPS, GROUP, STATE), f32) * c_scale
    C_im = jax.random.normal(ks[13], (N_GROUPS, GROUP, STATE), f32) * c_scale
    D_skip = jax.random.normal(ks[14], (N_GROUPS, GROUP), f32)
    w_glu = jax.random.normal(ks[15], (SSM_W, 2 * SSM_W), f32) * SSM_W ** -0.5
    b_glu = 0.01 * jax.random.normal(ks[16], (2 * SSM_W,), f32)
    w_ssm_proj = jax.random.normal(ks[17], (SSM_W, D_MODEL), f32) * SSM_W ** -0.5
    w_out = jax.random.normal(ks[18], (D_MODEL, D_MODEL), f32) * D_MODEL ** -0.5
    return {"x": x, "norm_w": norm_w, "w_in": w_in, "q_norm_w": q_norm_w,
            "k_norm_w": k_norm_w, "sinks": sinks, "w_attn_proj": w_attn_proj,
            "A_re": A_re, "A_im": A_im, "log_dt": log_dt, "B_re": B_re, "B_im": B_im,
            "C_re": C_re, "C_im": C_im, "D_skip": D_skip, "w_glu": w_glu,
            "b_glu": b_glu, "w_ssm_proj": w_ssm_proj, "w_out": w_out}

def second_block(x, norm_w, w_in, q_norm_w, k_norm_w, sinks, w_attn_proj, A_re, A_im,
              log_dt, B_re, B_im, C_re, C_im, D_skip, w_glu, b_glu, w_ssm_proj, w_out):
    b, l, _ = x.shape
    split_pts = list(np.cumsum(IN_SIZES_2)[:-1])
    f32 = jnp.float32
    for _layer in range(DEPTH_2):
        h = rms_norm_2(x, norm_w)
        proj = h @ w_in
        q, k, v, a_gate, u, z, g_a, g_s = jnp.split(proj, split_pts, axis=-1)
        q = rms_norm_2(q.reshape(b, l, N_Q_HEADS, HEAD_DIM_2), q_norm_w)
        k = rms_norm_2(k.reshape(b, l, N_KV_HEADS, HEAD_DIM_2), k_norm_w)
        v = v.reshape(b, l, N_KV_HEADS, HEAD_DIM_2)
        attn = sliding_window_attention(q, k, v, sinks)
        y_a = (attn * jax.nn.silu(a_gate)) @ w_attn_proj
        u_g = u.reshape(b, l, N_GROUPS, GROUP).astype(f32)
        y_ssm = s5_ssm(u_g, A_re.astype(f32), A_im.astype(f32), log_dt.astype(f32),
                       B_re.astype(f32), B_im.astype(f32), C_re.astype(f32),
                       C_im.astype(f32), D_skip.astype(f32))
        y_ssm = jax.nn.gelu(y_ssm.reshape(b, l, SSM_W)).astype(x.dtype)
        glu_a, glu_b = jnp.split(y_ssm @ w_glu + b_glu, 2, axis=-1)
        y_s = (glu_a * jax.nn.sigmoid(glu_b) * jax.nn.silu(z)) @ w_ssm_proj
        merged = jax.nn.sigmoid(g_a) * y_a + jax.nn.sigmoid(g_s) * y_s
        x = x + merged @ w_out
    return x


def setup_inputs(seed=0):
    out = dict(first_inputs(seed))
    for name, value in second_inputs(seed + 1).items():
        if name != "x":
            out[name + "_2"] = value
    return out


def reference(
    x, mem, rel_bias, mix_pre_g, mix_post_g, w_in, w_out, a_lambda, a_sub_g, b_cq_g, b_ckv_g,
    b_w_uq, b_w_qidx, b_w_uk, b_w_uv, c_ln_g, c_ln_b, c_w_s, c_b_s, x_pre_g, x_post_g, mem_g,
    x_wq, x_wkv, x_wo, f_pre_g, f_post_g, f_w_gu, f_w_down, norm_w_2, w_in_2, q_norm_w_2,
    k_norm_w_2, sinks_2, w_attn_proj_2, A_re_2, A_im_2, log_dt_2, B_re_2, B_im_2, C_re_2,
    C_im_2, D_skip_2, w_glu_2, b_glu_2, w_ssm_proj_2, w_out_2,
):
    x = first_block(
        x, mem, rel_bias, mix_pre_g, mix_post_g, w_in, w_out, a_lambda, a_sub_g, b_cq_g,
        b_ckv_g, b_w_uq, b_w_qidx, b_w_uk, b_w_uv, c_ln_g, c_ln_b, c_w_s, c_b_s, x_pre_g,
        x_post_g, mem_g, x_wq, x_wkv, x_wo, f_pre_g, f_post_g, f_w_gu, f_w_down,
    )
    return second_block(
        x, norm_w_2, w_in_2, q_norm_w_2, k_norm_w_2, sinks_2, w_attn_proj_2, A_re_2, A_im_2,
        log_dt_2, B_re_2, B_im_2, C_re_2, C_im_2, D_skip_2, w_glu_2, b_glu_2, w_ssm_proj_2,
        w_out_2,
    )


_drawn_inputs = setup_inputs


def setup_inputs(seed=0):
    import zlib

    import numpy as np

    out = dict(_drawn_inputs(seed))
    spreads = {}
    factors = {'c_ln_g': 2.932,
     'c_ln_b': 6.368,
     'norm_w_2': 8.0,
     'q_norm_w_2': 8.0,
     'k_norm_w_2': 8.0,
     'sinks_2': 8.0,
     'A_re_2': 64.0,
     'A_im_2': 64.0,
     'log_dt_2': 64.0,
     'B_re_2': 64.0,
     'B_im_2': 64.0,
     'C_re_2': 64.0,
     'C_im_2': 64.0,
     'b_glu_2': 53.093}
    for name, (base, spread) in spreads.items():
        noise = np.random.default_rng([zlib.crc32(name.encode()), seed]).standard_normal(out[name].shape)
        drawn = base * np.exp(spread * noise) if base else spread * noise
        out[name] = __import__('jax').numpy.asarray(drawn.astype(out[name].dtype))
    for name, factor in factors.items():
        out[name] = (out[name] * factor).astype(out[name].dtype)
    return out
```

```python
import math
from contextlib import ExitStack

import concourse.bass as bass
import numpy as np
from concourse import mybir

F32 = mybir.dt.float32
F32R = mybir.dt.float32r
ALU = mybir.AluOpType
ACT = mybir.ActivationFunctionType
AX = mybir.AxisListType

P = 128
D = 2048
KD = D // P
T = 256
NT = T // P
L = 2
HA, HB, HX = 6, 6, 4
NIDX = 16
TOPK = 64
FF = 5632
EPS = 1e-6
NEG = -1e30
FILL, TAKEN = -3.0e38, -3.3e38

KU = 2
W = 512
SLOTS = 4
WSLOT = KU * W


class Group:

    def __init__(self, name, kchunks, width, form, unit, index):
        self.name, self.kchunks, self.width, self.form = name, kchunks, width, form
        self.unit, self.index = unit, index
        self.units = kchunks // KU
        self.parity, self.turn = index % 2, index // 2
        self.end = unit + self.units
        self.blocks = width // P


def plan(specs):
    groups, unit = {}, 0
    for n, (name, kchunks, width, form) in enumerate(specs):
        groups[name] = Group(name, kchunks, width, form, unit, n)
        unit += kchunks // KU
    assert unit % SLOTS == 0 and len(specs) % 2 == 0
    return groups, unit


NJ = FF // W
LAYER = [("mem_k", KD, W, "C"), ("mem_v", KD, W, "T")]
LAYER += [(f"qk{n}", KD, W, "C") for n in range(3)]
LAYER += [("va0", KD, W, "T"), ("va1", KD, 256, "T"), ("cq", KD, W, "T"), ("ckv", KD, 336, "T"),
          ("cu", KD, W, "C"), ("cv", KD, W, "T")]
LAYER += [("uq0", 4, W, "C"), ("uq1", 4, 256, "C"), ("uk0", 2, W, "C"), ("uk1", 2, 256, "C"),
          ("uv0", 2, W, "T"), ("uv1", 2, 256, "T"), ("qi0", 4, W, "C"), ("qi1", 4, W, "C")]
LAYER += [(f"wo{n}", KD, W, "T") for n in range(4)]
LAYER += [("xq", KD, W, "C")] + [(f"xo{n}", 4, W, "T") for n in range(4)]
LAYER += [("gate0", KD, W, "T"), ("up0", KD, W, "T")]
for _j in range(1, NJ):
    LAYER += [(f"gate{_j}", KD, W, "T"), (f"up{_j}", KD, W, "T")]
    LAYER += [(f"down{_j - 1}_{n}", 4, W, "T") for n in range(4)]
LAYER += [(f"down{NJ - 1}_{n}", 4, W, "T") for n in range(4)]
LG, LU = plan(LAYER)
LN = len(LAYER)

SECOND = [("q0", KD, W, "T"), ("q1", KD, W, "T"), ("kv", KD, W, "T"), ("u0", KD, W, "C"), ("u1", KD, W, "C")]
SECOND += [("ag0", KD, W, "C"), ("ag1", KD, W, "C")]
for _n in range(4):
    SECOND += [(f"ga{_n}", KD, W, "C"), (f"ap{_n}", 8, W, "C")]
SECOND += [("z0", KD, W, "C"), ("z1", KD, W, "C")]
for _n in range(2):
    SECOND += [(f"glub{_n}", 8, W, "C"), (f"glua{_n}", 8, W, "C")]
for _n in range(4):
    SECOND += [(f"gs{_n}", KD, W, "C"), (f"sp{_n}", 8, W, "C")]
SECOND += [(f"out{n}", KD, W, "T") for n in range(4)]
SECOND += [("end", 0, W, "T")] if len(SECOND) % 2 else []
SG, SU = plan(SECOND)

PAIRS = [(i, hp) for i in range(NT) for hp in range(3)]


def turns_of_attention(tag, steps):
    out = [f"{tag}L0"]
    for k in range(steps):
        out += ([f"{tag}L{k + 1}"] if k + 1 < steps else []) + [f"{tag}T{k}", f"{tag}V{k}"]
    return out


def numbered(names):
    assert len(names) % 2 == 0, len(names)
    return {n: i for i, n in enumerate(names)}


LTURNS = [f"mem{q}" for q in range(4)] + [f"pre{q}" for q in range(4)]
LTURNS += turns_of_attention("a", 6) + ["an0", "an1", "c", "bq", "bkv"]
LTURNS += [f"ix{i}_{b}" for i in range(NT) for b in range(4)] + turns_of_attention("b", 6)
LTURNS += [f"xpre{q}" for q in range(4)] + turns_of_attention("x", 2)
LTURNS += [f"fpre{q}" for q in range(4)] + [f"h{j}" for j in range(NJ)]
LTP = numbered(LTURNS)
NTP = len(LTP)
NCT = 8
STURNS = [f"norm{q}" for q in range(4)] + ["tq0", "tq1", "tk"] + turns_of_attention("w", 8)
STURNS += [f"s{c}_{r}" for c in range(NCT) for r in ("re", "im", "y")]
STP = numbered(STURNS + ([] if len(STURNS) % 2 == 0 else ["end"]))



def woven(groups, steps):
    units = [("unit", g, n) for g in groups for n in range(g.units)]
    out, left = [], sorted(steps, key=lambda s: s[0])
    for n in range(len(units) + 1):
        while left and left[0][0] <= n:
            out.append(left.pop(0)[1:])
        out += units[n:n + 1]
    assert not left
    return out


def second_steps():
    steps = [(1, "head_rows"), (4, "head_turns"), (5, "wL", 0)]
    for k in range(8):
        at = 6 + 1.5 * k
        steps += [(at, "wL", k + 1)] * (k < 7) + [(at, "w_weights", k), (at, "wT", k), (at, "wV", k)]
    names = ["u0", "u1", "ag0", "ag1"] + [f"{a}{n}" for n in range(4) for a in ("ga", "ap")]
    at, ends = 0, {}
    for name in names:
        at += SG[name].units
        ends[name] = at
    steps += [(ends[name] + 1, "out", name) for name in names[:-1]]
    for c in range(NCT):
        at = 19 + 7.2 * c
        steps += [(at, "angles", c), (at + 1, "inputs", c), (at + 1, "turns", c), (at + 2, "maps", c),
                  (at + 3, "back", c), (at + 4, "scan", c), (at + 5, "forward", c), (at + 6.5, "outputs", c),
                  (at + 7, "skip", c)]
    return woven([SG[name] for name in names], steps) + [("out", names[-1])]


SMIX = second_steps()

HIS = {n: i for i, n in enumerate([f"mem{q}" for q in range(4)] + [f"pre{q}" for q in range(4)] + ["bq", "bkv"]
                                  + [f"xpre{q}" for q in range(4)] + ["xV0", "xV1"]
                                  + [f"fpre{q}" for q in range(4)] + [f"h{j}" for j in range(NJ)])}
COUNTS = {"unit": (LU, 48), "acc": (LN // 2, 6), "turn": (NTP, 2), "turn2": (NTP // 2, 1),
          "hi": (len(HIS), 2), "gated": (NJ, 2), "raw": (16 * LU // SLOTS, 16 * 48 // SLOTS)}


def hold(eng, semaphore, value, passed):
    eng.wait_ge(semaphore, value)
    eng.sem_inc(passed, 1)


class Pos:

    def __init__(self, layer, turn=None):
        self.layer, self.turn = layer, turn

    def n(self, kind, count):
        per, step = COUNTS[kind] if isinstance(kind, str) else (kind, 0)
        value = self.layer * per + count
        return value if self.turn is None or not step else self.turn * step + value


PC, _at = {}, 0
for _name, _n in [("mem_g", KD), ("mix_pre_g", KD), ("x_pre_g", KD), ("f_pre_g", KD), ("cq_g", 4),
                  ("ckv_g", 2), ("sub_g", 1), ("neg_lam_init", 1), ("one_minus_lam_init", 1), ("c_w", 4 * P)]:
    PC[_name] = slice(_at, _at + _n)
    _at += _n
NPC = _at
BR, _at = {}, 0
for _name, _n in [("ln_g", W), ("ln_b", W), ("b_s", W), ("lam", 256)]:
    BR[_name] = slice(_at, _at + _n)
    _at += _n
NBR = _at
SC, _at = {}, 0
for _name, _n in [("norm_w", KD), ("q_w", 1), ("k_w", 1), ("b_glu", KD), ("skip", NCT),
                  ("A_re", 32), ("A_im", 32), ("log_dt", 32)]:
    SC[_name] = slice(_at, _at + _n)
    _at += _n
NSC = _at
TOEP = 384
NQ = 16


def build(nc, stream, x, mem, params, rows, post_g, sparams, sinks, onehot, rel, b_pad, c_pack, out,
          toep_scratch):
    ctx = ExitStack()
    with ctx:
        place = [nc.sbuf_base + (-nc.sbuf_base) % 64]
        base = place[0]
        ctx.enter_context(nc.sbuf_tensor("arena", [P, (nc.sbuf_usable_end - base) // 4 - 16], F32))

        def at_offset(name, offset, shape, dt=F32):
            return nc.alloc_sbuf_tensor_at(name, shape, dt, offset=offset)

        def sb(name, shape, dt=F32):
            here = place[0]
            place[0] += (int(np.prod(shape[1:])) * 4 + 31) // 32 * 32
            assert place[0] <= nc.sbuf_usable_end - 64, (name, place[0])
            return at_offset(name, here, shape, dt)

        raw = [sb(f"raw{s}", [P, KU, W]) for s in range(SLOTS)]
        hi = [sb(f"hi{s}", [P, KU, W], F32R) for s in range(SLOTS)]
        lo = [sb(f"lo{s}", [P, KU, W], F32R) for s in range(SLOTS)]
        h = sb("h", [P, NT, D])
        x_at = place[0]
        xh = sb("xh", [P, KD, T], F32R)
        xl = sb("xl", [P, KD, T], F32R)
        y_at = place[0]
        y = sb("y", [P, NT, D])
        mixT = at_offset("mixT", y_at, [P, KD, T])
        par = sb("par", [P, NPC])
        row_at = place[0]
        row = sb("row", [P, NBR])
        gpost_at = place[0]
        gpost = sb("gpost", [P, D])
        bias = sb("bias", [P, HA + HB, T])
        ident = sb("ident", [P, P])
        mhalf = sb("mhalf", [P, 40])
        small = sb("small", [P, 384])
        spar = sb("spar", [P, NSC])
        ssm = sb("ssm", [P, 5, 32])
        lg = [at_offset(f"lg{n}", x_at + n * 4096, [P, 4, T]) for n in range(2)]
        pe_ = [at_offset(f"pe{n}", x_at + 8192 + n * 4096, [P, 4, T]) for n in range(2)]
        pT = [at_offset(f"pT{n}", x_at + 16384 + n * 2048, [P, 2, T]) for n in range(2)]
        cqh = at_offset("cqh", x_at + 20480, [P, 4, T], F32R)
        cql = at_offset("cql", x_at + 24576, [P, 4, T], F32R)
        ckh = at_offset("ckh", x_at + 28672, [P, 2, T], F32R)
        ckl = at_offset("ckl", x_at + 30720, [P, 2, T], F32R)
        qp_at = place[0]
        QP = sb("QP", [P, 8, 2, T])
        r_at = place[0]
        kaT = sb("kaT", [P, HA, T])
        va = sb("va", [P, NT, HA * P])
        oa = sb("oa", [P, NT, HA * P])
        cq = sb("cq", [P, NT, W])
        ckv = sb("ckv", [P, NT, 336])
        kk = sb("kk", [P, NT, P])
        cuT = sb("cuT", [P, 4, T])
        cv = sb("cv", [P, NT, W])
        kmT = sb("kmT", [P, HX, T])
        vm = sb("vm", [P, NT, W])
        kiT = sb("kiT", [P, T])
        junk = at_offset("junk", r_at, [P, D])
        qbT = at_offset("qbT", r_at, [P, HB, T])
        kbT = at_offset("kbT", r_at + 6144, [P, HB, T])
        vb = at_offset("vb", r_at + 12288, [P, NT, HB * P])
        cv_at = r_at + 3 * 6144 + 4096 + 336 * 8 + 1024 + 4096
        sc = at_offset("sc", cv_at, [P, NT, T])
        qxT = at_offset("qxT", r_at, [P, HX, T])
        sg = at_offset("sg", r_at, [P, NT, W])
        hm = [at_offset(f"hm{n}", r_at + 4096 * (1 + n), [P, NT, W]) for n in range(2)]
        hTh = at_offset("hTh", r_at + 12288, [P, 4, T], F32R)
        hTl = at_offset("hTl", r_at + 16384, [P, 4, T], F32R)
        toep = at_offset("toep", x_at, [P, 12, TOEP])
        relb = at_offset("relb", y_at, [32, 12, P])
        relt = at_offset("relt", y_at + 8192, [32, 12])
        oneh = at_offset("oneh", y_at + 10240, [32, TOEP])
        iota = sb("iota", [P, T])
        m_at = row_at
        uT = at_offset("uT", m_at, [P, NCT, T])
        rotc = at_offset("rotc", m_at + 8192, [P, 4, T])
        rots = at_offset("rots", m_at + 12288, [P, 4, T])
        sd = [at_offset(f"sd{n}", m_at + 16384 + 4096 * n, [P, 4, T]) for n in range(2)]
        window = at_offset("window", m_at + 24576, [P, T])
        sink = at_offset("sink", m_at + 25600, [P, NQ])
        qt = at_offset("qt", r_at, [P, NT, NQ * 64])
        kv = at_offset("kv", r_at + 8192, [P, NT, W])
        kT = at_offset("kT", r_at + 12288, [P, 4, T])
        vpad = at_offset("vpad", r_at + 16384, [P, NT, 4, 2, P])
        attnT = at_offset("attnT", r_at + 24576, [P, 8, T])
        sg2 = at_offset("sg2", r_at + 32768, [P, 4, T])
        cpad = [at_offset(f"cpad{n}", r_at + 36864 + 2560 * n, [P, 5 * P]) for n in range(2)]
        craw = at_offset("craw", r_at + 36864 + 5120, [P, 2, 4, 32])
        craw2 = at_offset("craw2", r_at + 36864 + 6144, [P, 4, 32])
        sw = at_offset("sw", gpost_at, [P, 14, 32])
        angle_hi = at_offset("angle_hi", gpost_at + 2048, [P, 32], F32R)
        kdup = at_offset("kdup", y_at + 8192, [P, NT, 4, 2, 64])
        zg = [at_offset(f"zg{n}", y_at + 4096 * n, [P, 4, T]) for n in range(2)]
        ze = [at_offset(f"ze{n}", y_at + 8192 + 4096 * n, [P, 4, T]) for n in range(2)]
        gath = at_offset("gath", qp_at, [P, 8, T], F32R)
        gatl = at_offset("gatl", qp_at + 8192, [P, 8, T], F32R)
        ysh = at_offset("ysh", qp_at, [P, 8, T], F32R)
        ysl = at_offset("ysl", qp_at + 8192, [P, 8, T], F32R)
        sr = [at_offset(f"sr{n}", r_at + 4096 * n, [P, 4, T]) for n in range(2)]
        st = at_offset("st", r_at + 8192, [P, 4, T])
        bpad = [at_offset(f"bpad{n}", r_at + 12288 + 4096 * n, [P, 2, 4, P]) for n in range(2)]
        zs = at_offset("zs", r_at + 24576, [P, 8, T])
        prh = at_offset("prh", r_at, [P, 8, T], F32R)
        prl = at_offset("prl", r_at + 8192, [P, 8, T], F32R)

        acc = [ctx.enter_context(nc.psum_tensor(f"acc{n}", [P, NT, W], F32)) for n in range(2)]
        tp = [ctx.enter_context(nc.psum_tensor(f"tp{n}", [P, 4, T], F32)) for n in range(2)]
        accC = [a[:, :, :].rearrange("p a (b t) -> p (a b) t", t=T) for a in acc]

        def sem(name):
            return ctx.enter_context(nc.semaphore(name))

        raw_loaded = [sem(f"raw_loaded{s}") for s in range(SLOTS)]
        hi_done = sem("hi_done")
        split_done = sem("split_done")
        unit_used = sem("unit_used")
        acc_read = [sem(f"acc_read{n}") for n in range(2)]
        tp_full = sem("tp_full")
        tp_read = [sem(f"tp_read{n}") for n in range(2)]
        const_ready = sem("const_ready")
        start_loaded = sem("start_loaded")
        rel_spread = sem("rel_spread")
        toep_full = sem("toep_full")
        toep_copied = sem("toep_copied")
        toep_moved = sem("toep_moved")
        bias_ready = sem("bias_ready")
        x_loaded = sem("x_loaded")
        mem_loaded = sem("mem_loaded")
        par_loaded = sem("par_loaded")
        gpost_loaded = sem("gpost_loaded")
        cw_ready = sem("cw_ready")
        lam_ready = sem("lam_ready")
        lam_exp = sem("lam_exp")
        h_rows = sem("h_rows")
        in_squares = sem("in_squares")
        in_roots = sem("in_roots")
        in_rows = sem("in_rows")
        out_squares = sem("out_squares")
        out_sums = sem("out_sums")
        out_roots = sem("out_roots")
        x_hi = sem("x_hi")
        max_ready = sem("max_ready")
        exp_ready = sem("exp_ready")
        weights_ready = sem("weights_ready")
        oa_squares = sem("oa_squares")
        oa_roots = sem("oa_roots")
        oa_rows = sem("oa_rows")
        v_stats = sem("v_stats")
        v_roots = sem("v_roots")
        v_rows = sem("v_rows")
        gated_c = sem("gated_c")
        lat_squares = sem("lat_squares")
        lat_roots = sem("lat_roots")
        lat_rows = sem("lat_rows")
        dots_used = sem("dots_used")
        score_masked = sem("score_masked")
        mix_hi = sem("mix_hi")
        mix_split = sem("mix_split")
        gated = sem("gated")
        out_stored = sem("out_stored")

        par2_loaded = sem("par2_loaded")
        sink_loaded = sem("sink_loaded")
        window_ready = sem("window_ready")
        ssm_ready = sem("ssm_ready")
        ssm_exp = sem("ssm_exp")
        q_squares = sem("q_squares")
        q_roots = sem("q_roots")
        q_rows = sem("q_rows")
        sink_exp = sem("sink_exp")
        ag_mul = sem("ag_mul")
        ag_hi = sem("ag_hi")
        ag_split = sem("ag_split")
        bc_loaded = [sem(f"bc_loaded{n}") for n in range(2)]
        angles = sem("angles")
        turned = sem("turned")
        states = sem("states")
        skipped = sem("skipped")
        ys_hi = sem("ys_hi")
        ys_split = sem("ys_split")
        glu_mul = sem("glu_mul")
        glu_hi = sem("glu_hi")
        glu_split = sem("glu_split")
        merged_done = sem("merged_done")

        ss, rs = small[:, 0:2], small[:, 2:4]
        pss, prs = small[:, 240:248].rearrange("p (t n) -> p t n", t=NT), small[:, 4:6]
        psum_ = small[:, 6:8]
        mx = [small[:, 8 + 4 * n:12 + 4 * n] for n in range(2)]
        nmx = [small[:, 16 + 4 * n:20 + 4 * n] for n in range(2)]
        sm = [small[:, 24 + 4 * n:28 + 4 * n] for n in range(2)]
        rc = [small[:, 32 + 4 * n:36 + 4 * n] for n in range(2)]
        lamv, lame, nlam, subg = small[:, 40:42], small[:, 42:44], small[:, 44:45], small[:, 45:46]
        oss, ors = small[:, 48:60], small[:, 60:72]
        vst = small[:, 72:84].rearrange("p (t s) -> p t s", s=6)
        vmv = small[:, 84:88].rearrange("p (t s) -> p t s", s=2)
        vrs = small[:, 88:90]
        lss, lrs = small[:, 92:96], small[:, 96:100]
        m8 = small[:, 104:112]
        widx = small[:, 112:144].rearrange("p (t g) -> p t g", g=NIDX)
        qss, qrs = small[:, 144:184], small[:, 184:224]
        snk = [small[:, 224 + 4 * n:228 + 4 * n] for n in range(2)]
        esk = [small[:, 232 + 4 * n:236 + 4 * n] for n in range(2)]
        lamp = small[:, 256:384].rearrange("p (a n) -> p a n", n=64)

        def flat(tensor):
            names = " ".join("abcd"[:len(tensor.shape) - 1])
            return tensor[tuple(slice(None) for _ in tensor.shape)].rearrange(f"p {names} -> p ({names})")

        def pcol(name, n=0):
            return par[:, PC[name].start + n:PC[name].start + n + 1]

        def take_turn(pe, pos, turn):
            pe.wait_ge(tp_read[turn % 2], pos.n("turn2", turn // 2 + 1))
            return tp[turn % 2]

        def see_turn(eng, pos, turn):
            eng.wait_ge(tp_full, pos.n("turn", turn + 1))
            return tp[turn % 2]

        def after_turn(eng, pos, turn):
            eng.wait_ge(tp_read[turn % 2], pos.n("turn2", turn // 2 + 2))

        def see_group(eng, pos, g):
            eng.wait_ge(unit_used, pos.n("unit", g.end + SLOTS))
            return (accC if g.form == "C" else acc)[g.parity]

        def after_group(eng, pos, g):
            eng.wait_ge(acc_read[g.parity], pos.n("acc", g.turn + 2))

        passed = sem("passed")

        SCALE_A, SCALE_B = 64 ** -0.5, P ** -0.5
        TWO_PI_HI = 6.28125
        TWO_PI_MID = float(np.float32(2 * math.pi - 6.28125))
        TWO_PI_LO = 2 * math.pi - 6.28125 - TWO_PI_MID
        ROUND = 1.5 * 2.0 ** 23
        PI_IN = 3.1415925

        def reduce_angle(dve, out, angle, turns):
            nc.vector.tensor_scalar(turns, angle, 1.0 / (2 * math.pi), ROUND, ALU.mult, ALU.add)
            dve.drain()
            nc.vector.tensor_scalar(turns, turns, -ROUND, None, ALU.add)
            dve.drain()
            nc.vector.scalar_tensor_tensor(out, turns, -TWO_PI_HI, angle, ALU.mult, ALU.add)
            dve.drain()
            nc.vector.scalar_tensor_tensor(out, turns, -TWO_PI_MID, out, ALU.mult, ALU.add)
            dve.drain()
            nc.vector.scalar_tensor_tensor(out, turns, -TWO_PI_LO, out, ALU.mult, ALU.add)
            dve.drain()
            nc.vector.tensor_scalar(out, out, PI_IN, -PI_IN, ALU.min, ALU.max)
            dve.drain()

        def cos_argument(dve, out, angle, negative):
            nc.vector.tensor_scalar(negative, angle, -1.0, None, ALU.mult)
            dve.drain()
            nc.vector.tensor_tensor(out, angle, negative, ALU.max)
            dve.drain()
            nc.vector.tensor_scalar(out, out, -1.0, math.pi / 2, ALU.mult, ALU.add)

        block = ctx.enter_context(nc.Block())

        @block.sync
        def _(sp):
            sp.dma_start(h[:, :, :], x.rearrange("(t p) d -> p t d", p=P)).then_inc(x_loaded, 16)
            with sp.Fori(0, (L * LU + SU) // SLOTS) as i:
                for s in range(SLOTS):
                    sp.wait_ge(split_done, i * SLOTS + (s + 1))
                    sp.dma_start(flat(raw[s]), stream[bass.ds((i * SLOTS + s) * P, P), :]).then_inc(raw_loaded[s], 16)
            for n in range(4):
                after_group(sp, Pos(L), SG[f"out{n}"])
                sp.dma_start(out.rearrange("(t p) d -> p t d", p=P)[:, :, n * W:(n + 1) * W],
                             h[:, :, n * W:(n + 1) * W]).then_inc(out_stored, 16)
            sp.wait_ge(out_stored, 64)

        @block.tensor
        def _(pe):
            def product(pos, g, a_h, a_l, only=None, quad_ready=None):
                a = (accC if g.form == "C" else acc)[g.parity]
                for n in range(g.units) if only is None else (only,):
                    if n == 0:
                        pe.wait_ge(acc_read[g.parity], pos.n("acc", g.turn + 1))
                    if quad_ready is not None and n % 2 == 0:
                        quad_ready(n // 2)
                    s = (g.unit + n) % SLOTS
                    pe.wait_ge(split_done, pos.n("unit", g.unit + n + 1 + SLOTS))
                    for k in range(KU):
                        c = n * KU + k
                        first, final = c == 0, c == g.kchunks - 1
                        if g.form == "T":
                            for t in range(NT):
                                o = a[:, t, 0:g.width]
                                ah, al = a_h[:, c, t * P:(t + 1) * P], a_l[:, c, t * P:(t + 1) * P]
                                nc.tensor.matmul(o, ah, hi[s][:, k, 0:g.width], start=first, stop=False)
                                nc.tensor.matmul(o, ah, lo[s][:, k, 0:g.width], start=False, stop=False)
                                last = nc.tensor.matmul(o, al, hi[s][:, k, 0:g.width], start=False, stop=final)
                        else:
                            for b in range(g.blocks):
                                o = a[:, b, :]
                                wh, wl = hi[s][:, k, b * P:(b + 1) * P], lo[s][:, k, b * P:(b + 1) * P]
                                nc.tensor.matmul(o, wh, a_h[:, c, :], start=first and b % 2 == 0, stop=False,
                                                 skip_group_check=True)
                                nc.tensor.matmul(o, wh, a_l[:, c, :], start=False, stop=False, skip_group_check=True)
                                last = nc.tensor.matmul(o, wl, a_h[:, c, :], start=False, stop=final,
                                                        skip_group_check=True)
                    last.then_inc(unit_used, 1)

            def transposes(pos, turn, blocks):
                o = take_turn(pe, pos, turn)
                for c, t, src in blocks:
                    last = nc.tensor.transpose(o[:, c, t * P:(t + 1) * P], src, ident[:, :])
                last.then_inc(tp_full, 1)

            def norm(pos, k, tag, turns):
                for t in range(NT):
                    pe.wait_ge(in_rows, pos.n(8, 2 * k + t + 1))
                for q in range(4):
                    transposes(pos, turns[f"{tag}{q}"], [(c, t, y[:, t, (4 * q + c) * P:(4 * q + c + 1) * P])
                                                         for c in range(4) for t in range(NT)])
                return lambda q: after_turn(pe, pos, turns[f"{tag}{q}"])

            pe.wait_ge(rel_spread, 1)
            for hd in range(HA + HB):
                if hd >= 4:
                    pe.wait_ge(toep_copied, hd - 3)
                bank = (flat(acc[hd % 4]) if hd % 4 < 2 else flat(tp[hd % 4 - 2]))[:, 0:TOEP]
                nc.tensor.matmul(bank, relb[:, hd, :], oneh[:, :], start=True, stop=True).then_inc(toep_full, 1)
            pe.wait_ge(toep_copied, HA + HB)
            pe.wait_ge(const_ready, 1)
            pe.sem_inc(unit_used, SLOTS)

            with pe.Fori(0, L) as layer:
                pos = Pos(layer)
                ready = norm(pos, 0, "mem", LTP)
                product(pos, LG["mem_k"], xh, xl, quad_ready=ready)
                product(pos, LG["mem_v"], xh, xl)
                ready = norm(pos, 1, "pre", LTP)
                product(pos, LG["qk0"], xh, xl, quad_ready=ready)
                for name in ("qk1", "qk2", "va0", "va1", "cq", "ckv", "cu", "cv"):
                    product(pos, LG[name], xh, xl)

                def a_logits(k):
                    i, hp = PAIRS[k]
                    o = take_turn(pe, pos, LTP[f"aL{k}"])
                    for m in range(2):
                        for hh in range(2):
                            last = nc.tensor.matmul(o[:, 2 * m + hh, 0:P * (i + 1)],
                                                    QP[:, 2 * hp + hh, m, i * P:(i + 1) * P],
                                                    kaT[:, 2 * hp + hh, 0:P * (i + 1)], start=True, stop=True)
                    last.then_inc(tp_full, 1)

                for name in ("cq", "ckv"):
                    after_group(pe, pos, LG[name])
                a_logits(0)
                for k, (i, hp) in enumerate(PAIRS):
                    if k < 5:
                        a_logits(k + 1)
                    pe.wait_ge(weights_ready, pos.n(14, k + 1))
                    transposes(pos, LTP[f"aT{k}"], [(hh, b, lg[k % 2][:, hh, b * P:(b + 1) * P])
                                                    for hh in range(2) for b in range(i + 1)])
                    after_turn(pe, pos, LTP[f"aT{k}"])
                    o = take_turn(pe, pos, LTP[f"aV{k}"])
                    for hh in range(2):
                        hd = 2 * hp + hh
                        for b in range(i + 1):
                            last = nc.tensor.matmul(o[:, 0, hh * P:(hh + 1) * P], pT[k % 2][:, hh, b * P:(b + 1) * P],
                                                    va[:, b, hd * P:(hd + 1) * P], start=b == 0, stop=b == i)
                    last.then_inc(tp_full, 1)
                pe.wait_ge(oa_rows, pos.n(1, 1))
                transposes(pos, LTP["an0"], [(c, t, oa[:, t, c * P:(c + 1) * P]) for c in range(4) for t in range(NT)])
                transposes(pos, LTP["an1"], [(c, t, oa[:, t, (4 + c) * P:(5 + c) * P])
                                             for c in range(2) for t in range(NT)])

                pe.wait_ge(v_rows, pos.n(1, 1))
                pe.wait_ge(cw_ready, pos.n(1, 1))
                o = take_turn(pe, pos, LTP["c"])
                for t in range(NT):
                    for g in range(4):
                        w = PC["c_w"].start + g * P
                        last = nc.tensor.matmul(o[:, g, t * P:(t + 1) * P], cv[:, t, g * P:(g + 1) * P],
                                                par[:, w:w + P], start=True, stop=True)
                last.then_inc(tp_full, 1)

                pe.wait_ge(lat_rows, pos.n(1, 1))
                transposes(pos, LTP["bq"], [(c, t, cq[:, t, c * P:(c + 1) * P]) for c in range(4) for t in range(NT)])
                transposes(pos, LTP["bkv"], [(c, t, ckv[:, t, c * P:(c + 1) * P] if c < 2 else kk[:, t, :])
                                             for c in range(3) for t in range(NT)])
                after_turn(pe, pos, LTP["bq"])
                after_turn(pe, pos, LTP["bkv"])
                for name in ("uq0", "uq1"):
                    product(pos, LG[name], cqh, cql)
                for name in ("uk0", "uk1", "uv0", "uv1"):
                    product(pos, LG[name], ckh, ckl)
                for name in ("qi0", "qi1"):
                    product(pos, LG[name], cqh, cql)
                for name in ("qi0", "qi1"):
                    after_group(pe, pos, LG[name])
                for i in range(NT):
                    for b in range(4):
                        o = take_turn(pe, pos, LTP[f"ix{i}_{b}"])
                        for hh in range(4):
                            g = 4 * b + hh
                            last = nc.tensor.matmul(o[:, hh, 0:P * (i + 1)], QP[:, g // 2, g % 2, i * P:(i + 1) * P],
                                                    kiT[:, 0:P * (i + 1)], start=True, stop=True)
                        last.then_inc(tp_full, 1)

                def b_logits(k):
                    i, hp = PAIRS[k]
                    o = take_turn(pe, pos, LTP[f"bL{k}"])
                    for hh in range(2):
                        hd = 2 * hp + hh
                        last = nc.tensor.matmul(o[:, hh, 0:P * (i + 1)], qbT[:, hd, i * P:(i + 1) * P],
                                                kbT[:, hd, 0:P * (i + 1)], start=True, stop=True)
                    last.then_inc(tp_full, 1)

                b_logits(0)
                for k, (i, hp) in enumerate(PAIRS):
                    if k < 5:
                        b_logits(k + 1)
                    pe.wait_ge(weights_ready, pos.n(14, 6 + k + 1))
                    transposes(pos, LTP[f"bT{k}"], [(hh, b, pe_[k % 2][:, hh, b * P:(b + 1) * P])
                                                    for hh in range(2) for b in range(i + 1)])
                    after_turn(pe, pos, LTP[f"bT{k}"])
                    o = take_turn(pe, pos, LTP[f"bV{k}"])
                    for hh in range(2):
                        hd = 2 * hp + hh
                        for b in range(i + 1):
                            last = nc.tensor.matmul(o[:, 0, hh * P:(hh + 1) * P], vb[:, b, hd * P:(hd + 1) * P],
                                                    pT[k % 2][:, hh, b * P:(b + 1) * P], start=b == 0, stop=b == i)
                    last.then_inc(tp_full, 1)

                for n in range(4):
                    product(pos, LG[f"wo{n}"], xh, xl,
                            quad_ready=None if n else lambda q: pe.wait_ge(mix_split, pos.n(4, q + 1)))

                ready = norm(pos, 2, "xpre", LTP)
                product(pos, LG["xq"], xh, xl, quad_ready=ready)
                after_group(pe, pos, LG["xq"])
                for i in range(NT):
                    o = take_turn(pe, pos, LTP[f"xL{i}"])
                    for hd in range(HX):
                        last = nc.tensor.matmul(o[:, hd, :], qxT[:, hd, i * P:(i + 1) * P], kmT[:, hd, :],
                                                start=True, stop=True)
                    last.then_inc(tp_full, 1)
                for i in range(NT):
                    pe.wait_ge(weights_ready, pos.n(14, 12 + i + 1))
                    transposes(pos, LTP[f"xT{i}"], [(hd, b, pe_[i][:, hd, b * P:(b + 1) * P])
                                                    for hd in range(HX) for b in range(NT)])
                    after_turn(pe, pos, LTP[f"xT{i}"])
                    o = take_turn(pe, pos, LTP[f"xV{i}"])
                    for hd in range(HX):
                        for b in range(NT):
                            last = nc.tensor.matmul(o[:, hd, 0:P], vm[:, b, hd * P:(hd + 1) * P],
                                                    lg[i][:, hd, b * P:(b + 1) * P], start=b == 0, stop=b == 1)
                    last.then_inc(tp_full, 1)
                for i in range(NT):
                    after_turn(pe, pos, LTP[f"xV{i}"])
                for n in range(4):
                    product(pos, LG[f"xo{n}"], cqh, cql)

                ready = norm(pos, 3, "fpre", LTP)

                def across(pos, j):
                    pe.wait_ge(gated, pos.n("gated", j + 1))
                    transposes(pos, LTP[f"h{j}"], [(c, t, hm[j % 2][:, t, c * P:(c + 1) * P])
                                                   for c in range(4) for t in range(NT)])

                def down(pos, j):
                    after_turn(pe, pos, LTP[f"h{j}"])
                    for n in range(4):
                        product(pos, LG[f"down{j}_{n}"], hTh, hTl)

                product(pos, LG["gate0"], xh, xl, quad_ready=ready)
                product(pos, LG["up0"], xh, xl)
                with pe.Fori(0, (NJ - 1) // 2) as turn:
                    here = Pos(layer, turn)
                    for j in (1, 2):
                        product(here, LG[f"gate{j}"], xh, xl)
                        across(here, j - 1)
                        product(here, LG[f"up{j}"], xh, xl)
                        down(here, j - 1)
                across(pos, NJ - 1)
                down(pos, NJ - 1)

            pos = Pos(L)
            ready = norm(pos, 0, "norm", STP)
            product(pos, SG["q0"], xh, xl, quad_ready=ready)
            product(pos, SG["q1"], xh, xl)
            product(pos, SG["kv"], xh, xl)
            for step, *at in SMIX:
                if step == "unit":
                    g, n = at
                    if g is SG["ap0"] and n == 0:
                        pe.wait_ge(ag_split, 2)
                    if g.kchunks == KD:
                        product(pos, g, xh, xl, only=n)
                    else:
                        product(pos, g, gath, gatl, only=n)
                elif step == "head_turns":
                    pe.wait_ge(q_rows, 1)
                    for n in range(2):
                        transposes(pos, STP[f"tq{n}"], [(c, t, qt[:, t, (4 * n + c) * P:(4 * n + c + 1) * P])
                                                        for c in range(4) for t in range(NT)])
                    transposes(pos, STP["tk"], [(g, t, kdup[:, t, g, :, :].rearrange("p a b -> p (a b)"))
                                                for g in range(4) for t in range(NT)])
                elif step == "wL":
                    k = at[0]
                    i, g = k // 4, k % 4
                    if k == 0:
                        for name in ("tq0", "tq1", "tk"):
                            after_turn(pe, pos, STP[name])
                    o = take_turn(pe, pos, STP[f"wL{k}"])
                    for r in range(4):
                        hd = 4 * g + r
                        last = nc.tensor.matmul(o[:, r, 0:P * (i + 1)], QP[:, hd // 2, hd % 2, i * P:(i + 1) * P],
                                                kT[:, g, 0:P * (i + 1)], start=True, stop=True)
                    last.then_inc(tp_full, 1)
                elif step == "wT":
                    k = at[0]
                    pe.wait_ge(weights_ready, pos.n(14, k + 1))
                    transposes(pos, STP[f"wT{k}"], [(r, b, ze[k % 2][:, r, b * P:(b + 1) * P])
                                                    for r in range(4) for b in range(k // 4 + 1)])
                elif step == "wV":
                    k = at[0]
                    i, g = k // 4, k % 4
                    after_turn(pe, pos, STP[f"wT{k}"])
                    o = take_turn(pe, pos, STP[f"wV{k}"])
                    for n in range(2):
                        for r in range(2):
                            for b in range(i + 1):
                                last = nc.tensor.matmul(o[:, n, 0:P], vpad[:, b, g, r, :],
                                                        zg[k % 2][:, 2 * n + r, b * P:(b + 1) * P],
                                                        start=r == 0 and b == 0, stop=r == 1 and b == i)
                    last.then_inc(tp_full, 1)
                elif step == "inputs":
                    c = at[0]
                    pe.wait_ge(bc_loaded[c % 2], 32 * (c // 2 + 1))
                    if c == 0:
                        after_group(pe, pos, SG["u1"])
                    for m, part in enumerate(("re", "im")):
                        o = take_turn(pe, pos, STP[f"s{c}_{part}"])
                        for j in range(4):
                            last = nc.tensor.matmul(o[:, j, :], bpad[c % 2][:, m, j, :], uT[:, c, :],
                                                    start=True, stop=True)
                        last.then_inc(tp_full, 1)
                elif step == "outputs":
                    c = at[0]
                    pe.wait_ge(states, c + 1)
                    o = take_turn(pe, pos, STP[f"s{c}_y"])
                    for j in range(4):
                        for m in range(2):
                            last = nc.tensor.matmul(o[:, 0, :], cpad[m][:, j * P:(j + 1) * P], sd[m][:, j, :],
                                                    start=j == 0 and m == 0, stop=j == 3 and m == 1)
                    last.then_inc(tp_full, 1)
            product(pos, SG["z0"], xh, xl)
            product(pos, SG["z1"], xh, xl)
            pe.wait_ge(ys_split, 1)
            for n in range(2):
                product(pos, SG[f"glub{n}"], ysh, ysl)
                product(pos, SG[f"glua{n}"], ysh, ysl)
            for n in range(4):
                product(pos, SG[f"gs{n}"], xh, xl)
                if n == 0:
                    pe.wait_ge(glu_split, 2)
                product(pos, SG[f"sp{n}"], prh, prl)
            for n in range(4):
                product(pos, SG[f"out{n}"], xh, xl,
                        quad_ready=None if n else lambda q: pe.wait_ge(mix_split, pos.n(4, q + 1)))

        class Splitter:
            LEAD = SLOTS - 1

            def __init__(self, split):
                self.split, self.next = split, 0

            def ahead(self, pos, g, limit=LU + SLOTS):
                while self.next < min(g.end + self.LEAD, limit):
                    self.split(pos, self.next)
                    self.next += 1

            def before(self, pos, g, n, limit):
                while self.next < min(g.unit + n + 1 + self.LEAD, limit):
                    self.split(pos, self.next)
                    self.next += 1

            def new_layer(self):
                self.next -= LU

        @block.scalar
        def _(act):
            def split(pos, u):
                s = u % SLOTS
                act.wait_ge(raw_loaded[s], pos.n("raw", 16 * (u // SLOTS + 1)))
                act.wait_ge(unit_used, pos.n("unit", u + 1))
                nc.scalar.activation(hi[s][:, :, :], raw[s][:, :, :], ACT.Copy).then_inc(hi_done, 1)

            units = Splitter(split)

            def copy_group(pos, g, out, func=ACT.Copy):
                units.ahead(pos, g)
                a = see_group(act, pos, g)
                a = a[:, 0:g.blocks, :] if g.form == "C" else a[:, :, 0:g.width]
                nc.scalar.activation(out, a, func).then_inc(acc_read[g.parity], 1)

            def halves(pos, g, b0, b1, at, rest=None):
                units.ahead(pos, g)
                a = see_group(act, pos, g)
                ins = [nc.scalar.activation(QP[64 * m:64 * m + 64, at:at + b1 - b0, m, :],
                                            a[64 * m:64 * m + 64, b0:b1, :], ACT.Copy) for m in range(2)]
                if rest is not None:
                    ins.append(nc.scalar.activation(rest, a[:, b1:4, :], ACT.Copy))
                ins[-1].then_inc(acc_read[g.parity], 1)

            def norm(pos, k, tag, turns, gain, src, branch=None):
                for t in range(NT):
                    act.drain()
                    if branch is not None:
                        hold(act, h_rows, pos.n(6, 2 * branch + t + 1), passed)
                    nc.scalar.activation(junk[:, :], src[:, t, :], ACT.Square,
                                         accum_out=ss[:, t:t + 1]).then_inc(in_squares, 1)
                for q in range(4):
                    o = see_turn(act, pos, turns[f"{tag}{q}"])
                    for c in range(4):
                        last = nc.scalar.activation(xh[:, 4 * q + c, :], o[:, c, :], ACT.Copy, scale=gain(4 * q + c))
                    last.then_inc(x_hi, 1)

            def squares_out(pos, branch, groups):
                for n, g in enumerate(groups):
                    units.ahead(pos, g)
                    hold(act, acc_read[g.parity], pos.n("acc", g.turn + 2), passed)
                    for t in range(NT):
                        act.drain()
                        last = nc.scalar.activation(junk[:, 0:W], y[:, t, n * W:(n + 1) * W], ACT.Square,
                                                    accum_out=pss[:, t, n:n + 1])
                    last.then_inc(out_squares, 1)

            def exps(pos, n, k, heads, S, per=12):
                act.wait_ge(max_ready, n)
                for c in range(heads):
                    last = nc.scalar.activation(pe_[k % 2][:, c, 0:S], lg[k % 2][:, c, 0:S], ACT.Exp,
                                                bias=nmx[k % 2][:, c:c + 1], accum_out=sm[k % 2][:, c:c + 1])
                last.then_inc(exp_ready, 1)

            act.dma_start(relt[:, :], rel).then_inc(start_loaded, 16)
            act.dma_start(oneh[:, :], onehot).then_inc(start_loaded, 16)
            for hd in range(HA + HB):
                act.wait_ge(toep_full, hd + 1)
                bank = (flat(acc[hd % 4]) if hd % 4 < 2 else flat(tp[hd % 4 - 2]))[:, 0:TOEP]
                nc.scalar.activation(toep[:, hd, :], bank, ACT.Copy).then_inc(toep_copied, 1)
            act.wait_ge(toep_copied, HA + HB)
            act.dma_start(toep_scratch.rearrange("(p w) -> p w", p=P), flat(toep)).then_inc(toep_moved, 16)
            act.wait_ge(toep_moved, 16)
            pitch = 12 * TOEP - 1
            shifted = toep_scratch[P - 1:P - 1 + P * pitch].rearrange("(p w) -> p w", w=pitch)
            act.dma_start(bias[:, 0:11, :], shifted[:, 0:11 * TOEP].rearrange("p (h s) -> p h s", s=TOEP)[:, :, 0:T])\
               .then_inc(toep_moved, 16)
            act.dma_start(bias[:, 11, :], shifted[:, 11 * TOEP:11 * TOEP + T]).then_inc(toep_moved, 16)
            act.wait_ge(const_ready, 1)
            act.dma_start(spar[:, :], sparams).then_inc(par2_loaded, 16)
            act.wait_ge(par2_loaded, 16)
            nc.scalar.activation(sw[:, 0, :], spar[:, SC["log_dt"]], ACT.Exp).then_inc(ssm_exp, 1)
            act.wait_ge(ssm_ready, 1)
            nc.scalar.activation(ssm[:, 0, :], sw[:, 1, :], ACT.Exp)
            nc.scalar.activation(sw[:, 5, :], sw[:, 3, :], ACT.Sin)
            nc.scalar.activation(sw[:, 6, :], sw[:, 4, :], ACT.Sin).then_inc(ssm_exp, 1)
            units.ahead(Pos(0), Group("", 0, 0, "T", 0, 0))

            with act.Fori(0, L) as layer:
                pos = Pos(layer)
                act.wait_ge(par_loaded, pos.n(32, 32))
                act.wait_ge(lam_ready, pos.n(2, 1))
                nc.scalar.activation(lame, lamv, ACT.Exp).then_inc(lam_exp, 1)
                hold(act, mem_loaded, pos.n(16, 16), passed)
                norm(pos, 0, "mem", LTP, lambda c: pcol("mem_g", c), y)
                copy_group(pos, LG["mem_k"], kmT[:, :, :])
                copy_group(pos, LG["mem_v"], vm[:, :, :])
                norm(pos, 1, "pre", LTP, lambda c: pcol("mix_pre_g", c), h, 0)
                halves(pos, LG["qk0"], 0, 4, 0)
                halves(pos, LG["qk1"], 0, 2, 4, kaT[:, 0:2, :])
                copy_group(pos, LG["qk2"], kaT[:, 2:6, :])
                copy_group(pos, LG["va0"], va[:, :, 0:W])
                copy_group(pos, LG["va1"], va[:, :, W:HA * P])
                copy_group(pos, LG["cq"], cq[:, :, :])
                copy_group(pos, LG["ckv"], ckv[:, :, :])
                copy_group(pos, LG["cu"], cuT[:, :, :], ACT.Gelu_apprx_tanh)
                copy_group(pos, LG["cv"], cv[:, :, :], ACT.Gelu_apprx_tanh)

                exps(pos, pos.n(14, 1), 0, 4, P)
                for k, (i, hp) in enumerate(PAIRS):
                    if k < 5:
                        exps(pos, pos.n(14, k + 2), k + 1, 4, P * (PAIRS[k + 1][0] + 1))
                    o = see_turn(act, pos, LTP[f"aT{k}"])
                    nc.scalar.activation(pT[k % 2][:, :, 0:P * (i + 1)], o[:, 0:2, 0:P * (i + 1)], ACT.Copy)\
                      .then_inc(tp_read[LTP[f"aT{k}"] % 2], 1)
                    o = see_turn(act, pos, LTP[f"aV{k}"])
                    nc.scalar.activation(oa[:, i, 2 * hp * P:(2 * hp + 2) * P], o[:, 0, :], ACT.Copy)\
                      .then_inc(tp_read[LTP[f"aV{k}"] % 2], 1)
                act.wait_ge(lam_ready, pos.n(2, 2))
                for n, b in ((0, 4), (1, 2)):
                    o = see_turn(act, pos, LTP[f"an{n}"])
                    nc.scalar.activation(mixT[:, 4 * n:4 * n + b, :], o[:, 0:b, :], ACT.Copy, scale=subg)\
                      .then_inc(tp_read[LTP[f"an{n}"] % 2], 1)

                for t in range(NT):
                    for n, (src, w) in enumerate(((cq, W), (ckv, 2 * P))):
                        act.drain()
                        last = nc.scalar.activation(flat(lg[0])[:, 0:w], src[:, t, 0:w], ACT.Square,
                                                    accum_out=lss[:, 2 * n + t:2 * n + t + 1])
                last.then_inc(lat_squares, 1)
                o = see_turn(act, pos, LTP["bq"])
                for c in range(4):
                    last = nc.scalar.activation(cqh[:, c, :], o[:, c, :], ACT.Copy, scale=pcol("cq_g", c))
                last.then_inc(x_hi, 1)
                o = see_turn(act, pos, LTP["bkv"])
                for c in range(2):
                    nc.scalar.activation(ckh[:, c, :], o[:, c, :], ACT.Copy, scale=pcol("ckv_g", c))
                nc.scalar.activation(kiT[:, :], o[:, 2, :], ACT.Copy).then_inc(x_hi, 1)
                copy_group(pos, LG["uq0"], qbT[:, 0:4, :])
                copy_group(pos, LG["uq1"], qbT[:, 4:6, :])
                copy_group(pos, LG["uk0"], kbT[:, 0:4, :])
                copy_group(pos, LG["uk1"], kbT[:, 4:6, :])
                copy_group(pos, LG["uv0"], vb[:, :, 0:W])
                copy_group(pos, LG["uv1"], vb[:, :, W:HB * P])
                halves(pos, LG["qi0"], 0, 4, 0)
                halves(pos, LG["qi1"], 0, 4, 4)

                for i in range(NT):
                    for b in range(4):
                        n = 4 * i + b
                        o = see_turn(act, pos, LTP[f"ix{i}_{b}"])
                        if n >= 2:
                            act.wait_ge(dots_used, pos.n(8, n - 1))
                        nc.scalar.activation(pe_[n % 2][:, :, 0:P * (i + 1)], o[:, :, 0:P * (i + 1)], ACT.Relu,
                                             scale=float(64 ** -0.5)).then_inc(tp_read[LTP[f"ix{i}_{b}"] % 2], 1)

                exps(pos, pos.n(14, 7), 0, 2, P)
                for k, (i, hp) in enumerate(PAIRS):
                    if k < 5:
                        exps(pos, pos.n(14, 6 + k + 2), k + 1, 2, P * (PAIRS[k + 1][0] + 1))
                    o = see_turn(act, pos, LTP[f"bT{k}"])
                    nc.scalar.activation(pT[k % 2][:, :, 0:P * (i + 1)], o[:, 0:2, 0:P * (i + 1)], ACT.Copy)\
                      .then_inc(tp_read[LTP[f"bT{k}"] % 2], 1)
                    o = see_turn(act, pos, LTP[f"bV{k}"])
                    nc.scalar.activation(mixT[:, HA + 2 * hp:HA + 2 * hp + 2, i * P:(i + 1) * P],
                                         o[:, 0, :].rearrange("p (a b) -> p a b", b=P), ACT.Copy)\
                      .then_inc(tp_read[LTP[f"bV{k}"] % 2], 1)

                act.drain()
                act.wait_ge(gated_c, pos.n(1, 1))
                for n in range(4):
                    nc.scalar.activation(xh[:, 4 * n:4 * n + 4, :], mixT[:, 4 * n:4 * n + 4, :], ACT.Copy)\
                      .then_inc(mix_hi, 1)
                squares_out(pos, 0, [LG[f"wo{n}"] for n in range(4)])

                norm(pos, 2, "xpre", LTP, lambda c: pcol("x_pre_g", c), h, 1)
                copy_group(pos, LG["xq"], qxT[:, :, :])
                for i in range(NT):
                    act.wait_ge(max_ready, pos.n(14, 12 + i + 1))
                    o = see_turn(act, pos, LTP[f"xL{i}"])
                    for hd in range(HX):
                        last = nc.scalar.activation(pe_[i][:, hd, :], o[:, hd, :], ACT.Exp, scale=SCALE_B,
                                                    bias=nmx[i][:, hd:hd + 1], accum_out=sm[i][:, hd:hd + 1])
                    last.then_inc(tp_read[LTP[f"xL{i}"] % 2], 1)
                for i in range(NT):
                    o = see_turn(act, pos, LTP[f"xT{i}"])
                    nc.scalar.activation(lg[i][:, :, :], o[:, :, :], ACT.Copy).then_inc(tp_read[LTP[f"xT{i}"] % 2], 1)
                    o = see_turn(act, pos, LTP[f"xV{i}"])
                    nc.scalar.activation(cqh[:, :, i * P:(i + 1) * P], o[:, :, 0:P], ACT.Copy).then_inc(x_hi, 1)
                squares_out(pos, 1, [LG[f"xo{n}"] for n in range(4)])

                norm(pos, 3, "fpre", LTP, lambda c: pcol("f_pre_g", c), h, 2)

                def gate(pos, j):
                    g = LG[f"gate{j}"]
                    units.ahead(pos, g)
                    a = see_group(act, pos, g)
                    if j:
                        act.wait_ge(gated, pos.n("gated", j))
                    nc.scalar.activation(sg[:, :, :], a[:, :, :], ACT.Silu).then_inc(acc_read[g.parity], 1)

                def across(pos, j):
                    o = see_turn(act, pos, LTP[f"h{j}"])
                    nc.scalar.activation(hTh[:, :, :], o[:, :, :], ACT.Copy).then_inc(x_hi, 1)

                gate(pos, 0)
                units.ahead(pos, LG["up0"])
                with act.Fori(0, (NJ - 1) // 2) as turn:
                    here = Pos(layer, turn)
                    for j in (1, 2):
                        gate(here, j)
                        across(here, j - 1)
                        units.ahead(here, LG[f"up{j}"])
                        units.ahead(here, LG[f"down{j - 1}_3"])
                units.next = LG[f"down{NJ - 2}_3"].end + units.LEAD
                across(pos, NJ - 1)
                squares_out(pos, 2, [LG[f"down{NJ - 1}_{n}"] for n in range(4)])
                units.new_layer()

            pos = Pos(L)

            def ahead(name):
                units.ahead(pos, SG[name], SU)

            def read_out(name, out, func=ACT.Copy):
                g = SG[name]
                ahead(name)
                a = see_group(act, pos, g)
                nc.scalar.activation(out, a[:, :, :], func).then_inc(acc_read[g.parity], 1)

            norm(pos, 0, "norm", STP, lambda c: spar[:, SC["norm_w"].start + c:SC["norm_w"].start + c + 1], h, 0)
            for n in range(2):
                read_out(f"q{n}", qt[:, :, n * W:(n + 1) * W])
            read_out("kv", kv[:, :, :])
            q_w, k_w = spar[:, SC["q_w"]], spar[:, SC["k_w"]]

            def w_exps(k):
                S = P * (k // 4 + 1)
                act.wait_ge(max_ready, pos.n(14, k + 1))
                for r in range(4):
                    nc.scalar.activation(ze[k % 2][:, r, 0:S], zg[k % 2][:, r, 0:S], ACT.Exp,
                                         bias=nmx[k % 2][:, r:r + 1], accum_out=sm[k % 2][:, r:r + 1])
                nc.scalar.activation(esk[k % 2], snk[k % 2], ACT.Exp).then_inc(exp_ready, 1)

            for step, *at in SMIX:
                if step == "unit":
                    units.before(pos, *at, SU)
                elif step == "out":
                    name = at[0]
                    n = int(name[-1])
                    if name in ("u0", "u1"):
                        read_out(name, uT[:, 4 * n:4 * n + 4, :])
                    elif name in ("ag0", "ag1"):
                        if n:
                            act.wait_ge(ag_mul, n)
                        read_out(name, sg2[:, :, :], ACT.Silu)
                        act.wait_ge(ag_mul, n + 1)
                        nc.scalar.activation(gath[:, 4 * n:4 * n + 4, :], attnT[:, 4 * n:4 * n + 4, :], ACT.Copy)\
                          .then_inc(ag_hi, 1)
                    elif name in ("ga0", "ga1", "ga2", "ga3"):
                        if n:
                            after_group(act, pos, SG[f"ap{n - 1}"])
                        else:
                            act.wait_ge(ag_mul, 2)
                        read_out(name, sg2[:, :, :], ACT.Sigmoid)
                elif step == "head_turns":
                    for n in range(2):
                        o = see_turn(act, pos, STP[f"tq{n}"])
                        for m in range(2):
                            rows_ = slice(64 * m, 64 * m + 64)
                            last = nc.scalar.activation(QP[rows_, 4 * n:4 * n + 4, m, :], o[rows_, :, :], ACT.Copy,
                                                        scale=q_w[rows_, :])
                        last.then_inc(tp_read[STP[f"tq{n}"] % 2], 1)
                    o = see_turn(act, pos, STP["tk"])
                    nc.scalar.activation(kT[:, :, :], o[:, :, :], ACT.Copy, scale=k_w)\
                      .then_inc(tp_read[STP["tk"] % 2], 1)
                elif step == "wL":
                    w_exps(at[0])
                elif step == "wT":
                    k = at[0]
                    S = P * (k // 4 + 1)
                    o = see_turn(act, pos, STP[f"wT{k}"])
                    nc.scalar.activation(zg[k % 2][:, :, 0:S], o[:, :, 0:S], ACT.Copy)\
                      .then_inc(tp_read[STP[f"wT{k}"] % 2], 1)
                elif step == "wV":
                    k = at[0]
                    i, g = k // 4, k % 4
                    o = see_turn(act, pos, STP[f"wV{k}"])
                    nc.scalar.activation(attnT[:, 2 * g:2 * g + 2, i * P:(i + 1) * P], o[:, 0:2, 0:P], ACT.Copy)\
                      .then_inc(tp_read[STP[f"wV{k}"] % 2], 1)
                elif step == "turns":
                    act.wait_ge(angles, at[0] + 1)
                    nc.scalar.activation(rots[:, :, :], sd[0][:, :, :], ACT.Sin)
                    nc.scalar.activation(rotc[:, :, :], sd[1][:, :, :], ACT.Sin).then_inc(turned, 1)
            ahead("z0")
            act.wait_ge(skipped, NCT)
            nc.scalar.activation(uT[:, :, :], uT[:, :, :], ACT.Gelu_apprx_tanh)
            act.drain()
            after_group(act, pos, SG["ap3"])
            nc.scalar.activation(ysh[:, :, :], uT[:, :, :], ACT.Copy).then_inc(ys_hi, 1)
            for n in range(2):
                read_out(f"z{n}", zs[:, 4 * n:4 * n + 4, :], ACT.Silu)
            b_glu = SC["b_glu"].start
            for n in range(2):
                g = SG[f"glub{n}"]
                ahead(f"glub{n}")
                a = see_group(act, pos, g)
                if n:
                    act.drain()
                for b in range(4):
                    at = b_glu + 8 + 4 * n + b
                    last = nc.scalar.activation(sg2[:, b, :], a[:, b, :], ACT.Sigmoid, bias=spar[:, at:at + 1])
                last.then_inc(acc_read[g.parity], 1)
                ahead(f"glua{n}")
                act.wait_ge(glu_mul, n + 1)
                nc.scalar.activation(prh[:, 4 * n:4 * n + 4, :], sg2[:, :, :], ACT.Copy).then_inc(glu_hi, 1)
                if n == 0:
                    act.wait_ge(glu_split, 1)
            for n in range(4):
                if n:
                    act.wait_ge(merged_done, n)
                else:
                    act.wait_ge(glu_split, 2)
                read_out(f"gs{n}", sg2[:, :, :], ACT.Sigmoid)
                ahead(f"sp{n}")
            act.wait_ge(merged_done, 4)
            for n in range(4):
                nc.scalar.activation(xh[:, 4 * n:4 * n + 4, :], mixT[:, 4 * n:4 * n + 4, :], ACT.Copy)\
                  .then_inc(mix_hi, 1)
            ahead("out3")

        @block.vector
        def _(dve):
            def split(pos, u):
                s = u % SLOTS
                dve.wait_ge(hi_done, pos.n("unit", u + 1))
                nc.vector.tensor_tensor(lo[s][:, :, :], raw[s][:, :, :], hi[s][:, :, :].bitcast(F32),
                                        ALU.subtract).then_inc(split_done, 1)

            units = Splitter(split)

            def norm(pos, k, tag, turns, gain, src):
                for t in range(NT):
                    dve.wait_ge(in_roots, pos.n(8, 2 * k + t + 1))
                    nc.vector.tensor_scalar(y[:, t, :], src[:, t, :], rs[:, t:t + 1], None, ALU.mult)\
                      .then_inc(in_rows, 1)
                for q in range(4):
                    dve.wait_ge(x_hi, pos.n("hi", HIS.get(f"{tag}{q}", q) + 1))
                    o = tp[turns[f"{tag}{q}"] % 2]
                    for c in range(4):
                        last = nc.vector.scalar_tensor_tensor(xl[:, 4 * q + c, :], o[:, c, :], gain(4 * q + c),
                                                              xh[:, 4 * q + c, :].bitcast(F32), ALU.mult, ALU.subtract)
                    last.then_inc(tp_read[turns[f"{tag}{q}"] % 2], 1)

            def branch_out(pos, k, groups, add=False):
                def times_gain(n):
                    dve.wait_ge(out_squares, pos.n(12, 4 * k + n + 1))
                    part = y[:, :, n * W:(n + 1) * W]
                    nc.vector.tensor_tensor(part, part, gpost[:, n * W:(n + 1) * W].unsqueeze(1)
                                            .to_broadcast([P, NT, W]), ALU.mult)

                for n, g in enumerate(groups):
                    units.ahead(pos, g)
                    a = see_group(dve, pos, g)
                    part = y[:, :, n * W:(n + 1) * W]
                    if add:
                        nc.vector.tensor_tensor(part, part, a[:, :, :], ALU.add).then_inc(acc_read[g.parity], 1)
                    else:
                        nc.vector.tensor_copy(part, a[:, :, :]).then_inc(acc_read[g.parity], 1)
                    if n == 0:
                        dve.wait_ge(gpost_loaded, pos.n(48, 16 * (k + 1)))
                    else:
                        times_gain(n - 1)
                dve.wait_ge(out_squares, pos.n(12, 4 * k + 4))
                nc.vector.tensor_reduce(psum_, pss, AX.X, ALU.add).then_inc(out_sums, 1)
                times_gain(3)
                dve.drain()
                dve.wait_ge(out_roots, pos.n(3, k + 1))
                for t in range(NT):
                    nc.vector.scalar_tensor_tensor(h[:, t, :], y[:, t, :], prs[:, t:t + 1], h[:, t, :],
                                                   ALU.mult, ALU.add).then_inc(h_rows, 1)

            def maxima(k, src, heads, S, scale):
                nc.vector.tensor_reduce(mx[k % 2][:, 0:heads], src, AX.X, ALU.max)
                dve.drain()
                nc.vector.tensor_scalar(nmx[k % 2][:, 0:heads], mx[k % 2][:, 0:heads], -scale, None, ALU.mult)\
                  .then_inc(max_ready, 1)

            dve.sem_inc(split_done, SLOTS)
            for n in range(2):
                dve.sem_inc(acc_read[n], 1)
                dve.sem_inc(tp_read[n], 1)
            dve.wait_ge(start_loaded, 32)
            nc.vector.tensor_copy(relb[:, :, :], relt[:, :].unsqueeze(2).to_broadcast([32, 12, P])).then_inc(rel_spread, 1)
            dve.wait_ge(x_loaded, 16)
            dve.wait_ge(toep_copied, HA + HB)
            dve.wait_ge(ssm_exp, 1)
            a_re, a_im = spar[:, SC["A_re"]], spar[:, SC["A_im"]]
            nc.vector.tensor_tensor(sw[:, 1, :], sw[:, 0, :], a_re, ALU.mult)
            nc.vector.tensor_tensor(sw[:, 2, :], sw[:, 0, :], a_im, ALU.mult)
            dve.drain()
            reduce_angle(dve, sw[:, 3, :], sw[:, 2, :], sw[:, 4, :])
            cos_argument(dve, sw[:, 4, :], sw[:, 3, :], sw[:, 7, :])
            dve.drain().then_inc(ssm_ready, 1)
            nc.vector.tensor_copy(angle_hi[:, :], sw[:, 3, :])
            dve.drain()
            nc.vector.tensor_copy(ssm[:, 3, :], angle_hi[:, :].bitcast(F32))
            nc.vector.tensor_tensor(ssm[:, 4, :], sw[:, 3, :], angle_hi[:, :].bitcast(F32), ALU.subtract)
            dve.wait_ge(ssm_exp, 2)
            nc.vector.tensor_tensor(sw[:, 7, :], ssm[:, 0, :], sw[:, 6, :], ALU.mult)
            nc.vector.tensor_tensor(sw[:, 8, :], ssm[:, 0, :], sw[:, 5, :], ALU.mult)
            nc.vector.tensor_tensor(sw[:, 9, :], a_re, a_re, ALU.mult)
            nc.vector.tensor_tensor(sw[:, 10, :], a_im, a_im, ALU.mult)
            dve.drain()
            nc.vector.tensor_scalar(sw[:, 7, :], sw[:, 7, :], -1.0, None, ALU.add)
            nc.vector.tensor_tensor(sw[:, 9, :], sw[:, 9, :], sw[:, 10, :], ALU.add)
            dve.drain()
            nc.vector.reciprocal(sw[:, 9, :], sw[:, 9, :])
            nc.vector.tensor_tensor(sw[:, 10, :], sw[:, 7, :], a_re, ALU.mult)
            nc.vector.tensor_tensor(sw[:, 11, :], sw[:, 8, :], a_im, ALU.mult)
            nc.vector.tensor_tensor(sw[:, 12, :], sw[:, 8, :], a_re, ALU.mult)
            nc.vector.tensor_tensor(sw[:, 13, :], sw[:, 7, :], a_im, ALU.mult)
            dve.drain()
            nc.vector.tensor_tensor(sw[:, 10, :], sw[:, 10, :], sw[:, 11, :], ALU.add)
            nc.vector.tensor_tensor(sw[:, 12, :], sw[:, 12, :], sw[:, 13, :], ALU.subtract)
            dve.drain()
            nc.vector.tensor_tensor(ssm[:, 1, :], sw[:, 10, :], sw[:, 9, :], ALU.mult)
            nc.vector.tensor_tensor(ssm[:, 2, :], sw[:, 12, :], sw[:, 9, :], ALU.mult)
            dve.drain()
            dve.sem_inc(h_rows, NT)
            units.ahead(Pos(0), Group("", 0, 0, "T", 0, 0))

            with dve.Fori(0, L) as layer:
                pos = Pos(layer)
                dve.wait_ge(par_loaded, pos.n(32, 32))
                lam = row[:, BR["lam"]].rearrange("p (a b n) -> p a b n", a=2, b=2)
                nc.vector.tensor_tensor(lamp, lam[:, :, 0, :], lam[:, :, 1, :], ALU.mult)
                dve.drain()
                nc.vector.tensor_reduce(lamv, lamp, AX.X, ALU.add).then_inc(lam_ready, 1)
                dve.wait_ge(lam_exp, pos.n(1, 1))
                nc.vector.tensor_tensor(nlam, lame[:, 1:2], lame[:, 0:1], ALU.subtract)
                dve.drain()
                nc.vector.tensor_tensor(nlam, nlam, pcol("neg_lam_init"), ALU.add)
                nc.vector.tensor_tensor(subg, pcol("sub_g"), pcol("one_minus_lam_init"), ALU.mult).then_inc(lam_ready, 1)

                norm(pos, 0, "mem", LTP, lambda c: pcol("mem_g", c), y)
                units.ahead(pos, LG["mem_v"])
                norm(pos, 1, "pre", LTP, lambda c: pcol("mix_pre_g", c), h)
                units.ahead(pos, LG["cv"])

                after_group(dve, pos, LG["cv"])
                for t in range(NT):
                    nc.vector.bn_stats(vst[:, t, :], cv[:, t, :])
                dve.drain()
                for t in range(NT):
                    last = nc.vector.bn_aggr(vmv[:, t, :], vst[:, t, :])
                last.then_inc(v_stats, 1)

                def a_max(k):
                    i, hp = PAIRS[k]
                    S = P * (i + 1)
                    o = see_turn(dve, pos, LTP[f"aL{k}"])
                    for m in range(2):
                        last = nc.vector.scalar_tensor_tensor(lg[k % 2][:, 2 * m:2 * m + 2, 0:S],
                                                              o[:, 2 * m:2 * m + 2, 0:S], SCALE_A,
                                                              bias[:, 2 * hp:2 * hp + 2, T - S:T], ALU.mult, ALU.add)
                    last.then_inc(tp_read[LTP[f"aL{k}"] % 2], 1)
                    dve.drain()
                    maxima(k, lg[k % 2][:, :, 0:S], 4, S, 1.0)

                dve.wait_ge(bias_ready, 1)
                a_max(0)
                for k, (i, hp) in enumerate(PAIRS):
                    if k < 5:
                        a_max(k + 1)
                    S = P * (i + 1)
                    e, r = pe_[k % 2], rc[k % 2]
                    dve.wait_ge(exp_ready, pos.n(12, k + 1))
                    nc.vector.reciprocal(r, sm[k % 2])
                    dve.drain()
                    nc.vector.tensor_scalar(r[:, 2:4], r[:, 2:4], nlam, None, ALU.mult)
                    dve.drain()
                    for hh in range(2):
                        nc.vector.tensor_scalar(e[:, 2 + hh, 0:S], e[:, 2 + hh, 0:S], r[:, 2 + hh:3 + hh], None, ALU.mult)
                    dve.drain()
                    for hh in range(2):
                        last = nc.vector.scalar_tensor_tensor(lg[k % 2][:, hh, 0:S], e[:, hh, 0:S], r[:, hh:hh + 1],
                                                              e[:, 2 + hh, 0:S], ALU.mult, ALU.add)
                    last.then_inc(weights_ready, 1)
                after_turn(dve, pos, LTP["aV4"])
                after_turn(dve, pos, LTP["aV5"])
                sq = junk[:, 0:NT * HA * P]
                nc.vector.tensor_tensor(sq, flat(oa), flat(oa), ALU.mult)
                dve.drain()
                nc.vector.tensor_reduce(oss, sq.rearrange("p (n d) -> p n d", d=P), AX.X, ALU.add)\
                  .then_inc(oa_squares, 1)
                dve.wait_ge(oa_roots, pos.n(1, 1))
                heads = flat(oa).rearrange("p (n d) -> p n d", d=P)
                nc.vector.tensor_tensor(heads, heads, ors.unsqueeze(2).to_broadcast([P, 12, P]), ALU.mult)\
                  .then_inc(oa_rows, 1)

                dve.wait_ge(v_roots, pos.n(1, 1))
                for t in range(NT):
                    nc.vector.tensor_scalar(cv[:, t, :], cv[:, t, :], vmv[:, t, 0:1], vrs[:, t:t + 1],
                                            ALU.subtract, ALU.mult)
                dve.drain()
                nc.vector.tensor_tensor(cv[:, :, :], cv[:, :, :],
                                        row[:, BR["ln_g"]].unsqueeze(1).to_broadcast([P, NT, W]), ALU.mult)
                dve.drain()
                nc.vector.tensor_tensor(cv[:, :, :], cv[:, :, :],
                                        row[:, BR["ln_b"]].unsqueeze(1).to_broadcast([P, NT, W]), ALU.add)\
                  .then_inc(v_rows, 1)
                o = see_turn(dve, pos, LTP["c"])
                for t in range(NT):
                    last = nc.vector.tensor_tensor(mixT[:, 12:16, t * P:(t + 1) * P], o[:, :, t * P:(t + 1) * P],
                                                   row[:, BR["b_s"]].rearrange("p (g t) -> p g t", t=P), ALU.add)
                last.then_inc(tp_read[LTP["c"] % 2], 1)
                dve.drain()
                nc.vector.tensor_tensor(mixT[:, 12:16, :], mixT[:, 12:16, :], cuT[:, :, :], ALU.mult)\
                  .then_inc(gated_c, 1)

                dve.wait_ge(lat_roots, pos.n(1, 1))
                for t in range(NT):
                    nc.vector.tensor_scalar(cq[:, t, :], cq[:, t, :], lrs[:, t:t + 1], None, ALU.mult)
                    nc.vector.tensor_scalar(ckv[:, t, 0:2 * P], ckv[:, t, 0:2 * P], lrs[:, 2 + t:3 + t], None, ALU.mult)
                    for m in range(2):
                        nc.vector.tensor_copy(kk[:, t, 64 * m:64 * m + 64], ckv[:, t, 256:320])
                nc.vector.tensor_scalar(widx, ckv[:, :, 320:336], float(NIDX ** -0.5), None, ALU.mult)\
                  .then_inc(lat_rows, 1)
                dve.wait_ge(x_hi, pos.n("hi", HIS["bq"] + 1))
                o = tp[LTP["bq"] % 2]
                for c in range(4):
                    last = nc.vector.scalar_tensor_tensor(cql[:, c, :], o[:, c, :], pcol("cq_g", c),
                                                          cqh[:, c, :].bitcast(F32), ALU.mult, ALU.subtract)
                last.then_inc(tp_read[LTP["bq"] % 2], 1)
                dve.wait_ge(x_hi, pos.n("hi", HIS["bkv"] + 1))
                o = tp[LTP["bkv"] % 2]
                for c in range(2):
                    last = nc.vector.scalar_tensor_tensor(ckl[:, c, :], o[:, c, :], pcol("ckv_g", c),
                                                          ckh[:, c, :].bitcast(F32), ALU.mult, ALU.subtract)
                last.then_inc(tp_read[LTP["bkv"] % 2], 1)
                units.ahead(pos, LG["qi1"])

                for i in range(NT):
                    S = P * (i + 1)
                    for b in range(4):
                        n = 4 * i + b
                        for hh in range(4):
                            g = 4 * b + hh
                            dots = pe_[n % 2][:, hh, 0:S]
                            dve.drain()
                            if hh == 0:
                                after_turn(dve, pos, LTP[f"ix{i}_{b}"])
                            if g == 0:
                                last = nc.vector.tensor_scalar(sc[:, i, 0:S], dots, widx[:, i, g:g + 1], None, ALU.mult)
                            else:
                                last = nc.vector.scalar_tensor_tensor(sc[:, i, 0:S], dots, widx[:, i, g:g + 1],
                                                                      sc[:, i, 0:S], ALU.mult, ALU.add)
                        last.then_inc(dots_used, 1)
                for i in range(NT):
                    S = P * (i + 1)
                    hold(dve, score_masked, pos.n(2, i + 1), passed)
                    for n in range(TOPK // 8):
                        nc.vector.max(m8, sc[:, i, 0:S])
                        dve.drain()
                        nc.vector.match_replace(sc[:, i, 0:S], m8, sc[:, i, 0:S], TAKEN)
                        dve.drain()
                    nc.vector.tensor_scalar(sc[:, i, 0:S], sc[:, i, 0:S], 0.5 * (FILL + TAKEN), NEG, ALU.is_ge, ALU.mult)
                    dve.drain()

                def b_max(k):
                    i, hp = PAIRS[k]
                    S = P * (i + 1)
                    o = see_turn(dve, pos, LTP[f"bL{k}"])
                    z = lg[k % 2][:, 0:2, 0:S]
                    nc.vector.scalar_tensor_tensor(z, o[:, 0:2, 0:S], SCALE_B, bias[:, HA + 2 * hp:HA + 2 * hp + 2, T - S:T],
                                                   ALU.mult, ALU.add).then_inc(tp_read[LTP[f"bL{k}"] % 2], 1)
                    dve.drain()
                    nc.vector.tensor_tensor(z, z, sc[:, i, 0:S].unsqueeze(1).to_broadcast([P, 2, S]), ALU.add)
                    dve.drain()
                    maxima(k, z, 2, S, 1.0)

                b_max(0)
                for k, (i, hp) in enumerate(PAIRS):
                    if k < 5:
                        b_max(k + 1)
                    dve.wait_ge(exp_ready, pos.n(12, 6 + k + 1))
                    nc.vector.reciprocal(rc[k % 2][:, 0:2], sm[k % 2][:, 0:2])
                    dve.drain()
                    for hh in range(2):
                        e = pe_[k % 2][:, hh, 0:P * (i + 1)]
                        last = nc.vector.tensor_scalar(e, e, rc[k % 2][:, hh:hh + 1], None, ALU.mult)
                    last.then_inc(weights_ready, 1)

                for n in range(4):
                    dve.wait_ge(mix_hi, pos.n(4, n + 1))
                    nc.vector.tensor_tensor(xl[:, 4 * n:4 * n + 4, :], mixT[:, 4 * n:4 * n + 4, :],
                                            xh[:, 4 * n:4 * n + 4, :].bitcast(F32), ALU.subtract)\
                      .then_inc(mix_split, 1)
                branch_out(pos, 0, [LG[f"wo{n}"] for n in range(4)])
                dve.drain()

                norm(pos, 2, "xpre", LTP, lambda c: pcol("x_pre_g", c), h)
                units.ahead(pos, LG["xq"])
                for i in range(NT):
                    o = see_turn(dve, pos, LTP[f"xL{i}"])
                    maxima(i, o[:, :, :], 4, T, SCALE_B)
                for i in range(NT):
                    after_turn(dve, pos, LTP[f"xL{i}"])
                    nc.vector.reciprocal(rc[i], sm[i])
                    dve.drain()
                    nc.vector.tensor_tensor(pe_[i][:, :, :], pe_[i][:, :, :], rc[i].unsqueeze(2).to_broadcast([P, HX, T]),
                                            ALU.mult).then_inc(weights_ready, 1)
                for i in range(NT):
                    dve.wait_ge(x_hi, pos.n("hi", HIS[f"xV{i}"] + 1))
                    o = tp[LTP[f"xV{i}"] % 2]
                    nc.vector.tensor_tensor(cql[:, :, i * P:(i + 1) * P], o[:, :, 0:P],
                                            cqh[:, :, i * P:(i + 1) * P].bitcast(F32), ALU.subtract)\
                      .then_inc(tp_read[LTP[f"xV{i}"] % 2], 1)
                branch_out(pos, 1, [LG[f"xo{n}"] for n in range(4)])
                dve.drain()

                norm(pos, 3, "fpre", LTP, lambda c: pcol("f_pre_g", c), h)
                nc.vector.memset(y[:, :, :], 0.0)

                def across(pos, j):
                    dve.wait_ge(x_hi, pos.n("hi", HIS[f"h{j}"] + 1))
                    o = tp[LTP[f"h{j}"] % 2]
                    nc.vector.tensor_tensor(hTl[:, :, :], o[:, :, :], hTh[:, :, :].bitcast(F32), ALU.subtract)\
                      .then_inc(tp_read[LTP[f"h{j}"] % 2], 1)

                def gate(pos, j):
                    g = LG[f"up{j}"]
                    units.ahead(pos, g)
                    after_group(dve, pos, LG[f"gate{j}"])
                    a = see_group(dve, pos, g)
                    nc.vector.tensor_tensor(hm[j % 2][:, :, :], sg[:, :, :], a[:, :, :], ALU.mult)\
                      .then_inc(acc_read[g.parity], 1)
                    dve.drain().then_inc(gated, 1)

                def down(pos, j):
                    for n in range(4):
                        g = LG[f"down{j}_{n}"]
                        units.ahead(pos, g)
                        a = see_group(dve, pos, g)
                        nc.vector.tensor_tensor(y[:, :, n * W:(n + 1) * W], y[:, :, n * W:(n + 1) * W], a[:, :, :],
                                                ALU.add).then_inc(acc_read[g.parity], 1)

                gate(pos, 0)
                with dve.Fori(0, (NJ - 1) // 2) as turn:
                    here = Pos(layer, turn)
                    for j in (1, 2):
                        units.ahead(here, LG[f"gate{j}"])
                        across(here, j - 1)
                        gate(here, j)
                        down(here, j - 1)
                units.next = LG[f"down{NJ - 2}_3"].end + units.LEAD
                across(pos, NJ - 1)
                branch_out(pos, 2, [LG[f"down{NJ - 1}_{n}"] for n in range(4)], add=True)
                dve.drain()
                units.new_layer()

            pos = Pos(L)

            def ahead(name):
                units.ahead(pos, SG[name], SU)

            dve.wait_ge(par2_loaded, 16)
            norm(pos, 0, "norm", STP, lambda c: spar[:, SC["norm_w"].start + c:SC["norm_w"].start + c + 1], h)
            for m in range(2):
                nc.vector.memset(cpad[m][:, :], 0.0)
            ahead("kv")
            for name in ("q0", "q1", "kv"):
                after_group(dve, pos, SG[name])

            def head_rows():
                sq = y[:, 0, :]
                nc.vector.tensor_tensor(sq, flat(qt), flat(qt), ALU.mult)
                dve.drain()
                nc.vector.tensor_reduce(qss[:, 0:32], sq.rearrange("p (n d) -> p n d", d=64), AX.X, ALU.add)
                dve.drain()
                sq = y[:, 0, 0:NT * 256].rearrange("p (t d) -> p t d", t=NT)
                nc.vector.tensor_tensor(sq, kv[:, :, 0:256], kv[:, :, 0:256], ALU.mult)
                dve.drain()
                nc.vector.tensor_reduce(qss[:, 32:40], sq.rearrange("p t (n d) -> p (t n) d", d=64), AX.X, ALU.add)\
                  .then_inc(q_squares, 1)
                dve.wait_ge(q_roots, 1)
                rows_ = flat(qt).rearrange("p (n d) -> p n d", d=64)
                nc.vector.tensor_tensor(rows_, rows_, qrs[:, 0:32].unsqueeze(2).to_broadcast([P, 32, 64]), ALU.mult)
                units.before(pos, SG["u0"], 3, SU)
                dve.drain()
                for t in range(NT):
                    keys = kv[:, t, 0:256].rearrange("p (g d) -> p g d", d=64)
                    vals = kv[:, t, 256:512].rearrange("p (g d) -> p g d", d=64)
                    roots_ = qrs[:, 32 + 4 * t:36 + 4 * t].unsqueeze(2).to_broadcast([P, 4, 64])
                    for m in range(2):
                        nc.vector.tensor_tensor(kdup[:, t, :, m, :], keys, roots_, ALU.mult)
                        last = nc.vector.tensor_copy(vpad[:, t, :, m, 64 * m:64 * m + 64], vals)
                last.then_inc(q_rows, 1)

            def w_max(k):
                i, g = k // 4, k % 4
                S = P * (i + 1)
                o = see_turn(dve, pos, STP[f"wL{k}"])
                sinks_ = sink[:, 4 * g:4 * g + 4]
                nc.vector.scalar_tensor_tensor(zg[k % 2][:, :, 0:S], o[:, :, 0:S], SCALE_A,
                                               window[:, T - S:T].unsqueeze(1).to_broadcast([P, 4, S]),
                                               ALU.mult, ALU.add).then_inc(tp_read[STP[f"wL{k}"] % 2], 1)
                dve.drain()
                nc.vector.tensor_reduce(mx[k % 2], zg[k % 2][:, :, 0:S], AX.X, ALU.max)
                dve.drain()
                nc.vector.tensor_tensor(mx[k % 2], mx[k % 2], sinks_, ALU.max)
                dve.drain()
                nc.vector.tensor_scalar(nmx[k % 2], mx[k % 2], -1.0, None, ALU.mult)
                nc.vector.tensor_tensor(snk[k % 2], sinks_, mx[k % 2], ALU.subtract).then_inc(max_ready, 1)

            for step, *at in SMIX:
                if step == "unit":
                    units.before(pos, *at, SU)
                elif step == "head_rows":
                    head_rows()
                elif step == "wL":
                    if at[0] == 0:
                        dve.wait_ge(window_ready, 1)
                        dve.wait_ge(sink_loaded, 16)
                    w_max(at[0])
                elif step == "w_weights":
                    k = at[0]
                    S = P * (k // 4 + 1)
                    dve.wait_ge(exp_ready, pos.n(12, k + 1))
                    nc.vector.tensor_tensor(sm[k % 2], sm[k % 2], esk[k % 2], ALU.add)
                    dve.drain()
                    nc.vector.reciprocal(rc[k % 2], sm[k % 2])
                    dve.drain()
                    e = ze[k % 2][:, :, 0:S]
                    nc.vector.tensor_tensor(e, e, rc[k % 2].unsqueeze(2).to_broadcast([P, 4, S]), ALU.mult)\
                      .then_inc(weights_ready, 1)
                elif step == "out":
                    name = at[0]
                    n = int(name[-1])
                    if name in ("ag0", "ag1"):
                        after_group(dve, pos, SG[name])
                        if n == 0:
                            after_turn(dve, pos, STP["wV6"])
                            after_turn(dve, pos, STP["wV7"])
                        part = attnT[:, 4 * n:4 * n + 4, :]
                        nc.vector.tensor_tensor(part, part, sg2[:, :, :], ALU.mult).then_inc(ag_mul, 1)
                        dve.wait_ge(ag_hi, n + 1)
                        nc.vector.tensor_tensor(gatl[:, 4 * n:4 * n + 4, :], part,
                                                gath[:, 4 * n:4 * n + 4, :].bitcast(F32), ALU.subtract)\
                          .then_inc(ag_split, 1)
                    elif name in ("ap0", "ap1", "ap2", "ap3"):
                        g = SG[name]
                        after_group(dve, pos, SG[f"ga{n}"])
                        a = see_group(dve, pos, g)
                        nc.vector.tensor_tensor(mixT[:, 4 * n:4 * n + 4, :], sg2[:, :, :], a[:, :, :], ALU.mult)\
                          .then_inc(acc_read[g.parity], 1)
                elif step == "angles":
                    c = at[0]
                    tiles = range(4 * c, 4 * c + 4)
                    for j, s in enumerate(tiles):
                        nc.vector.tensor_scalar(st[:, j, :], iota[:, :], ssm[:, 3, s:s + 1], None, ALU.mult)
                    dve.drain()
                    nc.vector.tensor_scalar(sr[0][:, :, :], st[:, :, :], 1.0 / (2 * math.pi), ROUND, ALU.mult, ALU.add)
                    dve.drain()
                    nc.vector.tensor_scalar(sr[0][:, :, :], sr[0][:, :, :], -ROUND, None, ALU.add)
                    dve.drain()
                    nc.vector.scalar_tensor_tensor(st[:, :, :], sr[0][:, :, :], -TWO_PI_HI, st[:, :, :], ALU.mult, ALU.add)
                    dve.drain()
                    nc.vector.scalar_tensor_tensor(st[:, :, :], sr[0][:, :, :], -TWO_PI_MID, st[:, :, :], ALU.mult, ALU.add)
                    dve.drain()
                    for j, s in enumerate(tiles):
                        nc.vector.scalar_tensor_tensor(st[:, j, :], iota[:, :], ssm[:, 4, s:s + 1], st[:, j, :],
                                                       ALU.mult, ALU.add)
                    dve.drain()
                    nc.vector.tensor_scalar(sd[0][:, :, :], st[:, :, :], PI_IN, -PI_IN, ALU.min, ALU.max)
                    dve.drain()
                    cos_argument(dve, sd[1][:, :, :], sd[0][:, :, :], st[:, :, :])
                    dve.drain().then_inc(angles, 1)
                elif step == "maps":
                    c = at[0]
                    dve.wait_ge(bc_loaded[c % 2], 32 * (c // 2 + 1))
                    gain = [ssm[:, 1 + m, 4 * c:4 * c + 4].unsqueeze(2).to_broadcast([P, 4, 32]) for m in range(2)]
                    diag = [cpad[m][:, :].rearrange("p (j w) -> p j w", w=160)[:, :, 0:32] for m in range(2)]
                    tmp = [small[:, 256:384].rearrange("p (j w) -> p j w", w=32), craw2[:, :, :]]
                    nc.vector.tensor_tensor(tmp[0], craw[:, 0, :, :], gain[0], ALU.mult)
                    nc.vector.tensor_tensor(tmp[1], craw[:, 1, :, :], gain[1], ALU.mult)
                    dve.drain()
                    nc.vector.tensor_tensor(diag[0], tmp[0], tmp[1], ALU.subtract)
                    dve.drain()
                    nc.vector.tensor_tensor(tmp[0], craw[:, 0, :, :], gain[1], ALU.mult)
                    nc.vector.tensor_tensor(tmp[1], craw[:, 1, :, :], gain[0], ALU.mult)
                    dve.drain()
                    nc.vector.scalar_tensor_tensor(diag[1], tmp[0], -1.0, tmp[1], ALU.mult, ALU.subtract)
                elif step == "back":
                    c = at[0]
                    dve.wait_ge(turned, c + 1)
                    o = see_turn(dve, pos, STP[f"s{c}_re"])
                    nc.vector.tensor_tensor(sd[0][:, :, :], o[:, :, :], rotc[:, :, :], ALU.mult)
                    nc.vector.tensor_tensor(sr[0][:, :, :], o[:, :, :], rots[:, :, :], ALU.mult)\
                      .then_inc(tp_read[STP[f"s{c}_re"] % 2], 1)
                    o = see_turn(dve, pos, STP[f"s{c}_im"])
                    nc.vector.tensor_tensor(sd[1][:, :, :], o[:, :, :], rotc[:, :, :], ALU.mult)
                    nc.vector.tensor_tensor(st[:, :, :], o[:, :, :], rots[:, :, :], ALU.mult)\
                      .then_inc(tp_read[STP[f"s{c}_im"] % 2], 1)
                    dve.drain()
                    nc.vector.tensor_tensor(sd[0][:, :, :], sd[0][:, :, :], st[:, :, :], ALU.add)
                    nc.vector.tensor_tensor(sd[1][:, :, :], sd[1][:, :, :], sr[0][:, :, :], ALU.subtract)
                    dve.drain()
                elif step == "scan":
                    c = at[0]
                    tiles = range(4 * c, 4 * c + 4)
                    for j, s in enumerate(tiles):
                        for m in range(2):
                            nc.vector.tensor_tensor_scan(sr[m][:, j, :], ssm[:, 0, s:s + 1].to_broadcast([P, T]),
                                                         sd[m][:, j, :], 0.0, ALU.mult, ALU.add)
                    dve.drain()
                elif step == "forward":
                    c = at[0]
                    nc.vector.tensor_tensor(sd[0][:, :, :], sr[0][:, :, :], rotc[:, :, :], ALU.mult)
                    nc.vector.tensor_tensor(st[:, :, :], sr[1][:, :, :], rots[:, :, :], ALU.mult)
                    nc.vector.tensor_tensor(sd[1][:, :, :], sr[0][:, :, :], rots[:, :, :], ALU.mult)
                    dve.drain()
                    nc.vector.tensor_tensor(sd[0][:, :, :], sd[0][:, :, :], st[:, :, :], ALU.subtract)
                    dve.drain()
                    nc.vector.tensor_tensor(st[:, :, :], sr[1][:, :, :], rotc[:, :, :], ALU.mult)
                    dve.drain()
                    nc.vector.tensor_tensor(sd[1][:, :, :], sd[1][:, :, :], st[:, :, :], ALU.add).then_inc(states, 1)
                elif step == "skip":
                    c = at[0]
                    o = see_turn(dve, pos, STP[f"s{c}_y"])
                    col = SC["skip"].start + c
                    nc.vector.scalar_tensor_tensor(uT[:, c, :], uT[:, c, :], spar[:, col:col + 1], o[:, 0, :],
                                                   ALU.mult, ALU.add).then_inc(tp_read[STP[f"s{c}_y"] % 2], 1)
                    dve.drain().then_inc(skipped, 1)
            ahead("z0")
            dve.wait_ge(ys_hi, 1)
            nc.vector.tensor_tensor(ysl[:, :, :], uT[:, :, :], ysh[:, :, :].bitcast(F32), ALU.subtract)\
              .then_inc(ys_split, 1)
            ahead("z1")
            for n in range(2):
                g = SG[f"glua{n}"]
                ahead(f"glub{n}")
                ahead(f"glua{n}")
                after_group(dve, pos, SG[f"glub{n}"])
                a = see_group(dve, pos, g)
                for b in range(4):
                    at = SC["b_glu"].start + 4 * n + b
                    last = nc.vector.scalar_tensor_tensor(sg2[:, b, :], a[:, b, :], spar[:, at:at + 1], sg2[:, b, :],
                                                          ALU.add, ALU.mult)
                last.then_inc(acc_read[g.parity], 1)
                dve.drain()
                if n == 0:
                    after_group(dve, pos, SG["z0"])
                    after_group(dve, pos, SG["z1"])
                nc.vector.tensor_tensor(sg2[:, :, :], sg2[:, :, :], zs[:, 4 * n:4 * n + 4, :], ALU.mult)\
                  .then_inc(glu_mul, 1)
                dve.wait_ge(glu_hi, n + 1)
                nc.vector.tensor_tensor(prl[:, 4 * n:4 * n + 4, :], sg2[:, :, :], prh[:, 4 * n:4 * n + 4, :].bitcast(F32),
                                        ALU.subtract).then_inc(glu_split, 1)
            for n in range(4):
                g = SG[f"sp{n}"]
                ahead(f"gs{n}")
                ahead(f"sp{n}")
                after_group(dve, pos, SG[f"gs{n}"])
                a = see_group(dve, pos, g)
                nc.vector.tensor_tensor(sg2[:, :, :], sg2[:, :, :], a[:, :, :], ALU.mult).then_inc(acc_read[g.parity], 1)
                dve.drain()
                part = mixT[:, 4 * n:4 * n + 4, :]
                nc.vector.tensor_tensor(part, part, sg2[:, :, :], ALU.add).then_inc(merged_done, 1)
            for n in range(4):
                dve.wait_ge(mix_hi, pos.n(4, n + 1))
                nc.vector.tensor_tensor(xl[:, 4 * n:4 * n + 4, :], mixT[:, 4 * n:4 * n + 4, :],
                                        xh[:, 4 * n:4 * n + 4, :].bitcast(F32), ALU.subtract)\
                  .then_inc(mix_split, 1)
            for n in range(4):
                g = SG[f"out{n}"]
                ahead(f"out{n}")
                a = see_group(dve, pos, g)
                part = h[:, :, n * W:(n + 1) * W]
                nc.vector.tensor_tensor(part, part, a[:, :, :], ALU.add).then_inc(acc_read[g.parity], 1)

        @block.gpsimd
        def _(pool):
            def roots(out, src, scale, n, signal, tmp=None):
                nc.gpsimd.tensor_scalar(out, src, scale, EPS, ALU.mult, ALU.add)
                pool.drain()
                nc.gpsimd.tensor_tensor(out, out, mhalf[:, 0:n], ALU.pow).then_inc(signal, 1)

            nc.gpsimd.memset(flat(QP), 0.0)
            nc.gpsimd.memset(mhalf[:, :], -0.5)
            nc.gpsimd.memset(ident[:, :], 0.0)
            pool.drain()
            nc.gpsimd.affine_select(out=ident[:, :], in_=ident[:, :], compare_op=ALU.not_equal, fill=1.0,
                                    base=0, pattern=[[-1, P]], channel_multiplier=1).then_inc(const_ready, 1)
            pool.wait_ge(toep_moved, 48)
            nc.gpsimd.affine_select(out=bias[:, :, P:T], in_=bias[:, :, P:T], compare_op=ALU.is_ge, fill=NEG,
                                    base=0, pattern=[[0, HA + HB], [-1, P]], channel_multiplier=1)\
              .then_inc(bias_ready, 1)
            nc.gpsimd.iota(iota[:, :], [[1, T]], base=0, channel_multiplier=0, allow_small_or_imprecise_dtypes=True)

            with pool.Fori(0, L) as layer:
                pos = Pos(layer)

                def load_gain(k):
                    pool.wait_ge(h_rows, pos.n(6, 2 * k + 2))
                    pool.dma_start(gpost[:, :], post_g[bass.ds(layer * 3 + k, 1), :].to_broadcast([P, D]))\
                        .then_inc(gpost_loaded, 16)

                def norm(k):
                    for t in range(NT):
                        hold(pool, in_squares, pos.n(8, 2 * k + t + 1), passed)
                        roots(rs[:, t:t + 1], ss[:, t:t + 1], 1.0 / D, 1, in_roots)

                def norm_out(k):
                    hold(pool, out_sums, pos.n(3, k + 1), passed)
                    roots(prs, psum_, 1.0 / D, 2, out_roots)

                pool.wait_ge(h_rows, pos.n(6, 2))
                pool.dma_start(par[:, :], params[bass.ds(layer * P, P), :]).then_inc(par_loaded, 16)
                pool.dma_start(row[:, :], rows[bass.ds(layer, 1), :].to_broadcast([P, NBR])).then_inc(par_loaded, 16)
                pool.dma_start(y[:, :, :], mem.rearrange("(t p) d -> p t d", p=P)).then_inc(mem_loaded, 16)
                load_gain(0)
                hold(pool, par_loaded, pos.n(32, 32), passed)
                cw = par[:, PC["c_w"]].rearrange("p (g t) -> p g t", t=P)
                nc.gpsimd.affine_select(out=cw, in_=cw, compare_op=ALU.is_ge, fill=0.0, base=0,
                                        pattern=[[0, 4], [1, P]], channel_multiplier=-1).then_inc(cw_ready, 1)
                norm(0)
                norm(1)
                hold(pool, v_stats, pos.n(1, 1), passed)
                roots(vrs, vmv[:, :, 1], 1.0, 2, v_roots)
                hold(pool, oa_squares, pos.n(1, 1), passed)
                roots(ors, oss, 1.0 / P, 12, oa_roots)
                hold(pool, lat_squares, pos.n(1, 1), passed)
                nc.gpsimd.tensor_scalar(lrs[:, 0:2], lss[:, 0:2], 1.0 / W, EPS, ALU.mult, ALU.add)
                nc.gpsimd.tensor_scalar(lrs[:, 2:4], lss[:, 2:4], 1.0 / (2 * P), EPS, ALU.mult, ALU.add)
                pool.drain()
                nc.gpsimd.tensor_tensor(lrs, lrs, mhalf[:, 0:4], ALU.pow).then_inc(lat_roots, 1)
                for i in range(NT):
                    hold(pool, dots_used, pos.n(8, 4 * i + 4), passed)
                    nc.gpsimd.affine_select(out=sc[:, i, 0:P * (i + 1)], in_=sc[:, i, 0:P * (i + 1)],
                                            compare_op=ALU.is_ge, fill=FILL, base=P * i,
                                            pattern=[[-1, P * (i + 1)]], channel_multiplier=1).then_inc(score_masked, 1)
                norm_out(0)
                load_gain(1)
                norm(2)
                norm_out(1)
                load_gain(2)
                norm(3)
                norm_out(2)

            pos = Pos(L)
            pool.wait_ge(h_rows, pos.n(6, 2))
            nc.gpsimd.memset(flat(vpad), 0.0)
            pool.dma_start(sink[:, :], sinks.to_broadcast([P, NQ])).then_inc(sink_loaded, 16)
            nc.gpsimd.memset(window[:, :], 0.0)
            pool.drain()
            nc.gpsimd.affine_select(out=window[:, 0:P], in_=window[:, 0:P], compare_op=ALU.is_gt, fill=NEG, base=0,
                                    pattern=[[1, P]], channel_multiplier=-1)
            nc.gpsimd.affine_select(out=window[:, P:T], in_=window[:, P:T], compare_op=ALU.is_ge, fill=NEG, base=0,
                                    pattern=[[-1, P]], channel_multiplier=1).then_inc(window_ready, 1)
            for t in range(NT):
                pool.wait_ge(in_squares, pos.n(8, t + 1))
                roots(rs[:, t:t + 1], ss[:, t:t + 1], 1.0 / D, 1, in_roots)
            pool.wait_ge(q_squares, 1)
            roots(qrs, qss, 1.0 / 64, 40, q_roots)
            for c in range(NCT):
                if c == 0:
                    pool.wait_ge(weights_ready, pos.n(14, 8))
                    after_turn(pool, pos, STP["wV7"])
                    after_turn(pool, pos, STP["wV6"])
                if c >= 1:
                    pool.wait_ge(states, c)
                pool.dma_start(flat(craw), c_pack[c * P:(c + 1) * P, :]).then_inc(bc_loaded[c % 2], 16)
                if c >= 2:
                    after_turn(pool, pos, STP[f"s{c - 2}_im"])
                pool.dma_start(flat(bpad[c % 2]), b_pad[c * P:(c + 1) * P, :]).then_inc(bc_loaded[c % 2], 16)


def bucket_rows():
    n = np.maximum(T - 1 - np.arange(TOEP), 0)
    nf = np.maximum(n, 1).astype(np.float32)
    large = 16 + (np.log(nf / np.float32(16)) / np.float32(math.log(8.0)) * 16).astype(np.int32)
    bucket = np.where(n < 16, n, np.minimum(large, 31))
    return (bucket[None, :] == np.arange(32)[:, None]).astype(np.float32)


def units_of(w, group):
    w = np.asarray(w)
    k, width = w.shape
    assert k == group.kchunks * P and width == group.width, (group.name, w.shape)
    out = np.zeros((group.units, P, KU, W), w.dtype)
    out[..., :width] = w.reshape(group.units, KU, P, width).transpose(0, 2, 1, 3)
    return out.reshape(group.units, P, KU * W)


def columns(v):
    return np.asarray(v).reshape(-1, P).T


def layer_blocks(a, l):
    w_in = a["w_in"][l]
    blocks = {"mem_k": a["x_wkv"][l][:, 0].reshape(D, W), "mem_v": a["x_wkv"][l][:, 1].reshape(D, W)}
    for n in range(3):
        blocks[f"qk{n}"] = w_in[:, n * W:(n + 1) * W]
    for name, lo_, hi_ in (("va0", 1536, 2048), ("va1", 2048, 2304), ("cq", 2304, 2816), ("ckv", 2816, 3152),
                           ("cu", 3152, 3664), ("cv", 3664, 4176)):
        blocks[name] = w_in[:, lo_:hi_]
    for tag, w in (("uq", a["b_w_uq"]), ("uk", a["b_w_uk"]), ("uv", a["b_w_uv"])):
        w = w[l].reshape(w.shape[1], -1)
        blocks[f"{tag}0"], blocks[f"{tag}1"] = w[:, :W], w[:, W:]
    w = a["b_w_qidx"][l].reshape(W, -1)
    blocks["qi0"], blocks["qi1"] = w[:, :W], w[:, W:]
    blocks["xq"] = a["x_wq"][l].reshape(D, W)
    xo = a["x_wo"][l].reshape(W, D)
    for n in range(4):
        blocks[f"wo{n}"] = a["w_out"][l][:, n * W:(n + 1) * W]
        blocks[f"xo{n}"] = xo[:, n * W:(n + 1) * W]
    for j in range(NJ):
        blocks[f"gate{j}"] = a["f_w_gu"][l][:, 0, j * W:(j + 1) * W]
        blocks[f"up{j}"] = a["f_w_gu"][l][:, 1, j * W:(j + 1) * W]
        for n in range(4):
            blocks[f"down{j}_{n}"] = a["f_w_down"][l][j * W:(j + 1) * W, n * W:(n + 1) * W]
    return blocks


def layer_params(a, l):
    lam_init = 0.8 - 0.6 * math.exp(-0.3 * l)
    ones = np.ones((P, 1), np.float32)
    cols = {"mem_g": columns(a["mem_g"][l]), "mix_pre_g": columns(a["mix_pre_g"][l]),
            "x_pre_g": columns(a["x_pre_g"][l]), "f_pre_g": columns(a["f_pre_g"][l]),
            "cq_g": columns(a["b_cq_g"][l]), "ckv_g": columns(a["b_ckv_g"][l]), "sub_g": columns(a["a_sub_g"][l]),
            "neg_lam_init": np.full((P, 1), -lam_init, np.float32),
            "one_minus_lam_init": np.full((P, 1), 1.0 - lam_init, np.float32),
            "c_w": a["c_w_s"][l].transpose(2, 0, 1).reshape(P, 4 * P)}
    return np.concatenate([cols[n] for n in PC], axis=1)


def layer_rows(a, l):
    parts = {"ln_g": a["c_ln_g"][l], "ln_b": a["c_ln_b"][l], "b_s": a["c_b_s"][l].reshape(-1),
             "lam": a["a_lambda"][l].reshape(-1)}
    return np.concatenate([parts[n] for n in BR])


def second_blocks(a):
    w_in, at, blocks = a["w_in_2"], 0, {}
    for names, width in ((["q0", "q1"], 1024), (["kv"], W), (["ag0", "ag1"], 1024), (["u0", "u1"], 1024),
                         (["z0", "z1"], 1024), ([f"ga{n}" for n in range(4)], D), ([f"gs{n}" for n in range(4)], D)):
        for n, name in enumerate(names):
            blocks[name] = w_in[:, at + n * W:at + (n + 1) * W]
        at += width
    for n in range(4):
        cols = slice(n * W, (n + 1) * W)
        blocks[f"ap{n}"], blocks[f"sp{n}"] = a["w_attn_proj_2"][:, cols], a["w_ssm_proj_2"][:, cols]
        blocks[f"out{n}"] = a["w_out_2"][:, cols]
        blocks[f"glu{'a' if n < 2 else 'b'}{n % 2}"] = a["w_glu_2"][:, cols]
    return blocks


def second_params(a):
    state = lambda v: np.asarray(v).reshape(32, P).T
    cols = {"norm_w": columns(a["norm_w_2"]), "q_w": np.tile(a["q_norm_w_2"], 2)[:, None],
            "k_w": np.tile(a["k_norm_w_2"], 2)[:, None], "b_glu": columns(a["b_glu_2"]),
            "skip": columns(a["D_skip_2"]), "A_re": state(a["A_re_2"]), "A_im": state(a["A_im_2"]),
            "log_dt": state(np.repeat(a["log_dt_2"], 64))}
    return np.concatenate([cols[n] for n in SC], axis=1)


def input_maps(a):
    out = np.zeros((NCT, P, 2, 4, P), np.float32)
    for m, b in enumerate((a["B_re_2"], a["B_im_2"])):
        for g in range(64):
            c, q = g // 8, g % 8
            out[c, 16 * q:16 * q + 16, m, q // 2, 64 * (q % 2):64 * (q % 2) + 64] = b[g].T
    return out.reshape(NCT * P, -1)


def output_maps(a):
    out = np.zeros((NCT, P, 2, 4, 32), np.float32)
    for m, w in enumerate((a["C_re_2"], a["C_im_2"])):
        for g in range(64):
            c, q = g // 8, g % 8
            out[c, 64 * (q % 2):64 * (q % 2) + 64, m, q // 2, 16 * (q % 2):16 * (q % 2) + 16] = w[g].T
    return out.reshape(NCT * P, -1)


def kernel(**inputs):
    from concourse import bacc
    from concourse.bass_utils import run_bass_kernel_spmd

    a = {n: np.asarray(v) for n, v in inputs.items()}
    stream = []
    for l in range(L):
        blocks = layer_blocks(a, l)
        stream += [units_of(blocks[name], g) for name, g in LG.items()]
    second = second_blocks(a)
    stream += [units_of(second[name], g) for name, g in SG.items() if g.units]
    arrays = {
        "stream": np.concatenate(stream).reshape(-1, WSLOT),
        "x": a["x"][0],
        "mem": a["mem"][0],
        "params": np.concatenate([layer_params(a, l) for l in range(L)]),
        "rows": np.stack([layer_rows(a, l) for l in range(L)]),
        "post_g": np.stack([a[n][l] for l in range(L) for n in ("mix_post_g", "x_post_g", "f_post_g")]),
        "sparams": second_params(a),
        "sinks": a["sinks_2"][None, :],
        "onehot": bucket_rows(),
        "rel": a["rel_bias"],
        "b_pad": input_maps(a),
        "c_pack": output_maps(a),
    }
    arrays = {f"in_{n}": np.ascontiguousarray(v) for n, v in arrays.items()}
    nc = bacc.Bacc("TRN2", target_bir_lowering=False, num_devices=1)
    ins = [nc.dram_tensor(n, v.shape, F32, kind="ExternalInput").ap() for n, v in arrays.items()]
    out = nc.dram_tensor("out", (T, D), F32, kind="ExternalOutput").ap()
    toep_scratch = nc.dram_tensor("toep_scratch", (P * 12 * TOEP,), F32, kind="Internal").ap()
    build(nc, *ins, out, toep_scratch)
    result = run_bass_kernel_spmd(nc, [arrays], core_ids=[0])
    return result.results[0]["out"].reshape(1, T, D)
```

```python
import math
from contextlib import ExitStack

import concourse.bass as bass
import numpy as np
from concourse import mybir

F32 = mybir.dt.float32
F32R = mybir.dt.float32r
ALU = mybir.AluOpType
ACT = mybir.ActivationFunctionType
AX = mybir.AxisListType

P = 128
D = 2048
KD = D // P
T = 256
NT = T // P
L = 2
HA, HB, HX = 6, 6, 4
NIDX = 16
TOPK = 64
FF = 5632
EPS = 1e-6
NEG = -1e30
FILL, TAKEN = -3.0e38, -3.3e38

KU = 2
W = 512
SLOTS = 4
WSLOT = KU * W


class Group:

    def __init__(self, name, kchunks, width, form, unit, index):
        self.name, self.kchunks, self.width, self.form = name, kchunks, width, form
        self.unit, self.index = unit, index
        self.units = kchunks // KU
        self.parity, self.turn = index % 2, index // 2
        self.end = unit + self.units
        self.blocks = width // P


def plan(specs):
    groups, unit = {}, 0
    for n, (name, kchunks, width, form) in enumerate(specs):
        groups[name] = Group(name, kchunks, width, form, unit, n)
        unit += kchunks // KU
    assert unit % SLOTS == 0 and len(specs) % 2 == 0
    return groups, unit


NJ = FF // W
START = [(f"mem_{a}{l}", KD, W, form) for l in range(L) for a, form in (("k", "C"), ("v", "T"))]
MG, MU = plan(START)
LAYER = [("cq", KD, W, "T"), ("ckv", KD, 336, "T"), ("qk0", KD, W, "C"), ("qi0", 4, W, "C"), ("qi1", 4, W, "C"),
         ("qk1", KD, W, "C"), ("uq0", 4, W, "C"), ("uq1", 4, 256, "C"), ("uk0", 2, W, "C"), ("uk1", 2, 256, "C"),
         ("uv0", 2, W, "T"), ("uv1", 2, 256, "T"), ("qk2", KD, W, "C"), ("va0", KD, W, "T"), ("va1", KD, 256, "T"),
         ("cv", KD, W, "T"), ("cu", KD, W, "C")]
MIXING = [name for name, *_ in LAYER]
LAYER += [(f"wo{n}", KD, W, "T") for n in range(4)]
LAYER += [("xq", KD, W, "C")] + [(f"xo{n}", 4, W, "T") for n in range(4)]
LAYER += [("gate0", KD, W, "T"), ("up0", KD, W, "T")]
for _j in range(1, NJ):
    LAYER += [(f"gate{_j}", KD, W, "T"), (f"up{_j}", KD, W, "T")]
    LAYER += [(f"down{_j - 1}_{n}", 4, W, "T") for n in range(4)]
LAYER += [(f"down{NJ - 1}_{n}", 4, W, "T") for n in range(4)]
LG, LU = plan(LAYER)
LN = len(LAYER)

SECOND = [("q0", KD, W, "T"), ("q1", KD, W, "T"), ("kv", KD, W, "T"), ("u0", KD, W, "C"), ("u1", KD, W, "C")]
SECOND += [("ag0", KD, W, "C"), ("ag1", KD, W, "C")]
for _n in range(4):
    SECOND += [(f"ga{_n}", KD, W, "C"), (f"ap{_n}", 8, W, "C")]
SECOND += [("z0", KD, W, "C"), ("z1", KD, W, "C")]
for _n in range(2):
    SECOND += [(f"glub{_n}", 8, W, "C"), (f"glua{_n}", 8, W, "C")]
for _n in range(4):
    SECOND += [(f"gs{_n}", KD, W, "C"), (f"sp{_n}", 8, W, "C")]
SECOND += [(f"out{n}", KD, W, "T") for n in range(4)]
SECOND += [("end", 0, W, "T")] if len(SECOND) % 2 else []
SG, SU = plan(SECOND)

PAIRS = [(i, hp) for i in range(NT) for hp in range(3)]


def turns_of_attention(tag, steps):
    out = [f"{tag}L0"]
    for k in range(steps):
        out += ([f"{tag}L{k + 1}"] if k + 1 < steps else []) + [f"{tag}T{k}", f"{tag}V{k}"]
    return out


def numbered(names):
    assert len(names) % 2 == 0, len(names)
    return {n: i for i, n in enumerate(names)}




def woven(groups, steps):
    units = [("unit", g, n) for g in groups for n in range(g.units)]
    out, left = [], sorted(steps, key=lambda s: s[0])
    for n in range(len(units) + 1):
        while left and left[0][0] <= n:
            out.append(left.pop(0)[1:])
        out += units[n:n + 1]
    assert not left
    return out


def mixing_steps():
    ends, at = {}, 0
    for name in MIXING:
        at += LG[name].units
        ends[name] = at
    steps = [(ends[name] + (name not in ("ckv", "cu")), "out", name) for name in MIXING]
    steps += [(ends["ckv"], "latents"), (ends["ckv"] + 3, "bq"), (ends["ckv"] + 3, "bkv")]
    at = ends["qi1"] + 2
    steps += [(at + 0.75 * n, "ix", n // 4, n % 4) for n in range(8)]
    steps += [(at + 7 + n, "top", i, first, last) for n, (i, first, last)
              in enumerate(((0, 0, 4), (0, 4, 8), (1, 0, 3), (1, 3, 6), (1, 6, 8)))]
    for tag, at, pitch, late in (("b", ends["uv1"] + 2, 3, (1, 2, 3, 4)), ("a", ends["va1"] - 3, 2, (1, 2, 3, 4))):
        spaced = [(at + pitch * k + d, n, tag + what, k) for k in range(6)
                  for n, (what, d) in enumerate(zip("LECTV", (0,) + late))]
        steps += [(p, name, k) for p, _, name, k in sorted(spaced, key=lambda e: (e[0], e[3], e[1]))]
    steps += [(ends["cv"] + 1, "v_stats"), (ends["cv"] + 2, "v_rows"), (ends["cv"] + 3, "c"),
              (ends["va1"] + 12, "oa_norm"), (ends["va1"] + 14, "oa_across"),
              (ends["cu"] - 1, "mix", 0), (ends["cu"] - 1, "mix", 1), (ends["cu"], "mix", 2), (ends["cu"], "mix", 3)]
    return woven([LG[name] for name in MIXING], steps)


MIX = mixing_steps()


def turns_of(step, *at):
    if step in ("aL", "aT", "aV", "bL", "bT", "bV"):
        return [f"{step}{at[0]}"]
    if step in ("wL", "wT", "wV"):
        return [f"{step}{at[0]}"]
    if step == "ix":
        return [f"ix{at[0]}_{at[1]}"]
    if step == "inputs":
        return [f"s{at[0]}_re", f"s{at[0]}_im"]
    if step == "outputs":
        return [f"s{at[0]}_y"]
    if step == "head_turns":
        return ["tq0", "tq1", "tk"]
    return {"bq": ["bq"], "bkv": ["bkv"], "c": ["c"], "oa_across": ["an0", "an1"]}.get(step, [])


MTP = numbered([f"mem{q}" for q in range(4)])
LTURNS = [f"pre{q}" for q in range(4)] + [name for step in MIX for name in turns_of(*step)]
LTURNS += [f"xpre{q}" for q in range(4)] + turns_of_attention("x", 2)
LTURNS += [f"fpre{q}" for q in range(4)] + [f"h{j}" for j in range(NJ)]
LTP = numbered(LTURNS)
NTP = len(LTP)
NCT = 8



def second_steps():
    steps = [(1, "head_rows"), (5, "head_turns")]
    for k in range(8):
        at = 6 + 2 * k
        steps += [(at, "wL", k), (at + 1, "wE", k), (at + 1, "w_weights", k), (at + 2, "wT", k), (at + 3, "wV", k)]
    names = ["u0", "u1", "ag0", "ag1"] + [f"{a}{n}" for n in range(4) for a in ("ga", "ap")] + ["z0", "z1"]
    at, ends = 0, {}
    for name in names:
        at += SG[name].units
        ends[name] = at
    steps = [(ends[name] + (3 if name == "ag0" else 1), "out", name) for name in names[:-1]] + \
        sorted(steps, key=lambda step: (step[0], step[-1] if len(step) == 3 else -1))
    steps += [(23, "whole", 0), (23, "angles", 0), (24, "turns", 0), (25, "whole", 1)]
    for c in range(NCT):
        at = 25 + 8.2 * c
        steps += [(at, "inputs", c), (at + 1, "back", c), (at + 2, "maps", c)]
        if c + 1 < NCT:
            steps += [(at + 5.2, "angles", c + 1)]
        steps += [(at + 2.8, "scan", c), (at + 4, "forward", c), (at + 5, "join", c),
                  (at + 7.2, "outputs", c), (at + 7.9, "skip", c)]
        if c + 1 < NCT:
            steps += [(at + 7, "turns", c + 1)]
        if c + 2 < NCT:
            steps += [(at + 8.5, "whole", c + 2)]
    steps += [(ends["z1"] - 11, "ys", 0), (ends["z1"] - 4, "ys", 1)]
    return woven([SG[name] for name in names], steps) + [("out", names[-1])]


SMIX = second_steps()
STURNS = [f"norm{q}" for q in range(4)] + [name for step in SMIX for name in turns_of(*step)]
STP = numbered(STURNS + ([] if len(STURNS) % 2 == 0 else ["end"]))

HIS = {n: i for i, n in enumerate([f"pre{q}" for q in range(4)] + ["bq", "bkv"]
                                  + [f"xpre{q}" for q in range(4)] + ["xV0", "xV1"]
                                  + [f"fpre{q}" for q in range(4)] + [f"h{j}" for j in range(NJ)])}
COUNTS = {"unit": (LU, 48, MU), "acc": (LN // 2, 6, len(START) // 2), "turn": (NTP, 2, 4), "turn2": (NTP // 2, 1, 2),
          "hi": (len(HIS), 2, 4), "gated": (NJ, 2, 0), "raw": (16 * LU // SLOTS, 16 * 48 // SLOTS, 16 * MU // SLOTS),
          "norm": (3 * NT, 0, NT)}


def hold(eng, semaphore, value, passed):
    eng.wait_ge(semaphore, value)
    eng.sem_inc(passed, 1)


class Pos:

    def __init__(self, layer, turn=None):
        self.layer, self.turn = layer, turn

    def n(self, kind, count):
        per, step, before = COUNTS[kind] if isinstance(kind, str) else (kind, 0, 0)
        if self.layer is None:
            return count
        value = self.layer * per + (before + count)
        return value if self.turn is None or not step else self.turn * step + value


PC, _at = {}, 0
for _name, _n in [("mix_pre_g", KD), ("x_pre_g", KD), ("f_pre_g", KD), ("cq_g", 4),
                  ("ckv_g", 2), ("sub_g", 1), ("neg_lam_init", 1), ("one_minus_lam_init", 1), ("c_w", 4 * P)]:
    PC[_name] = slice(_at, _at + _n)
    _at += _n
NPC = _at
BR, _at = {}, 0
for _name, _n in [("ln_g", W), ("ln_b", W), ("b_s", W), ("lam", 256)]:
    BR[_name] = slice(_at, _at + _n)
    _at += _n
NBR = _at
SC, _at = {}, 0
for _name, _n in [("norm_w", KD), ("mem_g", L * KD), ("q_w", 1), ("k_w", 1), ("b_glu", KD), ("skip", NCT),
                  ("A_re", 32), ("A_im", 32), ("log_dt", 32)]:
    SC[_name] = slice(_at, _at + _n)
    _at += _n
NSC = _at
TOEP = 384
NQ = 16


def build(nc, stream, x, mem, params, rows, post_g, sparams, sinks, onehot, rel, b_pad, c_pack, out,
          toep_scratch, mem_scratch):
    ctx = ExitStack()
    with ctx:
        place = [nc.sbuf_base + (-nc.sbuf_base) % 64]
        base = place[0]
        ctx.enter_context(nc.sbuf_tensor("arena", [P, (nc.sbuf_usable_end - base) // 4 - 16], F32))

        def at_offset(name, offset, shape, dt=F32):
            return nc.alloc_sbuf_tensor_at(name, shape, dt, offset=offset)

        def sb(name, shape, dt=F32):
            here = place[0]
            place[0] += (int(np.prod(shape[1:])) * 4 + 31) // 32 * 32
            assert place[0] <= nc.sbuf_usable_end - 64, (name, place[0])
            return at_offset(name, here, shape, dt)

        raw = [sb(f"raw{s}", [P, KU, W]) for s in range(SLOTS)]
        hi = [sb(f"hi{s}", [P, KU, W], F32R) for s in range(SLOTS)]
        lo = [sb(f"lo{s}", [P, KU, W], F32R) for s in range(SLOTS)]
        h = sb("h", [P, NT, D])
        x_at = place[0]
        xh = sb("xh", [P, KD, T], F32R)
        xl = sb("xl", [P, KD, T], F32R)
        y_at = place[0]
        y = sb("y", [P, NT, D])
        mixT = at_offset("mixT", y_at, [P, KD, T])
        par = sb("par", [P, NPC])
        row_at = place[0]
        row = sb("row", [P, NBR])
        gpost_at = place[0]
        gpost = sb("gpost", [P, D])
        bias = sb("bias", [P, HA + HB, T])
        ident = sb("ident", [P, P])
        mhalf = sb("mhalf", [P, 40])
        small = sb("small", [P, 384])
        spar = sb("spar", [P, NSC])
        ssm = sb("ssm", [P, 6, 32])
        lg = [at_offset(f"lg{n}", gpost_at + n * 4096, [P, 4, T]) for n in range(2)]
        xz = [at_offset(f"xz{n}", x_at + n * 4096, [P, 4, T]) for n in range(2)]
        xe = [at_offset(f"xe{n}", x_at + 8192 + n * 4096, [P, 4, T]) for n in range(2)]
        oa = at_offset("oa", y_at, [P, NT, HA * P])
        qbT = at_offset("qbT", y_at + HA * T * 4, [P, HB, T])
        iota = sb("iota", [P, T])
        qp_at = place[0]
        QA = sb("QA", [P, HA, T])
        QI = sb("QI", [P, NIDX // 2, T])
        kbT = at_offset("kbT", qp_at + 6144, [P, HB, T])
        r_at = place[0]
        kaT = sb("kaT", [P, HA, T])
        va = sb("va", [P, NT, HA * P])
        vb = sb("vb", [P, NT, HB * P])
        memk_at = place[0]
        cq = sb("cq", [P, NT, W])
        ckv = sb("ckv", [P, NT, 336])
        kk = sb("kk", [P, NT, P])
        memv_at = place[0]
        cv = sb("cv", [P, NT, W])
        kiT = sb("kiT", [P, T])
        sc = sb("sc", [P, NT, T])
        cqh = sb("cqh", [P, 4, T], F32R)
        cql = sb("cql", [P, 4, T], F32R)
        ckh = sb("ckh", [P, 2, T], F32R)
        ckl = sb("ckl", [P, 2, T], F32R)
        kmT = at_offset("kmT", memk_at, [P, HX, T])
        vm = at_offset("vm", memv_at, [P, NT, W])
        junk = at_offset("junk", r_at, [P, D])
        qxT = at_offset("qxT", r_at + 8192, [P, HX, T])
        sg = at_offset("sg", r_at, [P, NT, W])
        hm = [at_offset(f"hm{n}", r_at + 4096 * (1 + n), [P, NT, W]) for n in range(2)]
        hTh = at_offset("hTh", qp_at, [P, 4, T], F32R)
        hTl = at_offset("hTl", qp_at + 4096, [P, 4, T], F32R)
        relb = at_offset("relb", x_at, [32, 12, P])
        relt = at_offset("relt", x_at + 8192, [32, 12])
        oneh = at_offset("oneh", x_at + 10240, [32, TOEP])
        memT = at_offset("memT", qp_at, [P, KD, T])
        memkv = at_offset("memkv", r_at + 8192, [P, L, 2, 4 * T])
        toep = at_offset("toep", r_at + 8192 + 16384, [P, 12, TOEP])
        m_at = row_at
        uT = at_offset("uT", m_at, [P, NCT, T])
        rotc = at_offset("rotc", m_at + 8192, [P, 4, T])
        rots = at_offset("rots", m_at + 12288, [P, 4, T])
        sd = [at_offset(f"sd{n}", m_at + 16384 + 4096 * n, [P, 4, T]) for n in range(2)]
        window = at_offset("window", m_at + 24576, [P, T])
        sink = at_offset("sink", m_at + 25600, [P, NQ])
        QP = at_offset("QP", qp_at, [P, 8, 2, T])
        r_at = qp_at + 16384
        turn_a = at_offset("turn_a", r_at + 20480, [P, 4, T])
        turn_b = at_offset("turn_b", r_at + 41984, [P, 4, T])
        assert r_at + 41984 + 4096 <= nc.sbuf_usable_end - 64
        qt = at_offset("qt", r_at, [P, NT, NQ * 64])
        kv = at_offset("kv", r_at + 8192, [P, NT, W])
        kT = at_offset("kT", r_at + 12288, [P, 4, T])
        vpad = at_offset("vpad", r_at + 16384, [P, NT, 4, 2, P])
        attnT = at_offset("attnT", r_at + 24576, [P, 8, T])
        sg2 = at_offset("sg2", r_at + 32768, [P, 4, T])
        cpad = [at_offset(f"cpad{n}", r_at + 36864 + 2560 * n, [P, 5 * P]) for n in range(2)]
        craw = at_offset("craw", m_at + 26240, [P, 2, 4, 32])
        craw2 = at_offset("craw2", m_at + 25728, [P, 4, 32])
        sw = at_offset("sw", gpost_at, [P, 14, 32])
        angle_hi = at_offset("angle_hi", gpost_at + 2048, [P, 32], F32R)
        kdup = at_offset("kdup", y_at + 8192, [P, NT, 4, 2, 64])
        zg = [at_offset(f"zg{n}", y_at + 4096 * n, [P, 4, T]) for n in range(2)]
        ze = [at_offset(f"ze{n}", y_at + 8192 + 4096 * n, [P, 4, T]) for n in range(2)]
        gath = at_offset("gath", qp_at, [P, 8, T], F32R)
        gatl = at_offset("gatl", qp_at + 8192, [P, 8, T], F32R)
        ysh = at_offset("ysh", qp_at, [P, 8, T], F32R)
        ysl = at_offset("ysl", qp_at + 8192, [P, 8, T], F32R)
        sr = [at_offset(f"sr{n}", r_at + 4096 * n, [P, 4, T]) for n in range(2)]
        st = at_offset("st", r_at + 8192, [P, 4, T])
        bpad = [at_offset(f"bpad{n}", r_at + 12288 + 4096 * n, [P, 2, 4, P]) for n in range(2)]
        zs = at_offset("zs", r_at + 24576, [P, 8, T])
        prh = at_offset("prh", r_at, [P, 8, T], F32R)
        prl = at_offset("prl", r_at + 8192, [P, 8, T], F32R)

        acc = [ctx.enter_context(nc.psum_tensor(f"acc{n}", [P, NT, W], F32)) for n in range(2)]
        tp = [ctx.enter_context(nc.psum_tensor(f"tp{n}", [P, 4, T], F32)) for n in range(2)]
        accC = [a[:, :, :].rearrange("p a (b t) -> p (a b) t", t=T) for a in acc]

        def sem(name):
            return ctx.enter_context(nc.semaphore(name))

        raw_loaded = [sem(f"raw_loaded{s}") for s in range(SLOTS)]
        hi_done = sem("hi_done")
        split_done = sem("split_done")
        unit_used = sem("unit_used")
        acc_read = [sem(f"acc_read{n}") for n in range(2)]
        tp_full = sem("tp_full")
        tp_read = [sem(f"tp_read{n}") for n in range(2)]
        const_ready = sem("const_ready")
        start_loaded = sem("start_loaded")
        rel_spread = sem("rel_spread")
        toep_full = sem("toep_full")
        toep_copied = sem("toep_copied")
        toep_moved = sem("toep_moved")
        bias_ready = sem("bias_ready")
        x_loaded = sem("x_loaded")
        mem_loaded = sem("mem_loaded")
        mem_hi = sem("mem_hi")
        mem_split = sem("mem_split")
        memkv_stored = sem("memkv_stored")
        memkv_loaded = sem("memkv_loaded")
        par_loaded = sem("par_loaded")
        gpost_loaded = sem("gpost_loaded")
        cw_ready = sem("cw_ready")
        lam_ready = sem("lam_ready")
        lam_exp = sem("lam_exp")
        h_rows = sem("h_rows")
        in_squares = sem("in_squares")
        in_roots = sem("in_roots")
        in_rows = sem("in_rows")
        out_squares = sem("out_squares")
        out_sums = sem("out_sums")
        out_roots = sem("out_roots")
        x_hi = sem("x_hi")
        max_ready = sem("max_ready")
        exp_ready = sem("exp_ready")
        weights_ready = sem("weights_ready")
        oa_squares = sem("oa_squares")
        oa_roots = sem("oa_roots")
        oa_rows = sem("oa_rows")
        v_stats = sem("v_stats")
        v_roots = sem("v_roots")
        v_rows = sem("v_rows")
        gated_c = sem("gated_c")
        lat_squares = sem("lat_squares")
        lat_roots = sem("lat_roots")
        lat_rows = sem("lat_rows")
        dots_used = sem("dots_used")
        score_masked = sem("score_masked")
        mix_hi = sem("mix_hi")
        mix_split = sem("mix_split")
        gated = sem("gated")
        out_stored = sem("out_stored")

        par2_loaded = sem("par2_loaded")
        sink_loaded = sem("sink_loaded")
        window_ready = sem("window_ready")
        ssm_ready = sem("ssm_ready")
        ssm_exp = sem("ssm_exp")
        q_squares = sem("q_squares")
        q_roots = sem("q_roots")
        q_rows = sem("q_rows")
        sink_exp = sem("sink_exp")
        ag_mul = sem("ag_mul")
        ag_hi = sem("ag_hi")
        ag_split = sem("ag_split")
        bc_loaded = [sem(f"bc_loaded{n}") for n in range(2)]
        whole = sem("whole")
        backed = sem("backed")
        summed = sem("summed")
        angles = sem("angles")
        scanned = sem("scanned")
        parts_turned = sem("parts_turned")
        maps_loaded = sem("maps_loaded")
        turned = sem("turned")
        states = sem("states")
        skipped = sem("skipped")
        ys_hi = sem("ys_hi")
        ys_split = sem("ys_split")
        glu_mul = sem("glu_mul")
        glu_hi = sem("glu_hi")
        glu_split = sem("glu_split")
        merged_done = sem("merged_done")

        ss, rs = small[:, 0:2], small[:, 2:4]
        pss, prs = small[:, 240:248].rearrange("p (t n) -> p t n", t=NT), small[:, 4:6]
        psum_ = small[:, 6:8]
        mx = [small[:, 8 + 4 * n:12 + 4 * n] for n in range(2)]
        nmx = [small[:, 16 + 4 * n:20 + 4 * n] for n in range(2)]
        sm = [small[:, 24 + 4 * n:28 + 4 * n] for n in range(2)]
        rc = [small[:, 32 + 4 * n:36 + 4 * n] for n in range(2)]
        lamv, lame, nlam, subg = small[:, 40:42], small[:, 42:44], small[:, 44:45], small[:, 45:46]
        oss, ors = small[:, 48:60], small[:, 60:72]
        vst = small[:, 72:84].rearrange("p (t s) -> p t s", s=6)
        vmv = small[:, 84:88].rearrange("p (t s) -> p t s", s=2)
        vrs = small[:, 88:90]
        lss, lrs = small[:, 92:96], small[:, 96:100]
        m8 = small[:, 104:112]
        widx = small[:, 112:144].rearrange("p (t g) -> p t g", g=NIDX)
        qss, qrs = small[:, 144:184], small[:, 184:224]
        snk = [small[:, 224 + 4 * n:228 + 4 * n] for n in range(2)]
        esk = [small[:, 232 + 4 * n:236 + 4 * n] for n in range(2)]
        half_pi, round_ = small[:, 248:249], small[:, 249:250]
        lamp = small[:, 256:384].rearrange("p (a n) -> p a n", n=64)

        def flat(tensor):
            names = " ".join("abcd"[:len(tensor.shape) - 1])
            return tensor[tuple(slice(None) for _ in tensor.shape)].rearrange(f"p {names} -> p ({names})")

        def pcol(name, n=0):
            return par[:, PC[name].start + n:PC[name].start + n + 1]

        def take_turn(pe, pos, turn):
            pe.wait_ge(tp_read[turn % 2], pos.n("turn2", turn // 2 + 1))
            return tp[turn % 2]

        def see_turn(eng, pos, turn):
            eng.wait_ge(tp_full, pos.n("turn", turn + 1))
            return tp[turn % 2]

        def after_turn(eng, pos, turn):
            eng.wait_ge(tp_read[turn % 2], pos.n("turn2", turn // 2 + 2))

        def see_group(eng, pos, g):
            eng.wait_ge(unit_used, pos.n("unit", g.end + SLOTS))
            return (accC if g.form == "C" else acc)[g.parity]

        def after_group(eng, pos, g):
            eng.wait_ge(acc_read[g.parity], pos.n("acc", g.turn + 2))

        passed = sem("passed")

        SCALE_A, SCALE_B = 64 ** -0.5, P ** -0.5
        TWO_PI_HI = 6.28125
        TWO_PI_MID = float(np.float32(2 * math.pi - 6.28125))
        TWO_PI_LO = 2 * math.pi - 6.28125 - TWO_PI_MID
        ROUND = 1.5 * 2.0 ** 23
        PI_IN = 3.1415925
        HALF_IN = 0.49999997

        def reduce_angle(dve, out, angle, turns):
            nc.vector.tensor_scalar(turns, angle, 1.0 / (2 * math.pi), ROUND, ALU.mult, ALU.add)
            dve.drain()
            nc.vector.tensor_scalar(turns, turns, -ROUND, None, ALU.add)
            dve.drain()
            nc.vector.scalar_tensor_tensor(out, turns, -TWO_PI_HI, angle, ALU.mult, ALU.add)
            dve.drain()
            nc.vector.scalar_tensor_tensor(out, turns, -TWO_PI_MID, out, ALU.mult, ALU.add)
            dve.drain()
            nc.vector.scalar_tensor_tensor(out, turns, -TWO_PI_LO, out, ALU.mult, ALU.add)
            dve.drain()
            nc.vector.tensor_scalar(out, out, PI_IN, -PI_IN, ALU.min, ALU.max)
            dve.drain()

        def cos_argument(dve, out, angle, negative):
            nc.vector.tensor_scalar(negative, angle, -1.0, None, ALU.mult)
            dve.drain()
            nc.vector.tensor_tensor(out, angle, negative, ALU.max)
            dve.drain()
            nc.vector.tensor_scalar(out, out, -1.0, math.pi / 2, ALU.mult, ALU.add)

        block = ctx.enter_context(nc.Block())

        @block.sync
        def _(sp):
            sp.dma_start(y[:, :, :], mem.rearrange("(t p) d -> p t d", p=P)).then_inc(mem_loaded, 16)
            with sp.Fori(0, (MU + L * LU + SU) // SLOTS) as i:
                for s in range(SLOTS):
                    sp.wait_ge(split_done, i * SLOTS + (s + 1))
                    sp.dma_start(flat(raw[s]), stream[bass.ds((i * SLOTS + s) * P, P), :]).then_inc(raw_loaded[s], 16)
            for n in range(4):
                after_group(sp, Pos(L), SG[f"out{n}"])
                sp.dma_start(out.rearrange("(t p) d -> p t d", p=P)[:, :, n * W:(n + 1) * W],
                             h[:, :, n * W:(n + 1) * W]).then_inc(out_stored, 16)
            sp.wait_ge(out_stored, 64)

        @block.tensor
        def _(pe):
            def product(pos, g, a_h, a_l, only=None, quad_ready=None):
                a = (accC if g.form == "C" else acc)[g.parity]
                for n in range(g.units) if only is None else (only,):
                    if n == 0:
                        pe.wait_ge(acc_read[g.parity], pos.n("acc", g.turn + 1))
                    if quad_ready is not None and n % 2 == 0:
                        quad_ready(n // 2)
                    s = (g.unit + n) % SLOTS
                    pe.wait_ge(split_done, pos.n("unit", g.unit + n + 1 + SLOTS))
                    for k in range(KU):
                        c = n * KU + k
                        first, final = c == 0, c == g.kchunks - 1
                        if g.form == "T":
                            for t in range(NT):
                                o = a[:, t, 0:g.width]
                                ah, al = a_h[:, c, t * P:(t + 1) * P], a_l[:, c, t * P:(t + 1) * P]
                                nc.tensor.matmul(o, ah, hi[s][:, k, 0:g.width], start=first, stop=False)
                                nc.tensor.matmul(o, ah, lo[s][:, k, 0:g.width], start=False, stop=False)
                                last = nc.tensor.matmul(o, al, hi[s][:, k, 0:g.width], start=False, stop=final)
                        else:
                            for b in range(g.blocks):
                                o = a[:, b, :]
                                wh, wl = hi[s][:, k, b * P:(b + 1) * P], lo[s][:, k, b * P:(b + 1) * P]
                                nc.tensor.matmul(o, wh, a_h[:, c, :], start=first and b % 2 == 0, stop=False,
                                                 skip_group_check=True)
                                nc.tensor.matmul(o, wh, a_l[:, c, :], start=False, stop=False, skip_group_check=True)
                                last = nc.tensor.matmul(o, wl, a_h[:, c, :], start=False, stop=final,
                                                        skip_group_check=True)
                    last.then_inc(unit_used, 1)

            def transposes(pos, turn, blocks, begins=True, ends=True):
                o = take_turn(pe, pos, turn) if begins else tp[turn % 2]
                for c, t, src in blocks:
                    last = nc.tensor.transpose(o[:, c, t * P:(t + 1) * P], src, ident[:, :])
                if ends:
                    last.then_inc(tp_full, 1)

            def norm(pos, k, tag, turns):
                def part(q, ts):
                    return [(c, t, y[:, t, (4 * q + c) * P:(4 * q + c + 1) * P]) for t in ts for c in range(4)]

                pe.wait_ge(in_rows, pos.n("norm", NT * k + 1))
                for q in (0, 1):
                    transposes(pos, turns[f"{tag}{q}"], part(q, (0,)), ends=False)
                pe.wait_ge(in_rows, pos.n("norm", NT * k + NT))
                for q in (0, 1):
                    transposes(pos, turns[f"{tag}{q}"], part(q, (1,)), begins=False)

                def quad_ready(q):
                    after_turn(pe, pos, turns[f"{tag}{q}"])
                    if q < 2:
                        transposes(pos, turns[f"{tag}{q + 2}"], part(q + 2, range(NT)))

                return quad_ready

            pe.wait_ge(rel_spread, 1)
            for hd in range(HA + HB):
                if hd >= 4:
                    pe.wait_ge(toep_copied, hd - 3)
                bank = (flat(acc[hd % 4]) if hd % 4 < 2 else flat(tp[hd % 4 - 2]))[:, 0:TOEP]
                nc.tensor.matmul(bank, relb[:, hd, :], oneh[:, :], start=True, stop=True).then_inc(toep_full, 1)
            pe.wait_ge(toep_copied, HA + HB)
            pe.wait_ge(const_ready, 1)
            pe.sem_inc(unit_used, SLOTS)

            pos = Pos(None)
            ready = norm(pos, 0, "mem", MTP)
            product(pos, MG["mem_k0"], xh, xl, quad_ready=ready)
            product(pos, MG["mem_v0"], xh, xl)
            product(pos, MG["mem_k1"], xh, xl, quad_ready=lambda q: pe.wait_ge(mem_split, q + 1))
            product(pos, MG["mem_v1"], xh, xl)

            with pe.Fori(0, L) as layer:
                pos = Pos(layer)
                ready = norm(pos, 0, "pre", LTP)
                for step, *at in MIX:
                    if step == "unit":
                        g, n = at
                        if g is LG["qi0"] and n == 0:
                            after_turn(pe, pos, LTP["bq"])
                            after_turn(pe, pos, LTP["bkv"])
                        if g.kchunks == KD:
                            product(pos, g, xh, xl, only=n, quad_ready=ready if g is LG["cq"] else None)
                        elif g.kchunks == 4:
                            product(pos, g, cqh, cql, only=n)
                        else:
                            product(pos, g, ckh, ckl, only=n)
                    elif step == "bq":
                        pe.wait_ge(lat_rows, pos.n(1, 1))
                        transposes(pos, LTP["bq"], [(c, t, cq[:, t, c * P:(c + 1) * P])
                                                    for c in range(4) for t in range(NT)])
                    elif step == "bkv":
                        transposes(pos, LTP["bkv"], [(c, t, ckv[:, t, c * P:(c + 1) * P] if c < 2 else kk[:, t, :])
                                                     for c in range(3) for t in range(NT)])
                    elif step == "ix":
                        i, b = at
                        if i == 0 and b == 0:
                            after_group(pe, pos, LG["qi0"])
                            after_group(pe, pos, LG["qi1"])
                        o = take_turn(pe, pos, LTP[f"ix{i}_{b}"])
                        for hh in range(4):
                            g, half = 4 * b + hh, slice(64 * (hh % 2), 64 * (hh % 2) + 64)
                            last = nc.tensor.matmul(o[:, 2 * (hh % 2) + hh // 2, 0:P * (i + 1)],
                                                    QI[half, g // 2, i * P:(i + 1) * P], kiT[half, 0:P * (i + 1)],
                                                    start=True, stop=True)
                        last.then_inc(tp_full, 1)
                    elif step == "bL":
                        k = at[0]
                        i, hp = PAIRS[k]
                        if k == 0:
                            for name in ("uv0", "uv1"):
                                after_group(pe, pos, LG[name])
                        o = take_turn(pe, pos, LTP[f"bL{k}"])
                        for hh in range(2):
                            hd = 2 * hp + hh
                            last = nc.tensor.matmul(o[:, hh, 0:P * (i + 1)], qbT[:, hd, i * P:(i + 1) * P],
                                                    kbT[:, hd, 0:P * (i + 1)], start=True, stop=True)
                        last.then_inc(tp_full, 1)
                    elif step == "aL":
                        k = at[0]
                        i, hp = PAIRS[k]
                        if k == 0:
                            after_group(pe, pos, LG["qk2"])
                        o = take_turn(pe, pos, LTP[f"aL{k}"])
                        for hh in range(2):
                            for m in range(2):
                                half = slice(64 * m, 64 * m + 64)
                                last = nc.tensor.matmul(o[:, 2 * m + hh, 0:P * (i + 1)],
                                                        QA[half, 2 * hp + hh, i * P:(i + 1) * P],
                                                        kaT[half, 2 * hp + hh, 0:P * (i + 1)], start=True, stop=True)
                        last.then_inc(tp_full, 1)
                    elif step in ("aT", "bT"):
                        k = at[0]
                        pe.wait_ge(weights_ready, pos.n(14, 6 * (step == "aT") + k + 1))
                        transposes(pos, LTP[f"{step}{k}"], [(hh, b, lg[k % 2][:, hh, b * P:(b + 1) * P])
                                                            for hh in range(2) for b in range(PAIRS[k][0] + 1)])
                    elif step == "bV":
                        k = at[0]
                        i, hp = PAIRS[k]
                        after_turn(pe, pos, LTP[f"bT{k}"])
                        o = take_turn(pe, pos, LTP[f"bV{k}"])
                        for hh in range(2):
                            hd = 2 * hp + hh
                            for b in range(i + 1):
                                last = nc.tensor.matmul(o[:, 0, hh * P:(hh + 1) * P], vb[:, b, hd * P:(hd + 1) * P],
                                                        lg[k % 2][:, 2 + hh, b * P:(b + 1) * P],
                                                        start=b == 0, stop=b == i)
                        last.then_inc(tp_full, 1)
                    elif step == "aV":
                        k = at[0]
                        i, hp = PAIRS[k]
                        if k == 0:
                            after_group(pe, pos, LG["va0"])
                            after_group(pe, pos, LG["va1"])
                        after_turn(pe, pos, LTP[f"aT{k}"])
                        o = take_turn(pe, pos, LTP[f"aV{k}"])
                        for hh in range(2):
                            hd = 2 * hp + hh
                            for b in range(i + 1):
                                last = nc.tensor.matmul(o[:, 0, hh * P:(hh + 1) * P],
                                                        lg[k % 2][:, 2 + hh, b * P:(b + 1) * P],
                                                        va[:, b, hd * P:(hd + 1) * P], start=b == 0, stop=b == i)
                        last.then_inc(tp_full, 1)
                    elif step == "oa_across":
                        pe.wait_ge(oa_rows, pos.n(1, 1))
                        transposes(pos, LTP["an0"], [(c, t, oa[:, t, c * P:(c + 1) * P])
                                                     for c in range(4) for t in range(NT)])
                        transposes(pos, LTP["an1"], [(c, t, oa[:, t, (4 + c) * P:(5 + c) * P])
                                                     for c in range(2) for t in range(NT)])
                    elif step == "c":
                        pe.wait_ge(v_rows, pos.n(1, 1))
                        pe.wait_ge(cw_ready, pos.n(1, 1))
                        o = take_turn(pe, pos, LTP["c"])
                        for t in range(NT):
                            for g in range(4):
                                w = PC["c_w"].start + g * P
                                last = nc.tensor.matmul(o[:, g, t * P:(t + 1) * P], cv[:, t, g * P:(g + 1) * P],
                                                        par[:, w:w + P], start=True, stop=True)
                        last.then_inc(tp_full, 1)

                for n in range(4):
                    product(pos, LG[f"wo{n}"], xh, xl,
                            quad_ready=None if n else lambda q: pe.wait_ge(mix_split, pos.n(4, q + 1)))

                ready = norm(pos, 1, "xpre", LTP)
                product(pos, LG["xq"], xh, xl, quad_ready=ready)
                after_group(pe, pos, LG["xq"])
                pe.wait_ge(memkv_loaded, pos.n(32, 32))
                for i in range(NT):
                    o = take_turn(pe, pos, LTP[f"xL{i}"])
                    for hd in range(HX):
                        last = nc.tensor.matmul(o[:, hd, :], qxT[:, hd, i * P:(i + 1) * P], kmT[:, hd, :],
                                                start=True, stop=True)
                    last.then_inc(tp_full, 1)
                for i in range(NT):
                    pe.wait_ge(weights_ready, pos.n(14, 12 + i + 1))
                    transposes(pos, LTP[f"xT{i}"], [(hd, b, xe[i][:, hd, b * P:(b + 1) * P])
                                                    for hd in range(HX) for b in range(NT)])
                    after_turn(pe, pos, LTP[f"xT{i}"])
                    o = take_turn(pe, pos, LTP[f"xV{i}"])
                    for hd in range(HX):
                        for b in range(NT):
                            last = nc.tensor.matmul(o[:, hd, 0:P], vm[:, b, hd * P:(hd + 1) * P],
                                                    xz[i][:, hd, b * P:(b + 1) * P], start=b == 0, stop=b == 1)
                    last.then_inc(tp_full, 1)
                for i in range(NT):
                    after_turn(pe, pos, LTP[f"xV{i}"])
                for n in range(4):
                    product(pos, LG[f"xo{n}"], cqh, cql)

                ready = norm(pos, 2, "fpre", LTP)

                def across(pos, j):
                    pe.wait_ge(gated, pos.n("gated", j + 1))
                    transposes(pos, LTP[f"h{j}"], [(c, t, hm[j % 2][:, t, c * P:(c + 1) * P])
                                                   for c in range(4) for t in range(NT)])

                def down(pos, j):
                    after_turn(pe, pos, LTP[f"h{j}"])
                    for n in range(4):
                        product(pos, LG[f"down{j}_{n}"], hTh, hTl)

                product(pos, LG["gate0"], xh, xl, quad_ready=ready)
                product(pos, LG["up0"], xh, xl)
                with pe.Fori(0, (NJ - 1) // 2) as turn:
                    here = Pos(layer, turn)
                    for j in (1, 2):
                        product(here, LG[f"gate{j}"], xh, xl)
                        across(here, j - 1)
                        product(here, LG[f"up{j}"], xh, xl)
                        down(here, j - 1)
                across(pos, NJ - 1)
                down(pos, NJ - 1)

            pos = Pos(L)
            ready = norm(pos, 0, "norm", STP)
            product(pos, SG["q0"], xh, xl, quad_ready=ready)
            product(pos, SG["q1"], xh, xl)
            product(pos, SG["kv"], xh, xl)
            for step, *at in SMIX:
                if step == "unit":
                    g, n = at
                    if g is SG["ap0"] and n == 0:
                        pe.wait_ge(ag_split, 2)
                    if g.kchunks == KD:
                        product(pos, g, xh, xl, only=n)
                    else:
                        product(pos, g, gath, gatl, only=n)
                elif step == "head_turns":
                    pe.wait_ge(q_rows, 1)
                    for n in range(2):
                        transposes(pos, STP[f"tq{n}"], [(c, t, qt[:, t, (4 * n + c) * P:(4 * n + c + 1) * P])
                                                        for c in range(4) for t in range(NT)])
                    transposes(pos, STP["tk"], [(g, t, kdup[:, t, g, :, :].rearrange("p a b -> p (a b)"))
                                                for g in range(4) for t in range(NT)])
                elif step == "wL":
                    k = at[0]
                    i, g = k // 4, k % 4
                    if k == 0:
                        for name in ("tq0", "tq1", "tk"):
                            after_turn(pe, pos, STP[name])
                    o = take_turn(pe, pos, STP[f"wL{k}"])
                    for r in range(4):
                        hd = 4 * g + r
                        last = nc.tensor.matmul(o[:, r, 0:P * (i + 1)], QP[:, hd // 2, hd % 2, i * P:(i + 1) * P],
                                                kT[:, g, 0:P * (i + 1)], start=True, stop=True)
                    last.then_inc(tp_full, 1)
                elif step == "wT":
                    k = at[0]
                    pe.wait_ge(weights_ready, pos.n(14, k + 1))
                    transposes(pos, STP[f"wT{k}"], [(r, b, ze[k % 2][:, r, b * P:(b + 1) * P])
                                                    for r in range(4) for b in range(k // 4 + 1)])
                elif step == "wV":
                    k = at[0]
                    i, g = k // 4, k % 4
                    after_turn(pe, pos, STP[f"wT{k}"])
                    o = take_turn(pe, pos, STP[f"wV{k}"])
                    for n in range(2):
                        for r in range(2):
                            for b in range(i + 1):
                                last = nc.tensor.matmul(o[:, n, 0:P], vpad[:, b, g, r, :],
                                                        zg[k % 2][:, 2 * n + r, b * P:(b + 1) * P],
                                                        start=r == 0 and b == 0, stop=r == 1 and b == i)
                    last.then_inc(tp_full, 1)
                elif step == "inputs":
                    c = at[0]
                    pe.wait_ge(bc_loaded[c % 2], 16 * (c // 2 + 1))
                    if c == 0:
                        after_group(pe, pos, SG["u1"])
                    for m, part in enumerate(("re", "im")):
                        o = take_turn(pe, pos, STP[f"s{c}_{part}"])
                        for j in range(4):
                            last = nc.tensor.matmul(o[:, j, :], bpad[c % 2][:, m, j, :], uT[:, c, :],
                                                    start=True, stop=True)
                        last.then_inc(tp_full, 1)
                elif step == "outputs":
                    c = at[0]
                    pe.wait_ge(states, c + 1)
                    o = take_turn(pe, pos, STP[f"s{c}_y"])
                    for j in range(4):
                        for m in range(2):
                            last = nc.tensor.matmul(o[:, 0, :], cpad[m][:, j * P:(j + 1) * P], sd[m][:, j, :],
                                                    start=j == 0 and m == 0, stop=j == 3 and m == 1)
                    last.then_inc(tp_full, 1)
            for n in range(2):
                product(pos, SG[f"glub{n}"], ysh, ysl,
                        quad_ready=None if n else lambda q: pe.wait_ge(ys_split, q + 1))
                product(pos, SG[f"glua{n}"], ysh, ysl)
            for n in range(4):
                product(pos, SG[f"gs{n}"], xh, xl)
                if n == 0:
                    pe.wait_ge(glu_split, 2)
                product(pos, SG[f"sp{n}"], prh, prl)
            for n in range(4):
                product(pos, SG[f"out{n}"], xh, xl,
                        quad_ready=None if n else lambda q: pe.wait_ge(mix_split, pos.n(4, q + 1)))

        class Splitter:
            LEAD = SLOTS - 1

            def __init__(self, split):
                self.split, self.next = split, 0

            def ahead(self, pos, g, limit=LU + SLOTS):
                while self.next < min(g.end + self.LEAD, limit):
                    self.split(pos, self.next)
                    self.next += 1

            def before(self, pos, g, n, limit):
                while self.next < min(g.unit + n + 1 + self.LEAD, limit):
                    self.split(pos, self.next)
                    self.next += 1

            def new_layer(self):
                self.next -= LU

        @block.scalar
        def _(act):
            def split(pos, u):
                s = u % SLOTS
                act.wait_ge(raw_loaded[s], pos.n("raw", 16 * (u // SLOTS + 1)))
                act.wait_ge(unit_used, pos.n("unit", u + 1))
                nc.scalar.activation(hi[s][:, :, :], raw[s][:, :, :], ACT.Copy).then_inc(hi_done, 1)

            units = Splitter(split)

            def copy_group(pos, g, out, func=ACT.Copy):
                units.ahead(pos, g)
                a = see_group(act, pos, g)
                a = a[:, 0:g.blocks, :] if g.form == "C" else a[:, :, 0:g.width]
                nc.scalar.activation(out, a, func).then_inc(acc_read[g.parity], 1)

            def squares_in(pos, src, branch=None):
                for t in range(NT):
                    act.drain()
                    if branch is not None:
                        hold(act, h_rows, pos.n(6, 2 * branch + t + 1), passed)
                    nc.scalar.activation(junk[:, :], src[:, t, :], ACT.Square,
                                         accum_out=ss[:, t:t + 1]).then_inc(in_squares, 1)

            def across_high(pos, tag, turns, gain, g):
                for q in range(4):
                    if q >= 2:
                        units.before(pos, g, 2 * q - 4, g.end)
                    o = see_turn(act, pos, turns[f"{tag}{q}"])
                    for c in range(4):
                        last = nc.scalar.activation(xh[:, 4 * q + c, :], o[:, c, :], ACT.Copy, scale=gain(4 * q + c))
                    last.then_inc(x_hi, 1)

            def norm(pos, k, tag, turns, gain, src, g):
                squares_in(pos, src, k)
                across_high(pos, tag, turns, gain, g)

            def squares_out(pos, branch, groups):
                for n, g in enumerate(groups):
                    units.ahead(pos, g, g.end + 1 if n == 3 else LU + SLOTS)
                    hold(act, acc_read[g.parity], pos.n("acc", g.turn + 2), passed)
                    for t in range(NT):
                        act.drain()
                        last = nc.scalar.activation(junk[:, 0:W], y[:, t, n * W:(n + 1) * W], ACT.Square,
                                                    accum_out=pss[:, t, n:n + 1])
                    last.then_inc(out_squares, 1)
                units.ahead(pos, groups[3])

            def exps(pos, n, k, heads):
                S = P * (PAIRS[k][0] + 1)
                act.wait_ge(max_ready, n)
                for c in range(heads):
                    z = lg[k % 2][:, c, 0:S]
                    last = nc.scalar.activation(z, z, ACT.Exp, bias=nmx[k % 2][:, c:c + 1],
                                                accum_out=sm[k % 2][:, c:c + 1])
                last.then_inc(exp_ready, 1)

            act.dma_start(relt[:, :], rel).then_inc(start_loaded, 16)
            act.dma_start(oneh[:, :], onehot).then_inc(start_loaded, 16)
            act.dma_start(spar[:, :], sparams).then_inc(par2_loaded, 16)
            hold(act, mem_loaded, 16, passed)
            squares_in(Pos(None), y)
            for hd in range(HA + HB):
                act.wait_ge(toep_full, hd + 1)
                bank = (flat(acc[hd % 4]) if hd % 4 < 2 else flat(tp[hd % 4 - 2]))[:, 0:TOEP]
                nc.scalar.activation(toep[:, hd, :], bank, ACT.Copy).then_inc(toep_copied, 1)
            act.wait_ge(toep_copied, HA + HB)
            act.dma_start(toep_scratch.rearrange("(p w) -> p w", p=P), flat(toep)).then_inc(toep_moved, 16)
            act.dma_start(h[:, :, :], x.rearrange("(t p) d -> p t d", p=P)).then_inc(x_loaded, 16)
            pos = Pos(None)
            act.wait_ge(const_ready, 1)
            act.wait_ge(par2_loaded, 16)
            units.ahead(pos, Group("", 0, 0, "T", 0, 0), MU)
            mem_g = lambda l, c: spar[:, SC["mem_g"].start + l * KD + c:SC["mem_g"].start + l * KD + c + 1]
            across_high(pos, "mem", MTP, lambda c: mem_g(0, c), MG["mem_k0"])
            act.wait_ge(toep_moved, 16)
            pitch = 12 * TOEP - 1
            shifted = toep_scratch[P - 1:P - 1 + P * pitch].rearrange("(p w) -> p w", w=pitch)
            act.dma_start(bias[:, 0:11, :], shifted[:, 0:11 * TOEP].rearrange("p (h s) -> p h s", s=TOEP)[:, :, 0:T])\
               .then_inc(toep_moved, 16)
            act.dma_start(bias[:, 11, :], shifted[:, 11 * TOEP:11 * TOEP + T]).then_inc(toep_moved, 16)
            nc.scalar.activation(sw[:, 0, :], spar[:, SC["log_dt"]], ACT.Exp).then_inc(ssm_exp, 1)
            act.wait_ge(ssm_ready, 1)
            nc.scalar.activation(ssm[:, 0, :], sw[:, 1, :], ACT.Exp)
            nc.scalar.activation(sw[:, 5, :], sw[:, 3, :], ACT.Sin)
            nc.scalar.activation(sw[:, 6, :], sw[:, 4, :], ACT.Sin).then_inc(ssm_exp, 1)

            def mem_out(l, n):
                g = MG[f"mem_{'kv'[n]}{l}"]
                units.ahead(pos, g, MU + SLOTS)
                a = see_group(act, pos, g)
                nc.scalar.activation(memkv[:, l, n, :], a[:, :, :].rearrange("p a b -> p (a b)"), ACT.Copy)\
                  .then_inc(acc_read[g.parity], 1)

            mem_out(0, 0)
            for q in range(4):
                g = MG["mem_v0"]
                units.before(pos, g, 2 * q + 1, MU)
                act.wait_ge(unit_used, g.unit + 2 * q + 2 + SLOTS)
                for c in range(4 * q, 4 * q + 4):
                    last = nc.scalar.activation(xh[:, c, :], memT[:, c, :], ACT.Copy, scale=mem_g(1, c))
                last.then_inc(mem_hi, 1)
            for l, n in ((0, 1), (1, 0), (1, 1)):
                mem_out(l, n)
            for name in ("mem_k1", "mem_v1"):
                after_group(act, pos, MG[name])
            act.dma_start(mem_scratch.rearrange("l p w -> p l w"), memkv[:, :, :, :].rearrange("p l a w -> p l (a w)"))\
               .then_inc(memkv_stored, 16)
            units.next -= MU

            with act.Fori(0, L) as layer:
                pos = Pos(layer)
                hold(act, par_loaded, pos.n(32, 32), passed)
                norm(pos, 0, "pre", LTP, lambda c: pcol("mix_pre_g", c), h, LG["cq"])
                act.wait_ge(lam_ready, pos.n(2, 1))
                nc.scalar.activation(lame, lamv, ACT.Exp).then_inc(lam_exp, 1)
                act.wait_ge(memkv_stored, 16)
                for step, *at in MIX:
                    if step == "unit":
                        units.before(pos, *at, LU + SLOTS)
                    elif step == "out":
                        name = at[0]
                        if name == "cu":
                            act.drain()
                        out, func = {
                            "cq": (cq[:, :, :], ACT.Copy), "ckv": (ckv[:, :, :], ACT.Copy),
                            "qk0": (QA[:, 0:4, :], ACT.Copy), "qk2": (kaT[:, 2:6, :], ACT.Copy),
                            "qi0": (QI[:, 0:4, :], ACT.Copy), "qi1": (QI[:, 4:8, :], ACT.Copy),
                            "uq0": (qbT[:, 0:4, :], ACT.Copy), "uq1": (qbT[:, 4:6, :], ACT.Copy),
                            "uk0": (kbT[:, 0:4, :], ACT.Copy), "uk1": (kbT[:, 4:6, :], ACT.Copy),
                            "uv0": (vb[:, :, 0:W], ACT.Copy), "uv1": (vb[:, :, W:HB * P], ACT.Copy),
                            "va0": (va[:, :, 0:W], ACT.Copy), "va1": (va[:, :, W:HA * P], ACT.Copy),
                            "cv": (cv[:, :, :], ACT.Gelu_apprx_tanh), "cu": (lg[0][:, :, :], ACT.Gelu_apprx_tanh),
                        }.get(name, (None, None))
                        if name == "qk1":
                            a = see_group(act, pos, LG[name])
                            nc.scalar.activation(QA[:, 4:6, :], a[:, 0:2, :], ACT.Copy)
                            nc.scalar.activation(kaT[:, 0:2, :], a[:, 2:4, :], ACT.Copy)\
                              .then_inc(acc_read[LG[name].parity], 1)
                        else:
                            copy_group(pos, LG[name], out, func)
                    elif step == "latents":
                        for name in ("cq", "ckv"):
                            hold(act, acc_read[LG[name].parity], pos.n("acc", LG[name].turn + 2), passed)
                        for t in range(NT):
                            for n, (src, w) in enumerate(((cq, W), (ckv, 2 * P))):
                                act.drain()
                                last = nc.scalar.activation(flat(lg[0])[:, 0:w], src[:, t, 0:w], ACT.Square,
                                                            accum_out=lss[:, 2 * n + t:2 * n + t + 1])
                        last.then_inc(lat_squares, 1)
                    elif step == "bq":
                        o = see_turn(act, pos, LTP["bq"])
                        for c in range(4):
                            last = nc.scalar.activation(cqh[:, c, :], o[:, c, :], ACT.Copy, scale=pcol("cq_g", c))
                        last.then_inc(x_hi, 1)
                    elif step == "bkv":
                        o = see_turn(act, pos, LTP["bkv"])
                        for c in range(2):
                            nc.scalar.activation(ckh[:, c, :], o[:, c, :], ACT.Copy, scale=pcol("ckv_g", c))
                        nc.scalar.activation(kiT[:, :], o[:, 2, :], ACT.Copy).then_inc(x_hi, 1)
                    elif step == "ix":
                        i, b = at
                        n = 4 * i + b
                        act.drain()
                        o = see_turn(act, pos, LTP[f"ix{i}_{b}"])
                        if n >= 2:
                            act.wait_ge(dots_used, pos.n(8, n - 1))
                        nc.scalar.activation(lg[n % 2][:, :, 0:P * (i + 1)], o[:, :, 0:P * (i + 1)], ACT.Relu,
                                             scale=float(64 ** -0.5)).then_inc(tp_read[LTP[f"ix{i}_{b}"] % 2], 1)
                    elif step == "bE":
                        exps(pos, pos.n(14, at[0] + 1), at[0], 2)
                    elif step == "aE":
                        exps(pos, pos.n(14, 6 + at[0] + 1), at[0], 4)
                    elif step in ("aT", "bT"):
                        k = at[0]
                        S = P * (PAIRS[k][0] + 1)
                        o = see_turn(act, pos, LTP[f"{step}{k}"])
                        nc.scalar.activation(lg[k % 2][:, 2:4, 0:S], o[:, 0:2, 0:S], ACT.Copy)\
                          .then_inc(tp_read[LTP[f"{step}{k}"] % 2], 1)
                    elif step == "aV":
                        k = at[0]
                        i, hp = PAIRS[k]
                        o = see_turn(act, pos, LTP[f"aV{k}"])
                        nc.scalar.activation(oa[:, i, 2 * hp * P:(2 * hp + 2) * P], o[:, 0, :], ACT.Copy)\
                          .then_inc(tp_read[LTP[f"aV{k}"] % 2], 1)
                    elif step == "bV":
                        k = at[0]
                        i, hp = PAIRS[k]
                        o = see_turn(act, pos, LTP[f"bV{k}"])
                        nc.scalar.activation(mixT[:, HA + 2 * hp:HA + 2 * hp + 2, i * P:(i + 1) * P],
                                             o[:, 0, :].rearrange("p (a b) -> p a b", b=P), ACT.Copy)\
                          .then_inc(tp_read[LTP[f"bV{k}"] % 2], 1)
                    elif step == "oa_across":
                        act.wait_ge(lam_ready, pos.n(2, 2))
                        see_turn(act, pos, LTP["an1"])
                        for n, b in ((0, 4), (1, 2)):
                            o = tp[LTP[f"an{n}"] % 2]
                            nc.scalar.activation(mixT[:, 4 * n:4 * n + b, :], o[:, 0:b, :], ACT.Copy, scale=subg)\
                              .then_inc(tp_read[LTP[f"an{n}"] % 2], 1)
                    elif step == "mix":
                        n = at[0]
                        act.drain()
                        if n == 3:
                            act.wait_ge(gated_c, pos.n(1, 1))
                        else:
                            act.wait_ge(unit_used, pos.n("unit", LG["cu"].unit + 2 * n + 2 + SLOTS))
                        nc.scalar.activation(xh[:, 4 * n:4 * n + 4, :], mixT[:, 4 * n:4 * n + 4, :], ACT.Copy)\
                          .then_inc(mix_hi, 1)
                squares_out(pos, 0, [LG[f"wo{n}"] for n in range(4)])

                norm(pos, 1, "xpre", LTP, lambda c: pcol("x_pre_g", c), h, LG["xq"])
                copy_group(pos, LG["xq"], qxT[:, :, :])
                for i in range(NT):
                    act.wait_ge(max_ready, pos.n(14, 12 + i + 1))
                    o = see_turn(act, pos, LTP[f"xL{i}"])
                    for hd in range(HX):
                        last = nc.scalar.activation(xe[i][:, hd, :], o[:, hd, :], ACT.Exp, scale=SCALE_B,
                                                    bias=nmx[i][:, hd:hd + 1], accum_out=sm[i][:, hd:hd + 1])
                    last.then_inc(tp_read[LTP[f"xL{i}"] % 2], 1)
                for i in range(NT):
                    o = see_turn(act, pos, LTP[f"xT{i}"])
                    nc.scalar.activation(xz[i][:, :, :], o[:, :, :], ACT.Copy).then_inc(tp_read[LTP[f"xT{i}"] % 2], 1)
                    o = see_turn(act, pos, LTP[f"xV{i}"])
                    nc.scalar.activation(cqh[:, :, i * P:(i + 1) * P], o[:, :, 0:P], ACT.Copy).then_inc(x_hi, 1)
                squares_out(pos, 1, [LG[f"xo{n}"] for n in range(4)])

                norm(pos, 2, "fpre", LTP, lambda c: pcol("f_pre_g", c), h, LG["gate0"])

                def gate(pos, j):
                    g = LG[f"gate{j}"]
                    units.ahead(pos, g)
                    a = see_group(act, pos, g)
                    if j:
                        act.wait_ge(gated, pos.n("gated", j))
                    nc.scalar.activation(sg[:, :, :], a[:, :, :], ACT.Silu).then_inc(acc_read[g.parity], 1)

                def across(pos, j):
                    o = see_turn(act, pos, LTP[f"h{j}"])
                    nc.scalar.activation(hTh[:, :, :], o[:, :, :], ACT.Copy).then_inc(x_hi, 1)

                gate(pos, 0)
                units.ahead(pos, LG["up0"])
                with act.Fori(0, (NJ - 1) // 2) as turn:
                    here = Pos(layer, turn)
                    for j in (1, 2):
                        gate(here, j)
                        across(here, j - 1)
                        units.ahead(here, LG[f"up{j}"])
                        units.ahead(here, LG[f"down{j - 1}_3"])
                units.next = LG[f"down{NJ - 2}_3"].end + units.LEAD
                across(pos, NJ - 1)
                squares_out(pos, 2, [LG[f"down{NJ - 1}_{n}"] for n in range(4)])
                units.new_layer()

            pos = Pos(L)

            def ahead(name):
                units.ahead(pos, SG[name], SU)

            def read_out(name, out, func=ACT.Copy):
                g = SG[name]
                ahead(name)
                a = see_group(act, pos, g)
                nc.scalar.activation(out, a[:, :, :], func).then_inc(acc_read[g.parity], 1)

            norm(pos, 0, "norm", STP, lambda c: spar[:, SC["norm_w"].start + c:SC["norm_w"].start + c + 1], h,
                 SG["q0"])
            for n in range(2):
                read_out(f"q{n}", qt[:, :, n * W:(n + 1) * W])
            read_out("kv", kv[:, :, :])
            q_w, k_w = spar[:, SC["q_w"]], spar[:, SC["k_w"]]

            def w_exps(k):
                S = P * (k // 4 + 1)
                act.wait_ge(max_ready, pos.n(14, k + 1))
                for r in range(4):
                    nc.scalar.activation(ze[k % 2][:, r, 0:S], zg[k % 2][:, r, 0:S], ACT.Exp,
                                         bias=nmx[k % 2][:, r:r + 1], accum_out=sm[k % 2][:, r:r + 1])
                nc.scalar.activation(esk[k % 2], snk[k % 2], ACT.Exp).then_inc(exp_ready, 1)

            for step, *at in SMIX:
                if step == "unit":
                    units.before(pos, *at, SU)
                elif step == "out":
                    name = at[0]
                    n = int(name[-1])
                    if name in ("u0", "u1"):
                        if n == 0:
                            act.wait_ge(par_loaded, pos.n(32, 32))
                        read_out(name, uT[:, 4 * n:4 * n + 4, :])
                    elif name in ("ag0", "ag1"):
                        if n:
                            act.wait_ge(ag_mul, n)
                        read_out(name, sg2[:, :, :], ACT.Silu)
                        act.wait_ge(ag_mul, n + 1)
                        nc.scalar.activation(gath[:, 4 * n:4 * n + 4, :], attnT[:, 4 * n:4 * n + 4, :], ACT.Copy)\
                          .then_inc(ag_hi, 1)
                    elif name in ("ga0", "ga1", "ga2", "ga3"):
                        if n:
                            after_group(act, pos, SG[f"ap{n - 1}"])
                        else:
                            act.wait_ge(ag_mul, 2)
                        read_out(name, sg2[:, :, :], ACT.Sigmoid)
                    elif name in ("z0", "z1"):
                        if n == 0:
                            act.wait_ge(ag_split, 2)
                        read_out(name, zs[:, 4 * n:4 * n + 4, :], ACT.Silu)
                elif step == "head_turns":
                    for n in range(2):
                        o = see_turn(act, pos, STP[f"tq{n}"])
                        for m in range(2):
                            rows_ = slice(64 * m, 64 * m + 64)
                            last = nc.scalar.activation(QP[rows_, 4 * n:4 * n + 4, m, :], o[rows_, :, :], ACT.Copy,
                                                        scale=q_w[rows_, :])
                        last.then_inc(tp_read[STP[f"tq{n}"] % 2], 1)
                    o = see_turn(act, pos, STP["tk"])
                    nc.scalar.activation(kT[:, :, :], o[:, :, :], ACT.Copy, scale=k_w)\
                      .then_inc(tp_read[STP["tk"] % 2], 1)
                elif step == "wE":
                    w_exps(at[0])
                elif step == "wT":
                    k = at[0]
                    S = P * (k // 4 + 1)
                    o = see_turn(act, pos, STP[f"wT{k}"])
                    nc.scalar.activation(zg[k % 2][:, :, 0:S], o[:, :, 0:S], ACT.Copy)\
                      .then_inc(tp_read[STP[f"wT{k}"] % 2], 1)
                elif step == "wV":
                    k = at[0]
                    i, g = k // 4, k % 4
                    o = see_turn(act, pos, STP[f"wV{k}"])
                    nc.scalar.activation(attnT[:, 2 * g:2 * g + 2, i * P:(i + 1) * P], o[:, 0:2, 0:P], ACT.Copy)\
                      .then_inc(tp_read[STP[f"wV{k}"] % 2], 1)
                elif step == "whole":
                    c = at[0]
                    act.drain()
                    for j in range(4):
                        n = 4 * c + j
                        nc.scalar.activation(turn_a[:, j, :], iota[:, :], ACT.Copy, scale=ssm[:, 3, n:n + 1])
                        last = nc.scalar.activation(turn_b[:, j, :], iota[:, :], ACT.Identity,
                                                    scale=ssm[:, 5, n:n + 1], bias=round_)
                    last.then_inc(whole, 1)
                    if c == 0:
                        act.dma_start(flat(bpad[0]), b_pad[0:P, :]).then_inc(bc_loaded[0], 16)
                elif step == "turns":
                    c = at[0]
                    if c:
                        act.wait_ge(states, c)
                    act.dma_start(flat(craw), c_pack[c * P:(c + 1) * P, :]).then_inc(maps_loaded, 16)
                    act.wait_ge(angles, c + 1)
                    nc.scalar.activation(rots[:, :, :], turn_a[:, :, :], ACT.Sin, scale=2 * math.pi)
                    nc.scalar.activation(rotc[:, :, :], turn_b[:, :, :], ACT.Sin, scale=-2 * math.pi, bias=half_pi)\
                      .then_inc(turned, 1)
                    if c + 1 < NCT:
                        if c:
                            after_turn(act, pos, STP[f"s{c - 1}_im"])
                        act.dma_start(flat(bpad[(c + 1) % 2]), b_pad[(c + 1) * P:(c + 2) * P, :])\
                           .then_inc(bc_loaded[(c + 1) % 2], 16)
                elif step == "ys":
                    n = at[0]
                    half = slice(4 * n, 4 * n + 4)
                    act.wait_ge(skipped, 4 * n + 4)
                    nc.scalar.activation(uT[:, half, :], uT[:, half, :], ACT.Gelu_apprx_tanh)
                    act.drain()
                    if n == 0:
                        after_group(act, pos, SG["ap3"])
                    nc.scalar.activation(ysh[:, half, :], uT[:, half, :], ACT.Copy).then_inc(ys_hi, 1)
            b_glu = SC["b_glu"].start
            for n in range(2):
                g = SG[f"glub{n}"]
                ahead(f"glub{n}")
                a = see_group(act, pos, g)
                if n:
                    act.drain()
                for b in range(4):
                    at = b_glu + 8 + 4 * n + b
                    last = nc.scalar.activation(sg2[:, b, :], a[:, b, :], ACT.Sigmoid, bias=spar[:, at:at + 1])
                last.then_inc(acc_read[g.parity], 1)
                ahead(f"glua{n}")
                act.wait_ge(glu_mul, n + 1)
                nc.scalar.activation(prh[:, 4 * n:4 * n + 4, :], sg2[:, :, :], ACT.Copy).then_inc(glu_hi, 1)
                if n == 0:
                    act.wait_ge(glu_split, 1)
            for n in range(4):
                if n:
                    act.wait_ge(merged_done, n)
                else:
                    act.wait_ge(glu_split, 2)
                read_out(f"gs{n}", sg2[:, :, :], ACT.Sigmoid)
                if n == 3:
                    for q in range(3):
                        nc.scalar.activation(xh[:, 4 * q:4 * q + 4, :], mixT[:, 4 * q:4 * q + 4, :], ACT.Copy)\
                          .then_inc(mix_hi, 1)
                ahead(f"sp{n}")
            act.wait_ge(merged_done, 4)
            nc.scalar.activation(xh[:, 12:16, :], mixT[:, 12:16, :], ACT.Copy).then_inc(mix_hi, 1)
            ahead("out3")

        @block.vector
        def _(dve):
            def split(pos, u):
                s = u % SLOTS
                dve.wait_ge(hi_done, pos.n("unit", u + 1))
                nc.vector.tensor_tensor(lo[s][:, :, :], raw[s][:, :, :], hi[s][:, :, :].bitcast(F32),
                                        ALU.subtract).then_inc(split_done, 1)

            units = Splitter(split)

            def norm(pos, k, tag, turns, gain, src, g, keep=None):
                for t in range(NT):
                    dve.wait_ge(in_roots, pos.n("norm", NT * k + t + 1))
                    nc.vector.tensor_scalar(y[:, t, :], src[:, t, :], rs[:, t:t + 1], None, ALU.mult)\
                      .then_inc(in_rows, 1)
                units.before(pos, g, -1, g.end)
                for q in range(4):
                    if q >= 2:
                        units.before(pos, g, 2 * q - 4, g.end)
                    dve.wait_ge(x_hi, pos.n("hi", HIS.get(f"{tag}{q}", q) + 1))
                    o = tp[turns[f"{tag}{q}"] % 2]
                    if keep is not None:
                        nc.vector.tensor_copy(keep[:, 4 * q:4 * q + 4, :], o[:, :, :])
                    for c in range(4):
                        last = nc.vector.scalar_tensor_tensor(xl[:, 4 * q + c, :], o[:, c, :], gain(4 * q + c),
                                                              xh[:, 4 * q + c, :].bitcast(F32), ALU.mult, ALU.subtract)
                    last.then_inc(tp_read[turns[f"{tag}{q}"] % 2], 1)

            def branch_out(pos, k, groups, add=False):
                def times_gain(n):
                    dve.wait_ge(out_squares, pos.n(12, 4 * k + n + 1))
                    part = y[:, :, n * W:(n + 1) * W]
                    nc.vector.tensor_tensor(part, part, gpost[:, n * W:(n + 1) * W].unsqueeze(1)
                                            .to_broadcast([P, NT, W]), ALU.mult)

                for n, g in enumerate(groups):
                    units.ahead(pos, g, g.end + 1 if n == 3 else LU + SLOTS)
                    a = see_group(dve, pos, g)
                    part = y[:, :, n * W:(n + 1) * W]
                    if add:
                        nc.vector.tensor_tensor(part, part, a[:, :, :], ALU.add).then_inc(acc_read[g.parity], 1)
                    else:
                        nc.vector.tensor_copy(part, a[:, :, :]).then_inc(acc_read[g.parity], 1)
                    if n == 0:
                        dve.wait_ge(gpost_loaded, pos.n(48, 16 * (k + 1)))
                    else:
                        times_gain(n - 1)
                dve.wait_ge(out_squares, pos.n(12, 4 * k + 4))
                nc.vector.tensor_reduce(psum_, pss, AX.X, ALU.add).then_inc(out_sums, 1)
                times_gain(3)
                dve.drain()
                dve.wait_ge(out_roots, pos.n(3, k + 1))
                for t in range(NT):
                    nc.vector.scalar_tensor_tensor(h[:, t, :], y[:, t, :], prs[:, t:t + 1], h[:, t, :],
                                                   ALU.mult, ALU.add).then_inc(h_rows, 1)

            def maxima(k, src, heads, S, scale):
                nc.vector.tensor_reduce(mx[k % 2][:, 0:heads], src, AX.X, ALU.max)
                dve.drain()
                nc.vector.tensor_scalar(nmx[k % 2][:, 0:heads], mx[k % 2][:, 0:heads], -scale, None, ALU.mult)\
                  .then_inc(max_ready, 1)

            dve.sem_inc(split_done, SLOTS)
            for n in range(2):
                dve.sem_inc(acc_read[n], 1)
                dve.sem_inc(tp_read[n], 1)
            dve.wait_ge(start_loaded, 32)
            nc.vector.tensor_copy(relb[:, :, :], relt[:, :].unsqueeze(2).to_broadcast([32, 12, P])).then_inc(rel_spread, 1)
            dve.wait_ge(mem_loaded, 16)
            pos = Pos(None)
            dve.wait_ge(par2_loaded, 16)
            mem_g = lambda l, c: spar[:, SC["mem_g"].start + l * KD + c:SC["mem_g"].start + l * KD + c + 1]
            norm(pos, 0, "mem", MTP, lambda c: mem_g(0, c), y, MG["mem_k0"], memT)
            dve.wait_ge(ssm_exp, 1)
            a_re, a_im = spar[:, SC["A_re"]], spar[:, SC["A_im"]]
            nc.vector.tensor_tensor(sw[:, 1, :], sw[:, 0, :], a_re, ALU.mult)
            nc.vector.tensor_tensor(sw[:, 2, :], sw[:, 0, :], a_im, ALU.mult)
            dve.drain()
            reduce_angle(dve, sw[:, 3, :], sw[:, 2, :], sw[:, 4, :])
            cos_argument(dve, sw[:, 4, :], sw[:, 3, :], sw[:, 7, :])
            dve.drain().then_inc(ssm_ready, 1)
            nc.vector.tensor_scalar(angle_hi[:, :], sw[:, 3, :], 1.0 / (2 * math.pi), None, ALU.mult)
            nc.vector.tensor_scalar(ssm[:, 5, :], sw[:, 3, :], 1.0 / (2 * math.pi), None, ALU.mult)
            dve.drain()
            nc.vector.tensor_copy(ssm[:, 3, :], angle_hi[:, :].bitcast(F32))
            dve.drain()
            nc.vector.scalar_tensor_tensor(sw[:, 7, :], ssm[:, 3, :], -TWO_PI_HI, sw[:, 3, :], ALU.mult, ALU.add)
            dve.drain()
            nc.vector.scalar_tensor_tensor(sw[:, 7, :], ssm[:, 3, :], -TWO_PI_MID, sw[:, 7, :], ALU.mult, ALU.add)
            dve.drain()
            nc.vector.scalar_tensor_tensor(sw[:, 7, :], ssm[:, 3, :], -TWO_PI_LO, sw[:, 7, :], ALU.mult, ALU.add)
            dve.drain()
            nc.vector.tensor_scalar(ssm[:, 4, :], sw[:, 7, :], 1.0 / (2 * math.pi), None, ALU.mult)
            dve.drain()
            dve.wait_ge(ssm_exp, 2)
            nc.vector.tensor_tensor(sw[:, 7, :], ssm[:, 0, :], sw[:, 6, :], ALU.mult)
            nc.vector.tensor_tensor(sw[:, 8, :], ssm[:, 0, :], sw[:, 5, :], ALU.mult)
            nc.vector.tensor_tensor(sw[:, 9, :], a_re, a_re, ALU.mult)
            nc.vector.tensor_tensor(sw[:, 10, :], a_im, a_im, ALU.mult)
            dve.drain()
            nc.vector.tensor_scalar(sw[:, 7, :], sw[:, 7, :], -1.0, None, ALU.add)
            nc.vector.tensor_tensor(sw[:, 9, :], sw[:, 9, :], sw[:, 10, :], ALU.add)
            dve.drain()
            nc.vector.reciprocal(sw[:, 9, :], sw[:, 9, :])
            nc.vector.tensor_tensor(sw[:, 10, :], sw[:, 7, :], a_re, ALU.mult)
            nc.vector.tensor_tensor(sw[:, 11, :], sw[:, 8, :], a_im, ALU.mult)
            nc.vector.tensor_tensor(sw[:, 12, :], sw[:, 8, :], a_re, ALU.mult)
            nc.vector.tensor_tensor(sw[:, 13, :], sw[:, 7, :], a_im, ALU.mult)
            dve.drain()
            nc.vector.tensor_tensor(sw[:, 10, :], sw[:, 10, :], sw[:, 11, :], ALU.add)
            nc.vector.tensor_tensor(sw[:, 12, :], sw[:, 12, :], sw[:, 13, :], ALU.subtract)
            dve.drain()
            nc.vector.tensor_tensor(ssm[:, 1, :], sw[:, 10, :], sw[:, 9, :], ALU.mult)
            nc.vector.tensor_tensor(ssm[:, 2, :], sw[:, 12, :], sw[:, 9, :], ALU.mult)
            dve.drain()
            dve.wait_ge(x_loaded, 16)
            dve.sem_inc(h_rows, NT)
            units.ahead(pos, MG["mem_k0"], MU)
            for q in range(4):
                units.before(pos, MG["mem_v0"], 2 * q + 1, MU)
                dve.wait_ge(mem_hi, q + 1)
                for c in range(4 * q, 4 * q + 4):
                    last = nc.vector.scalar_tensor_tensor(xl[:, c, :], memT[:, c, :], mem_g(1, c),
                                                          xh[:, c, :].bitcast(F32), ALU.mult, ALU.subtract)
                last.then_inc(mem_split, 1)
            units.ahead(pos, MG["mem_v1"], MU + 1)
            units.next -= MU

            with dve.Fori(0, L) as layer:
                pos = Pos(layer)
                dve.wait_ge(par_loaded, pos.n(32, 32))
                norm(pos, 0, "pre", LTP, lambda c: pcol("mix_pre_g", c), h, LG["cq"])
                lam = row[:, BR["lam"]].rearrange("p (a b n) -> p a b n", a=2, b=2)
                nc.vector.tensor_tensor(lamp, lam[:, :, 0, :], lam[:, :, 1, :], ALU.mult)
                dve.drain()
                nc.vector.tensor_reduce(lamv, lamp, AX.X, ALU.add).then_inc(lam_ready, 1)
                dve.wait_ge(lam_exp, pos.n(1, 1))
                nc.vector.tensor_tensor(nlam, lame[:, 1:2], lame[:, 0:1], ALU.subtract)
                dve.drain()
                nc.vector.tensor_tensor(nlam, nlam, pcol("neg_lam_init"), ALU.add)
                nc.vector.tensor_tensor(subg, pcol("sub_g"), pcol("one_minus_lam_init"), ALU.mult).then_inc(lam_ready, 1)

                for step, *at in MIX:
                    if step == "unit":
                        units.before(pos, *at, LU + SLOTS)
                    elif step == "latents":
                        dve.wait_ge(lat_roots, pos.n(1, 1))
                        for t in range(NT):
                            nc.vector.tensor_scalar(cq[:, t, :], cq[:, t, :], lrs[:, t:t + 1], None, ALU.mult)
                            nc.vector.tensor_scalar(ckv[:, t, 0:2 * P], ckv[:, t, 0:2 * P], lrs[:, 2 + t:3 + t], None, ALU.mult)
                            for m in range(2):
                                nc.vector.tensor_copy(kk[:, t, 64 * m:64 * m + 64], ckv[:, t, 256:320])
                        nc.vector.tensor_scalar(widx, ckv[:, :, 320:336], float(NIDX ** -0.5), None, ALU.mult)\
                          .then_inc(lat_rows, 1)
                    elif step == "bq":
                        dve.wait_ge(x_hi, pos.n("hi", HIS["bq"] + 1))
                        o = tp[LTP["bq"] % 2]
                        for c in range(4):
                            last = nc.vector.scalar_tensor_tensor(cql[:, c, :], o[:, c, :], pcol("cq_g", c),
                                                                  cqh[:, c, :].bitcast(F32), ALU.mult, ALU.subtract)
                        last.then_inc(tp_read[LTP["bq"] % 2], 1)
                    elif step == "bkv":
                        dve.wait_ge(x_hi, pos.n("hi", HIS["bkv"] + 1))
                        o = tp[LTP["bkv"] % 2]
                        for c in range(2):
                            last = nc.vector.scalar_tensor_tensor(ckl[:, c, :], o[:, c, :], pcol("ckv_g", c),
                                                                  ckh[:, c, :].bitcast(F32), ALU.mult, ALU.subtract)
                        last.then_inc(tp_read[LTP["bkv"] % 2], 1)
                    elif step == "ix":
                        i, b = at
                        n, S = 4 * i + b, P * (i + 1)
                        for hh in range(4):
                            g = 4 * b + hh
                            dots = lg[n % 2][:, 2 * (hh % 2) + hh // 2, 0:S]
                            dve.drain()
                            if hh == 0:
                                after_turn(dve, pos, LTP[f"ix{i}_{b}"])
                            if g == 0:
                                last = nc.vector.tensor_scalar(sc[:, i, 0:S], dots, widx[:, i, g:g + 1], None, ALU.mult)
                            else:
                                last = nc.vector.scalar_tensor_tensor(sc[:, i, 0:S], dots, widx[:, i, g:g + 1],
                                                                      sc[:, i, 0:S], ALU.mult, ALU.add)
                        last.then_inc(dots_used, 1)
                    elif step == "top":
                        i, first, final = at
                        S = P * (i + 1)
                        if first == 0:
                            hold(dve, score_masked, pos.n(2, i + 1), passed)
                        for n in range(first, final):
                            nc.vector.max(m8, sc[:, i, 0:S])
                            dve.drain()
                            nc.vector.match_replace(sc[:, i, 0:S], m8, sc[:, i, 0:S], TAKEN)
                            dve.drain()
                        if final == TOPK // 8:
                            nc.vector.tensor_scalar(sc[:, i, 0:S], sc[:, i, 0:S], 0.5 * (FILL + TAKEN), NEG,
                                                    ALU.is_ge, ALU.mult)
                            dve.drain()
                    elif step == "bL":
                        k = at[0]
                        i, hp = PAIRS[k]
                        S = P * (i + 1)
                        if k == 0:
                            dve.wait_ge(bias_ready, 1)
                        o = see_turn(dve, pos, LTP[f"bL{k}"])
                        z = lg[k % 2][:, 0:2, 0:S]
                        nc.vector.scalar_tensor_tensor(z, o[:, 0:2, 0:S], SCALE_B,
                                                       bias[:, HA + 2 * hp:HA + 2 * hp + 2, T - S:T],
                                                       ALU.mult, ALU.add).then_inc(tp_read[LTP[f"bL{k}"] % 2], 1)
                        dve.drain()
                        nc.vector.tensor_tensor(z, z, sc[:, i, 0:S].unsqueeze(1).to_broadcast([P, 2, S]), ALU.add)
                        dve.drain()
                        maxima(k, z, 2, S, 1.0)
                    elif step == "bC":
                        k = at[0]
                        dve.wait_ge(exp_ready, pos.n(12, k + 1))
                        nc.vector.reciprocal(rc[k % 2][:, 0:2], sm[k % 2][:, 0:2])
                        dve.drain()
                        for hh in range(2):
                            e = lg[k % 2][:, hh, 0:P * (PAIRS[k][0] + 1)]
                            last = nc.vector.tensor_scalar(e, e, rc[k % 2][:, hh:hh + 1], None, ALU.mult)
                        last.then_inc(weights_ready, 1)
                    elif step == "aL":
                        k = at[0]
                        i, hp = PAIRS[k]
                        S = P * (i + 1)
                        o = see_turn(dve, pos, LTP[f"aL{k}"])
                        for m in range(2):
                            last = nc.vector.scalar_tensor_tensor(lg[k % 2][:, 2 * m:2 * m + 2, 0:S],
                                                                  o[:, 2 * m:2 * m + 2, 0:S], SCALE_A,
                                                                  bias[:, 2 * hp:2 * hp + 2, T - S:T], ALU.mult, ALU.add)
                        last.then_inc(tp_read[LTP[f"aL{k}"] % 2], 1)
                        dve.drain()
                        maxima(k, lg[k % 2][:, :, 0:S], 4, S, 1.0)
                    elif step == "aC":
                        k = at[0]
                        S = P * (PAIRS[k][0] + 1)
                        e, r = lg[k % 2], rc[k % 2]
                        dve.wait_ge(exp_ready, pos.n(12, 6 + k + 1))
                        nc.vector.reciprocal(r, sm[k % 2])
                        dve.drain()
                        nc.vector.tensor_scalar(r[:, 2:4], r[:, 2:4], nlam, None, ALU.mult)
                        dve.drain()
                        for hh in range(2):
                            nc.vector.tensor_scalar(e[:, 2 + hh, 0:S], e[:, 2 + hh, 0:S], r[:, 2 + hh:3 + hh], None, ALU.mult)
                        dve.drain()
                        for hh in range(2):
                            last = nc.vector.scalar_tensor_tensor(lg[k % 2][:, hh, 0:S], e[:, hh, 0:S], r[:, hh:hh + 1],
                                                                  e[:, 2 + hh, 0:S], ALU.mult, ALU.add)
                        last.then_inc(weights_ready, 1)
                    elif step == "oa_norm":
                        after_turn(dve, pos, LTP["aV4"])
                        after_turn(dve, pos, LTP["aV5"])
                        sq = flat(kaT)[:, 0:NT * HA * P]
                        nc.vector.tensor_tensor(sq, flat(oa), flat(oa), ALU.mult)
                        dve.drain()
                        nc.vector.tensor_reduce(oss, sq.rearrange("p (n d) -> p n d", d=P), AX.X, ALU.add)\
                          .then_inc(oa_squares, 1)
                        dve.wait_ge(oa_roots, pos.n(1, 1))
                        heads = flat(oa).rearrange("p (n d) -> p n d", d=P)
                        nc.vector.tensor_tensor(heads, heads, ors.unsqueeze(2).to_broadcast([P, 12, P]), ALU.mult)\
                          .then_inc(oa_rows, 1)

                    elif step == "v_stats":
                        after_group(dve, pos, LG["cv"])
                        for t in range(NT):
                            nc.vector.bn_stats(vst[:, t, :], cv[:, t, :])
                        dve.drain()
                        for t in range(NT):
                            last = nc.vector.bn_aggr(vmv[:, t, :], vst[:, t, :])
                        last.then_inc(v_stats, 1)
                    elif step == "v_rows":
                        dve.wait_ge(v_roots, pos.n(1, 1))
                        for t in range(NT):
                            nc.vector.tensor_scalar(cv[:, t, :], cv[:, t, :], vmv[:, t, 0:1], vrs[:, t:t + 1],
                                                    ALU.subtract, ALU.mult)
                        dve.drain()
                        nc.vector.tensor_tensor(cv[:, :, :], cv[:, :, :],
                                                row[:, BR["ln_g"]].unsqueeze(1).to_broadcast([P, NT, W]), ALU.mult)
                        dve.drain()
                        nc.vector.tensor_tensor(cv[:, :, :], cv[:, :, :],
                                                row[:, BR["ln_b"]].unsqueeze(1).to_broadcast([P, NT, W]), ALU.add)\
                          .then_inc(v_rows, 1)
                    elif step == "c":
                        o = see_turn(dve, pos, LTP["c"])
                        for t in range(NT):
                            last = nc.vector.tensor_tensor(mixT[:, 12:16, t * P:(t + 1) * P], o[:, :, t * P:(t + 1) * P],
                                                           row[:, BR["b_s"]].rearrange("p (g t) -> p g t", t=P), ALU.add)
                        last.then_inc(tp_read[LTP["c"] % 2], 1)
                    elif step == "out" and at[0] == "cu":
                        after_group(dve, pos, LG["cu"])
                        nc.vector.tensor_tensor(mixT[:, 12:16, :], mixT[:, 12:16, :], lg[0][:, :, :], ALU.mult)\
                          .then_inc(gated_c, 1)
                    elif step == "mix":
                        n = at[0]
                        dve.wait_ge(mix_hi, pos.n(4, n + 1))
                        nc.vector.tensor_tensor(xl[:, 4 * n:4 * n + 4, :], mixT[:, 4 * n:4 * n + 4, :],
                                                xh[:, 4 * n:4 * n + 4, :].bitcast(F32), ALU.subtract)\
                          .then_inc(mix_split, 1)
                branch_out(pos, 0, [LG[f"wo{n}"] for n in range(4)])
                dve.drain()

                norm(pos, 1, "xpre", LTP, lambda c: pcol("x_pre_g", c), h, LG["xq"])
                units.ahead(pos, LG["xq"])
                for i in range(NT):
                    o = see_turn(dve, pos, LTP[f"xL{i}"])
                    maxima(i, o[:, :, :], 4, T, SCALE_B)
                for i in range(NT):
                    after_turn(dve, pos, LTP[f"xL{i}"])
                    nc.vector.reciprocal(rc[i], sm[i])
                    dve.drain()
                    nc.vector.tensor_tensor(xe[i][:, :, :], xe[i][:, :, :], rc[i].unsqueeze(2).to_broadcast([P, HX, T]),
                                            ALU.mult).then_inc(weights_ready, 1)
                for i in range(NT):
                    dve.wait_ge(x_hi, pos.n("hi", HIS[f"xV{i}"] + 1))
                    o = tp[LTP[f"xV{i}"] % 2]
                    nc.vector.tensor_tensor(cql[:, :, i * P:(i + 1) * P], o[:, :, 0:P],
                                            cqh[:, :, i * P:(i + 1) * P].bitcast(F32), ALU.subtract)\
                      .then_inc(tp_read[LTP[f"xV{i}"] % 2], 1)
                branch_out(pos, 1, [LG[f"xo{n}"] for n in range(4)])
                dve.drain()

                norm(pos, 2, "fpre", LTP, lambda c: pcol("f_pre_g", c), h, LG["gate0"])
                nc.vector.memset(y[:, :, :], 0.0)

                def across(pos, j):
                    dve.wait_ge(x_hi, pos.n("hi", HIS[f"h{j}"] + 1))
                    o = tp[LTP[f"h{j}"] % 2]
                    nc.vector.tensor_tensor(hTl[:, :, :], o[:, :, :], hTh[:, :, :].bitcast(F32), ALU.subtract)\
                      .then_inc(tp_read[LTP[f"h{j}"] % 2], 1)

                def gate(pos, j):
                    g = LG[f"up{j}"]
                    units.ahead(pos, g)
                    after_group(dve, pos, LG[f"gate{j}"])
                    a = see_group(dve, pos, g)
                    nc.vector.tensor_tensor(hm[j % 2][:, :, :], sg[:, :, :], a[:, :, :], ALU.mult)\
                      .then_inc(acc_read[g.parity], 1)
                    dve.drain().then_inc(gated, 1)

                def down(pos, j):
                    for n in range(4):
                        g = LG[f"down{j}_{n}"]
                        units.ahead(pos, g)
                        a = see_group(dve, pos, g)
                        nc.vector.tensor_tensor(y[:, :, n * W:(n + 1) * W], y[:, :, n * W:(n + 1) * W], a[:, :, :],
                                                ALU.add).then_inc(acc_read[g.parity], 1)

                gate(pos, 0)
                with dve.Fori(0, (NJ - 1) // 2) as turn:
                    here = Pos(layer, turn)
                    for j in (1, 2):
                        units.ahead(here, LG[f"gate{j}"])
                        across(here, j - 1)
                        gate(here, j)
                        down(here, j - 1)
                units.next = LG[f"down{NJ - 2}_3"].end + units.LEAD
                across(pos, NJ - 1)
                branch_out(pos, 2, [LG[f"down{NJ - 1}_{n}"] for n in range(4)], add=True)
                dve.drain()
                units.new_layer()

            pos = Pos(L)

            def ahead(name):
                units.ahead(pos, SG[name], SU)

            dve.wait_ge(par2_loaded, 16)
            norm(pos, 0, "norm", STP, lambda c: spar[:, SC["norm_w"].start + c:SC["norm_w"].start + c + 1], h,
                 SG["q0"])
            for m in range(2):
                nc.vector.memset(cpad[m][:, :], 0.0)
            ahead("q1")
            for name in ("q0", "q1"):
                after_group(dve, pos, SG[name])
            sq = y[:, 0, :]
            nc.vector.tensor_tensor(sq, flat(qt), flat(qt), ALU.mult)
            dve.drain()
            nc.vector.tensor_reduce(qss[:, 0:32], sq.rearrange("p (n d) -> p n d", d=64), AX.X, ALU.add)
            dve.drain()
            ahead("kv")
            after_group(dve, pos, SG["kv"])

            def head_rows():
                sq = y[:, 0, 0:NT * 256].rearrange("p (t d) -> p t d", t=NT)
                nc.vector.tensor_tensor(sq, kv[:, :, 0:256], kv[:, :, 0:256], ALU.mult)
                dve.drain()
                nc.vector.tensor_reduce(qss[:, 32:40], sq.rearrange("p t (n d) -> p (t n) d", d=64), AX.X, ALU.add)\
                  .then_inc(q_squares, 1)
                dve.wait_ge(q_roots, 1)
                rows_ = flat(qt).rearrange("p (n d) -> p n d", d=64)
                nc.vector.tensor_tensor(rows_, rows_, qrs[:, 0:32].unsqueeze(2).to_broadcast([P, 32, 64]), ALU.mult)
                units.before(pos, SG["u0"], 3, SU)
                dve.drain()
                for t in range(NT):
                    keys = kv[:, t, 0:256].rearrange("p (g d) -> p g d", d=64)
                    vals = kv[:, t, 256:512].rearrange("p (g d) -> p g d", d=64)
                    roots_ = qrs[:, 32 + 4 * t:36 + 4 * t].unsqueeze(2).to_broadcast([P, 4, 64])
                    for m in range(2):
                        nc.vector.tensor_tensor(kdup[:, t, :, m, :], keys, roots_, ALU.mult)
                        last = nc.vector.tensor_copy(vpad[:, t, :, m, 64 * m:64 * m + 64], vals)
                last.then_inc(q_rows, 1)

            def w_max(k):
                i, g = k // 4, k % 4
                S = P * (i + 1)
                o = see_turn(dve, pos, STP[f"wL{k}"])
                sinks_ = sink[:, 4 * g:4 * g + 4]
                nc.vector.scalar_tensor_tensor(zg[k % 2][:, :, 0:S], o[:, :, 0:S], SCALE_A,
                                               window[:, T - S:T].unsqueeze(1).to_broadcast([P, 4, S]),
                                               ALU.mult, ALU.add).then_inc(tp_read[STP[f"wL{k}"] % 2], 1)
                dve.drain()
                nc.vector.tensor_reduce(mx[k % 2], zg[k % 2][:, :, 0:S], AX.X, ALU.max)
                dve.drain()
                nc.vector.tensor_tensor(mx[k % 2], mx[k % 2], sinks_, ALU.max)
                dve.drain()
                nc.vector.tensor_scalar(nmx[k % 2], mx[k % 2], -1.0, None, ALU.mult)
                nc.vector.tensor_tensor(snk[k % 2], sinks_, mx[k % 2], ALU.subtract).then_inc(max_ready, 1)

            for step, *at in SMIX:
                if step == "unit":
                    units.before(pos, *at, SU)
                elif step == "head_rows":
                    head_rows()
                elif step == "wL":
                    if at[0] == 0:
                        dve.wait_ge(window_ready, 1)
                        dve.wait_ge(sink_loaded, 16)
                    w_max(at[0])
                elif step == "w_weights":
                    k = at[0]
                    S = P * (k // 4 + 1)
                    dve.wait_ge(exp_ready, pos.n(12, k + 1))
                    nc.vector.tensor_tensor(sm[k % 2], sm[k % 2], esk[k % 2], ALU.add)
                    dve.drain()
                    nc.vector.reciprocal(rc[k % 2], sm[k % 2])
                    dve.drain()
                    e = ze[k % 2][:, :, 0:S]
                    nc.vector.tensor_tensor(e, e, rc[k % 2].unsqueeze(2).to_broadcast([P, 4, S]), ALU.mult)\
                      .then_inc(weights_ready, 1)
                elif step == "out":
                    name = at[0]
                    n = int(name[-1])
                    if name in ("ag0", "ag1"):
                        after_group(dve, pos, SG[name])
                        if n == 0:
                            after_turn(dve, pos, STP["wV6"])
                            after_turn(dve, pos, STP["wV7"])
                        part = attnT[:, 4 * n:4 * n + 4, :]
                        nc.vector.tensor_tensor(part, part, sg2[:, :, :], ALU.mult).then_inc(ag_mul, 1)
                        dve.wait_ge(ag_hi, n + 1)
                        nc.vector.tensor_tensor(gatl[:, 4 * n:4 * n + 4, :], part,
                                                gath[:, 4 * n:4 * n + 4, :].bitcast(F32), ALU.subtract)\
                          .then_inc(ag_split, 1)
                    elif name in ("ap0", "ap1", "ap2", "ap3"):
                        g = SG[name]
                        after_group(dve, pos, SG[f"ga{n}"])
                        a = see_group(dve, pos, g)
                        nc.vector.tensor_tensor(mixT[:, 4 * n:4 * n + 4, :], sg2[:, :, :], a[:, :, :], ALU.mult)\
                          .then_inc(acc_read[g.parity], 1)
                elif step == "maps":
                    c = at[0]
                    dve.wait_ge(maps_loaded, 16 * (c + 1))
                    gain = [ssm[:, 1 + m, 4 * c:4 * c + 4].unsqueeze(2).to_broadcast([P, 4, 32]) for m in range(2)]
                    diag = [cpad[m][:, :].rearrange("p (j w) -> p j w", w=160)[:, :, 0:32] for m in range(2)]
                    tmp = [small[:, 256:384].rearrange("p (j w) -> p j w", w=32), craw2[:, :, :]]
                    nc.vector.tensor_tensor(tmp[0], craw[:, 0, :, :], gain[0], ALU.mult)
                    nc.vector.tensor_tensor(tmp[1], craw[:, 1, :, :], gain[1], ALU.mult)
                    dve.drain()
                    nc.vector.tensor_tensor(diag[0], tmp[0], tmp[1], ALU.subtract)
                    dve.drain()
                    nc.vector.tensor_tensor(tmp[0], craw[:, 0, :, :], gain[1], ALU.mult)
                    nc.vector.tensor_tensor(tmp[1], craw[:, 1, :, :], gain[0], ALU.mult)
                    dve.drain()
                    nc.vector.scalar_tensor_tensor(diag[1], tmp[0], -1.0, tmp[1], ALU.mult, ALU.subtract)
                elif step == "back":
                    c = at[0]
                    dve.wait_ge(turned, c + 1)
                    o = see_turn(dve, pos, STP[f"s{c}_re"])
                    nc.vector.tensor_tensor(sd[0][:, :, :], o[:, :, :], rotc[:, :, :], ALU.mult)
                    nc.vector.tensor_tensor(sr[0][:, :, :], o[:, :, :], rots[:, :, :], ALU.mult)\
                      .then_inc(tp_read[STP[f"s{c}_re"] % 2], 1)
                    o = see_turn(dve, pos, STP[f"s{c}_im"])
                    nc.vector.tensor_tensor(sd[1][:, :, :], o[:, :, :], rotc[:, :, :], ALU.mult)
                    nc.vector.tensor_tensor(st[:, :, :], o[:, :, :], rots[:, :, :], ALU.mult)\
                      .then_inc(tp_read[STP[f"s{c}_im"] % 2], 1)
                    dve.drain().then_inc(backed, 1)
                elif step == "angles":
                    c = at[0]
                    dve.wait_ge(whole, c + 1)
                    nc.vector.scalar_tensor_tensor(turn_a[:, :, :], turn_b[:, :, :], ROUND, turn_a[:, :, :],
                                                   ALU.subtract, ALU.subtract)
                    dve.drain()
                    for j, s in enumerate(range(4 * c, 4 * c + 4)):
                        nc.vector.scalar_tensor_tensor(turn_a[:, j, :], iota[:, :], ssm[:, 4, s:s + 1],
                                                       turn_a[:, j, :], ALU.mult, ALU.subtract)
                    dve.drain()
                    nc.vector.tensor_scalar(turn_a[:, :, :], turn_a[:, :, :], HALF_IN, -HALF_IN, ALU.min, ALU.max)
                    dve.drain()
                    nc.vector.scalar_tensor_tensor(turn_b[:, :, :], turn_a[:, :, :], -1.0, turn_a[:, :, :],
                                                   ALU.mult, ALU.max).then_inc(angles, 1)
                elif step == "scan":
                    c = at[0]
                    dve.wait_ge(summed, c + 1)
                    for j, s in enumerate(range(4 * c, 4 * c + 4)):
                        for m in range(2):
                            nc.vector.tensor_tensor_scan(sr[m][:, j, :], ssm[:, 0, s:s + 1].to_broadcast([P, T]),
                                                         sd[m][:, j, :], 0.0, ALU.mult, ALU.add)
                    dve.drain().then_inc(scanned, 1)
                elif step == "forward":
                    c = at[0]
                    nc.vector.tensor_tensor(sd[0][:, :, :], sr[0][:, :, :], rotc[:, :, :], ALU.mult)
                    nc.vector.tensor_tensor(sd[1][:, :, :], sr[0][:, :, :], rots[:, :, :], ALU.mult)
                elif step == "join":
                    c = at[0]
                    dve.drain()
                    dve.wait_ge(parts_turned, c + 1)
                    nc.vector.tensor_tensor(sd[0][:, :, :], sd[0][:, :, :], st[:, :, :], ALU.subtract)
                    nc.vector.tensor_tensor(sd[1][:, :, :], sd[1][:, :, :], sr[1][:, :, :], ALU.add).then_inc(states, 1)
                elif step == "ys":
                    n = at[0]
                    half = slice(4 * n, 4 * n + 4)
                    dve.wait_ge(ys_hi, n + 1)
                    nc.vector.tensor_tensor(ysl[:, half, :], uT[:, half, :], ysh[:, half, :].bitcast(F32), ALU.subtract)\
                      .then_inc(ys_split, 1)
                elif step == "skip":
                    c = at[0]
                    o = see_turn(dve, pos, STP[f"s{c}_y"])
                    col = SC["skip"].start + c
                    nc.vector.scalar_tensor_tensor(uT[:, c, :], uT[:, c, :], spar[:, col:col + 1], o[:, 0, :],
                                                   ALU.mult, ALU.add).then_inc(tp_read[STP[f"s{c}_y"] % 2], 1)
                    dve.drain().then_inc(skipped, 1)
            for n in range(2):
                g = SG[f"glua{n}"]
                ahead(f"glub{n}")
                ahead(f"glua{n}")
                after_group(dve, pos, SG[f"glub{n}"])
                a = see_group(dve, pos, g)
                for b in range(4):
                    at = SC["b_glu"].start + 4 * n + b
                    last = nc.vector.scalar_tensor_tensor(sg2[:, b, :], a[:, b, :], spar[:, at:at + 1], sg2[:, b, :],
                                                          ALU.add, ALU.mult)
                last.then_inc(acc_read[g.parity], 1)
                dve.drain()
                if n == 0:
                    after_group(dve, pos, SG["z0"])
                    after_group(dve, pos, SG["z1"])
                nc.vector.tensor_tensor(sg2[:, :, :], sg2[:, :, :], zs[:, 4 * n:4 * n + 4, :], ALU.mult)\
                  .then_inc(glu_mul, 1)
                dve.wait_ge(glu_hi, n + 1)
                nc.vector.tensor_tensor(prl[:, 4 * n:4 * n + 4, :], sg2[:, :, :], prh[:, 4 * n:4 * n + 4, :].bitcast(F32),
                                        ALU.subtract).then_inc(glu_split, 1)

            def merged_low(n):
                dve.wait_ge(mix_hi, pos.n(4, n + 1))
                nc.vector.tensor_tensor(xl[:, 4 * n:4 * n + 4, :], mixT[:, 4 * n:4 * n + 4, :],
                                        xh[:, 4 * n:4 * n + 4, :].bitcast(F32), ALU.subtract).then_inc(mix_split, 1)

            for n in range(4):
                g = SG[f"sp{n}"]
                ahead(f"gs{n}")
                if n == 3:
                    for q in range(3):
                        merged_low(q)
                ahead(f"sp{n}")
                after_group(dve, pos, SG[f"gs{n}"])
                a = see_group(dve, pos, g)
                nc.vector.tensor_tensor(sg2[:, :, :], sg2[:, :, :], a[:, :, :], ALU.mult).then_inc(acc_read[g.parity], 1)
                dve.drain()
                part = mixT[:, 4 * n:4 * n + 4, :]
                nc.vector.tensor_tensor(part, part, sg2[:, :, :], ALU.add).then_inc(merged_done, 1)
            merged_low(3)
            for n in range(4):
                g = SG[f"out{n}"]
                ahead(f"out{n}")
                a = see_group(dve, pos, g)
                part = h[:, :, n * W:(n + 1) * W]
                nc.vector.tensor_tensor(part, part, a[:, :, :], ALU.add).then_inc(acc_read[g.parity], 1)

        @block.gpsimd
        def _(pool):
            def roots(out, src, scale, n, signal, tmp=None):
                nc.gpsimd.tensor_scalar(out, src, scale, EPS, ALU.mult, ALU.add)
                pool.drain()
                nc.gpsimd.tensor_tensor(out, out, mhalf[:, 0:n], ALU.pow).then_inc(signal, 1)

            nc.gpsimd.memset(mhalf[:, :], -0.5)
            nc.gpsimd.memset(half_pi, math.pi / 2)
            nc.gpsimd.memset(round_, ROUND)
            nc.gpsimd.memset(ident[:, :], 0.0)
            pool.drain()
            nc.gpsimd.affine_select(out=ident[:, :], in_=ident[:, :], compare_op=ALU.not_equal, fill=1.0,
                                    base=0, pattern=[[-1, P]], channel_multiplier=1).then_inc(const_ready, 1)
            for t in range(NT):
                hold(pool, in_squares, t + 1, passed)
                roots(rs[:, t:t + 1], ss[:, t:t + 1], 1.0 / D, 1, in_roots)
            pool.wait_ge(toep_moved, 48)
            nc.gpsimd.affine_select(out=bias[:, :, P:T], in_=bias[:, :, P:T], compare_op=ALU.is_ge, fill=NEG,
                                    base=0, pattern=[[0, HA + HB], [-1, P]], channel_multiplier=1)\
              .then_inc(bias_ready, 1)
            nc.gpsimd.iota(iota[:, :], [[1, T]], base=0, channel_multiplier=0, allow_small_or_imprecise_dtypes=True)

            def load_parameters(at, row_):
                pool.dma_start(par[:, :], params[bass.ds(at, P), :]).then_inc(par_loaded, 16)
                pool.dma_start(row[:, :], rows[bass.ds(row_, 1), :].to_broadcast([P, NBR])).then_inc(par_loaded, 16)

            load_parameters(0, 0)
            with pool.Fori(0, L) as layer:
                pos = Pos(layer)

                def load_gain(k):
                    if k:
                        pool.wait_ge(h_rows, pos.n(6, 2 * k + 2))
                    else:
                        pool.wait_ge(gated_c, pos.n(1, 1))
                    pool.dma_start(gpost[:, :], post_g[bass.ds(layer * 3 + k, 1), :].to_broadcast([P, D]))\
                        .then_inc(gpost_loaded, 16)

                def norm(k):
                    for t in range(NT):
                        hold(pool, in_squares, pos.n("norm", NT * k + t + 1), passed)
                        roots(rs[:, t:t + 1], ss[:, t:t + 1], 1.0 / D, 1, in_roots)

                def norm_out(k):
                    hold(pool, out_sums, pos.n(3, k + 1), passed)
                    roots(prs, psum_, 1.0 / D, 2, out_roots)

                norm(0)
                hold(pool, par_loaded, pos.n(32, 32), passed)
                cw = par[:, PC["c_w"]].rearrange("p (g t) -> p g t", t=P)
                nc.gpsimd.affine_select(out=cw, in_=cw, compare_op=ALU.is_ge, fill=0.0, base=0,
                                        pattern=[[0, 4], [1, P]], channel_multiplier=-1).then_inc(cw_ready, 1)
                hold(pool, lat_squares, pos.n(1, 1), passed)
                nc.gpsimd.tensor_scalar(lrs[:, 0:2], lss[:, 0:2], 1.0 / W, EPS, ALU.mult, ALU.add)
                nc.gpsimd.tensor_scalar(lrs[:, 2:4], lss[:, 2:4], 1.0 / (2 * P), EPS, ALU.mult, ALU.add)
                pool.drain()
                nc.gpsimd.tensor_tensor(lrs, lrs, mhalf[:, 0:4], ALU.pow).then_inc(lat_roots, 1)
                for i in range(NT):
                    hold(pool, dots_used, pos.n(8, 4 * i + 4), passed)
                    nc.gpsimd.affine_select(out=sc[:, i, 0:P * (i + 1)], in_=sc[:, i, 0:P * (i + 1)],
                                            compare_op=ALU.is_ge, fill=FILL, base=P * i,
                                            pattern=[[-1, P * (i + 1)]], channel_multiplier=1).then_inc(score_masked, 1)
                hold(pool, v_stats, pos.n(1, 1), passed)
                roots(vrs, vmv[:, :, 1], 1.0, 2, v_roots)
                see_turn(pool, pos, LTP["c"])
                pool.wait_ge(memkv_stored, 16)
                pool.dma_start(flat(kmT), mem_scratch[bass.ds(layer, 1), :, 0:4 * T].rearrange("l p w -> (l p) w"))\
                    .then_inc(memkv_loaded, 16)
                pool.dma_start(flat(vm), mem_scratch[bass.ds(layer, 1), :, 4 * T:8 * T].rearrange("l p w -> (l p) w"))\
                    .then_inc(memkv_loaded, 16)
                hold(pool, oa_squares, pos.n(1, 1), passed)
                roots(ors, oss, 1.0 / P, 12, oa_roots)
                load_gain(0)
                norm_out(0)
                norm(1)
                load_gain(1)
                norm_out(1)
                norm(2)
                load_gain(2)
                after_turn(pool, pos, LTP["fpre3"])
                load_parameters((layer + 1) * P, layer + 1)
                norm_out(2)

            pos = Pos(L)
            pool.wait_ge(h_rows, pos.n(6, 2))
            for t in range(NT):
                pool.wait_ge(in_squares, pos.n("norm", t + 1))
                roots(rs[:, t:t + 1], ss[:, t:t + 1], 1.0 / D, 1, in_roots)
            pool.dma_start(sink[:, :], sinks.to_broadcast([P, NQ])).then_inc(sink_loaded, 16)
            nc.gpsimd.memset(window[:, :], 0.0)
            pool.drain()
            nc.gpsimd.affine_select(out=window[:, 0:P], in_=window[:, 0:P], compare_op=ALU.is_gt, fill=NEG, base=0,
                                    pattern=[[1, P]], channel_multiplier=-1)
            nc.gpsimd.affine_select(out=window[:, P:T], in_=window[:, P:T], compare_op=ALU.is_ge, fill=NEG, base=0,
                                    pattern=[[-1, P]], channel_multiplier=1).then_inc(window_ready, 1)
            nc.gpsimd.memset(flat(vpad), 0.0)
            nc.gpsimd.memset(flat(QP), 0.0)
            pool.wait_ge(q_squares, 1)
            roots(qrs, qss, 1.0 / 64, 40, q_roots)
            for c in range(NCT):
                hold(pool, backed, c + 1, passed)
                nc.gpsimd.tensor_tensor(sd[0][:, :, :], sd[0][:, :, :], st[:, :, :], ALU.add)
                nc.gpsimd.tensor_tensor(sd[1][:, :, :], sd[1][:, :, :], sr[0][:, :, :], ALU.subtract)
                pool.drain().then_inc(summed, 1)
                hold(pool, scanned, c + 1, passed)
                nc.gpsimd.tensor_tensor(st[:, :, :], sr[1][:, :, :], rots[:, :, :], ALU.mult)
                pool.drain()
                nc.gpsimd.tensor_tensor(sr[1][:, :, :], sr[1][:, :, :], rotc[:, :, :], ALU.mult)\
                  .then_inc(parts_turned, 1)


def bucket_rows():
    n = np.maximum(T - 1 - np.arange(TOEP), 0)
    nf = np.maximum(n, 1).astype(np.float32)
    large = 16 + (np.log(nf / np.float32(16)) / np.float32(math.log(8.0)) * 16).astype(np.int32)
    bucket = np.where(n < 16, n, np.minimum(large, 31))
    return (bucket[None, :] == np.arange(32)[:, None]).astype(np.float32)


def units_of(w, group):
    w = np.asarray(w)
    k, width = w.shape
    assert k == group.kchunks * P and width == group.width, (group.name, w.shape)
    out = np.zeros((group.units, P, KU, W), w.dtype)
    out[..., :width] = w.reshape(group.units, KU, P, width).transpose(0, 2, 1, 3)
    return out.reshape(group.units, P, KU * W)


def columns(v):
    return np.asarray(v).reshape(-1, P).T


def layer_blocks(a, l):
    w_in = a["w_in"][l]
    blocks = {}
    for n in range(3):
        blocks[f"qk{n}"] = w_in[:, n * W:(n + 1) * W]
    for name, lo_, hi_ in (("va0", 1536, 2048), ("va1", 2048, 2304), ("cq", 2304, 2816), ("ckv", 2816, 3152),
                           ("cu", 3152, 3664), ("cv", 3664, 4176)):
        blocks[name] = w_in[:, lo_:hi_]
    for tag, w in (("uq", a["b_w_uq"]), ("uk", a["b_w_uk"]), ("uv", a["b_w_uv"])):
        w = w[l].reshape(w.shape[1], -1)
        blocks[f"{tag}0"], blocks[f"{tag}1"] = w[:, :W], w[:, W:]
    w = a["b_w_qidx"][l].reshape(W, -1)
    blocks["qi0"], blocks["qi1"] = w[:, :W], w[:, W:]
    blocks["xq"] = a["x_wq"][l].reshape(D, W)
    xo = a["x_wo"][l].reshape(W, D)
    for n in range(4):
        blocks[f"wo{n}"] = a["w_out"][l][:, n * W:(n + 1) * W]
        blocks[f"xo{n}"] = xo[:, n * W:(n + 1) * W]
    for j in range(NJ):
        blocks[f"gate{j}"] = a["f_w_gu"][l][:, 0, j * W:(j + 1) * W]
        blocks[f"up{j}"] = a["f_w_gu"][l][:, 1, j * W:(j + 1) * W]
        for n in range(4):
            blocks[f"down{j}_{n}"] = a["f_w_down"][l][j * W:(j + 1) * W, n * W:(n + 1) * W]
    return blocks


def layer_params(a, l):
    lam_init = 0.8 - 0.6 * math.exp(-0.3 * l)
    ones = np.ones((P, 1), np.float32)
    cols = {"mix_pre_g": columns(a["mix_pre_g"][l]),
            "x_pre_g": columns(a["x_pre_g"][l]), "f_pre_g": columns(a["f_pre_g"][l]),
            "cq_g": columns(a["b_cq_g"][l]), "ckv_g": columns(a["b_ckv_g"][l]), "sub_g": columns(a["a_sub_g"][l]),
            "neg_lam_init": np.full((P, 1), -lam_init, np.float32),
            "one_minus_lam_init": np.full((P, 1), 1.0 - lam_init, np.float32),
            "c_w": a["c_w_s"][l].transpose(2, 0, 1).reshape(P, 4 * P)}
    return np.concatenate([cols[n] for n in PC], axis=1)


def layer_rows(a, l):
    parts = {"ln_g": a["c_ln_g"][l], "ln_b": a["c_ln_b"][l], "b_s": a["c_b_s"][l].reshape(-1),
             "lam": a["a_lambda"][l].reshape(-1)}
    return np.concatenate([parts[n] for n in BR])


def second_blocks(a):
    w_in, at, blocks = a["w_in_2"], 0, {}
    for names, width in ((["q0", "q1"], 1024), (["kv"], W), (["ag0", "ag1"], 1024), (["u0", "u1"], 1024),
                         (["z0", "z1"], 1024), ([f"ga{n}" for n in range(4)], D), ([f"gs{n}" for n in range(4)], D)):
        for n, name in enumerate(names):
            blocks[name] = w_in[:, at + n * W:at + (n + 1) * W]
        at += width
    for n in range(4):
        cols = slice(n * W, (n + 1) * W)
        blocks[f"ap{n}"], blocks[f"sp{n}"] = a["w_attn_proj_2"][:, cols], a["w_ssm_proj_2"][:, cols]
        blocks[f"out{n}"] = a["w_out_2"][:, cols]
        blocks[f"glu{'a' if n < 2 else 'b'}{n % 2}"] = a["w_glu_2"][:, cols]
    return blocks


def second_params(a):
    state = lambda v: np.asarray(v).reshape(32, P).T
    cols = {"norm_w": columns(a["norm_w_2"]), "mem_g": columns(a["mem_g"]), "q_w": np.tile(a["q_norm_w_2"], 2)[:, None],
            "k_w": np.tile(a["k_norm_w_2"], 2)[:, None], "b_glu": columns(a["b_glu_2"]),
            "skip": columns(a["D_skip_2"]), "A_re": state(a["A_re_2"]), "A_im": state(a["A_im_2"]),
            "log_dt": state(np.repeat(a["log_dt_2"], 64))}
    return np.concatenate([cols[n] for n in SC], axis=1)


def input_maps(a):
    out = np.zeros((NCT, P, 2, 4, P), np.float32)
    for m, b in enumerate((a["B_re_2"], a["B_im_2"])):
        for g in range(64):
            c, q = g // 8, g % 8
            out[c, 16 * q:16 * q + 16, m, q // 2, 64 * (q % 2):64 * (q % 2) + 64] = b[g].T
    return out.reshape(NCT * P, -1)


def output_maps(a):
    out = np.zeros((NCT, P, 2, 4, 32), np.float32)
    for m, w in enumerate((a["C_re_2"], a["C_im_2"])):
        for g in range(64):
            c, q = g // 8, g % 8
            out[c, 64 * (q % 2):64 * (q % 2) + 64, m, q // 2, 16 * (q % 2):16 * (q % 2) + 16] = w[g].T
    return out.reshape(NCT * P, -1)


def kernel(**inputs):
    from concourse import bacc
    from concourse.bass_utils import run_bass_kernel_spmd

    a = {n: np.asarray(v) for n, v in inputs.items()}
    stream = [units_of(a["x_wkv"][l][:, n].reshape(D, W), MG[f"mem_{'kv'[n]}{l}"]) for l in range(L) for n in range(2)]
    for l in range(L):
        blocks = layer_blocks(a, l)
        stream += [units_of(blocks[name], g) for name, g in LG.items()]
    second = second_blocks(a)
    stream += [units_of(second[name], g) for name, g in SG.items() if g.units]
    arrays = {
        "stream": np.concatenate(stream).reshape(-1, WSLOT),
        "x": a["x"][0],
        "mem": a["mem"][0],
        "params": np.concatenate([layer_params(a, min(l, L - 1)) for l in range(L + 1)]),
        "rows": np.stack([layer_rows(a, min(l, L - 1)) for l in range(L + 1)]),
        "post_g": np.stack([a[n][l] for l in range(L) for n in ("mix_post_g", "x_post_g", "f_post_g")]),
        "sparams": second_params(a),
        "sinks": a["sinks_2"][None, :],
        "onehot": bucket_rows(),
        "rel": a["rel_bias"],
        "b_pad": input_maps(a),
        "c_pack": output_maps(a),
    }
    arrays = {f"in_{n}": np.ascontiguousarray(v) for n, v in arrays.items()}
    nc = bacc.Bacc("TRN2", target_bir_lowering=False, num_devices=1)
    ins = [nc.dram_tensor(n, v.shape, F32, kind="ExternalInput").ap() for n, v in arrays.items()]
    out = nc.dram_tensor("out", (T, D), F32, kind="ExternalOutput").ap()
    toep_scratch = nc.dram_tensor("toep_scratch", (P * 12 * TOEP,), F32, kind="Internal").ap()
    mem_scratch = nc.dram_tensor("mem_scratch", (L, P, 2 * 4 * T), F32, kind="Internal").ap()
    build(nc, *ins, out, toep_scratch, mem_scratch)
    result = run_bass_kernel_spmd(nc, [arrays], core_ids=[0])
    return result.results[0]["out"].reshape(1, T, D)
```
